# Optimizing a Trainium2 kernel written in Bass

```python
import math
import jax
import jax.numpy as jnp
from jax import lax
import numpy as np
import jax, jax.numpy as jnp

D_MODEL = 1024
BATCH = 1
SEQ = 512
DEPTH = 1

D_INNER = 2 * D_MODEL
D_ATTN = D_INNER // 2
D_SSM = D_INNER - D_ATTN
SB_HEAD_DIM = 64
SB_HEADS = D_ATTN // SB_HEAD_DIM
SSM_HEAD_DIM = 64
SSM_HEADS = D_SSM // SSM_HEAD_DIM
SSM_GROUPS = 2
SSM_STATE = 128
CONV_WIDTH = 4
SSD_CHUNK = 128
Q_BLOCK = 128
NORM_EPS = 1e-6
D_XBC = D_SSM + 2 * SSM_GROUPS * SSM_STATE
D_PROJ = 4 * D_ATTN + D_XBC + SSM_HEADS + D_SSM
DT_MIN = 1e-3
DT_MAX = 1e-1


def rms_norm(x, gain):
    xf = x.astype(jnp.float32)
    y = xf * lax.rsqrt(jnp.mean(xf * xf, axis=-1, keepdims=True) + NORM_EPS)
    return (y * gain.astype(jnp.float32)).astype(x.dtype)

def stick_breaking_attention(q, k, v):
    seq = q.shape[1]
    scale = q.shape[-1] ** -0.5
    outs = []
    for blk in range(seq // Q_BLOCK):
        start = blk * Q_BLOCK
        end = start + Q_BLOCK
        z = jnp.einsum("bqhd,bkhd->bhqk", q[:, start:end], k[:, :end]).astype(jnp.float32) * scale
        t_idx = start + jnp.arange(Q_BLOCK)[:, None]
        s_idx = jnp.arange(end)[None, :]
        mask = s_idx < t_idx
        log_beta = jax.nn.log_sigmoid(z)
        log_one_minus = jnp.where(mask, jax.nn.log_sigmoid(-z), 0.0)
        tail = lax.cumsum(log_one_minus, axis=3, reverse=True) - log_one_minus
        weights = jnp.exp(jnp.where(mask, log_beta + tail, -jnp.inf))
        outs.append(jnp.einsum("bhqk,bkhd->bqhd", weights.astype(v.dtype), v[:, :end]))
    return jnp.concatenate(outs, axis=1)

def causal_depthwise_conv(u, w, b):
    ch = u.shape[-1]
    y = lax.conv_general_dilated(
        u, w[:, None, :].astype(u.dtype), window_strides=(1,),
        padding=[(CONV_WIDTH - 1, 0)], dimension_numbers=("NWC", "WIO", "NWC"),
        feature_group_count=ch)
    return y + b.astype(u.dtype)

def ssd_scan(xs, dt, a, b_in, c_in, d_skip):
    bsz, seq, nh, hp = xs.shape
    ng, ns = b_in.shape[-2:]
    hpg = nh // ng
    nc = seq // SSD_CHUNK
    cl = SSD_CHUNK
    xf = xs.astype(jnp.float32)
    xdt = (xf * dt[..., None]).reshape(bsz, nc, cl, ng, hpg, hp)
    bc = b_in.astype(jnp.float32).reshape(bsz, nc, cl, ng, ns)
    cc = c_in.astype(jnp.float32).reshape(bsz, nc, cl, ng, ns)
    log_decay = (dt * a).reshape(bsz, nc, cl, ng, hpg).transpose(0, 1, 3, 4, 2)
    a_cum = jnp.cumsum(log_decay, axis=-1)
    causal = jnp.tril(jnp.ones((cl, cl), dtype=bool))
    seg = a_cum[..., :, None] - a_cum[..., None, :]
    decay = jnp.exp(jnp.where(causal, seg, -jnp.inf))
    cb = jnp.einsum("bclgn,bcsgn->bcgls", cc, bc)
    y_diag = jnp.einsum("bcgrls,bcsgrp->bclgrp", cb[:, :, :, None] * decay, xdt)
    decay_to_end = jnp.exp(a_cum[..., -1:] - a_cum)
    chunk_states = jnp.einsum("bclgn,bcgrl,bclgrp->bcgrpn", bc, decay_to_end, xdt)
    chunk_decay = jnp.exp(a_cum[..., -1])

    def step(h, inp):
        st, dec = inp
        return h * dec[..., None, None] + st, h

    h0 = jnp.zeros((bsz, ng, hpg, hp, ns), jnp.float32)
    _, prev = lax.scan(step, h0, (jnp.moveaxis(chunk_states, 1, 0), jnp.moveaxis(chunk_decay, 1, 0)))
    prev = jnp.moveaxis(prev, 0, 1)
    y_off = jnp.einsum("bclgn,bcgrpn,bcgrl->bclgrp", cc, prev, jnp.exp(a_cum))
    y = (y_diag + y_off).reshape(bsz, seq, nh, hp)
    return y + xf * d_skip.astype(jnp.float32)[:, None]

def first_inputs(seed: int = 0) -> dict:
    key = jax.random.key(seed)
    ks = jax.random.split(key, 16)
    f = jnp.float32
    nrm = jax.random.normal
    x = nrm(ks[0], (BATCH, SEQ, D_MODEL), f)
    c = nrm(ks[1], (BATCH, D_MODEL), f)
    w_ada = nrm(ks[2], (DEPTH, D_MODEL, 3 * D_MODEL), f) * D_MODEL ** -0.5
    b_ada = 0.02 * nrm(ks[3], (DEPTH, 3 * D_MODEL), f)
    norm_in_gain = 1.0 + 0.1 * nrm(ks[4], (DEPTH, D_MODEL), f)
    w_in = nrm(ks[5], (DEPTH, D_MODEL, D_PROJ), f) * D_MODEL ** -0.5
    conv_w = nrm(ks[6], (DEPTH, CONV_WIDTH, D_XBC), f) * CONV_WIDTH ** -0.5
    conv_b = 0.02 * nrm(ks[7], (DEPTH, D_XBC), f)
    dt0 = jnp.exp(jax.random.uniform(ks[8], (DEPTH, SSM_HEADS), f, math.log(DT_MIN), math.log(DT_MAX)))
    dt_bias = dt0 + jnp.log(-jnp.expm1(-dt0))
    a_log = jnp.log(jax.random.uniform(ks[9], (DEPTH, SSM_HEADS), f, 1.0, 16.0))
    d_skip = 1.0 + 0.1 * nrm(ks[10], (DEPTH, SSM_HEADS), f)
    sb_norm_gain = 1.0 + 0.1 * nrm(ks[11], (DEPTH, D_ATTN), f)
    ssm_norm_gain = 1.0 + 0.1 * nrm(ks[12], (DEPTH, D_SSM), f)
    w_out = nrm(ks[13], (DEPTH, D_INNER, D_MODEL), f) * D_INNER ** -0.5
    norm_f_gain = 1.0 + 0.1 * nrm(ks[14], (D_MODEL,), f)
    return {"x": x, "c": c, "w_ada": w_ada, "b_ada": b_ada, "norm_in_gain": norm_in_gain,
            "w_in": w_in, "conv_w": conv_w, "conv_b": conv_b, "dt_bias": dt_bias,
            "a_log": a_log, "d_skip": d_skip, "sb_norm_gain": sb_norm_gain,
            "ssm_norm_gain": ssm_norm_gain, "w_out": w_out, "norm_f_gain": norm_f_gain}

def first_block(x, c, w_ada, b_ada, norm_in_gain, w_in, conv_w, conv_b, dt_bias, a_log,
              d_skip, sb_norm_gain, ssm_norm_gain, w_out, norm_f_gain):
    bsz, seq, _ = x.shape
    splits = [D_ATTN, 2 * D_ATTN, 3 * D_ATTN, 4 * D_ATTN, 4 * D_ATTN + D_XBC,
              4 * D_ATTN + D_XBC + SSM_HEADS]
    c_act = jax.nn.silu(c)
    for layer in range(DEPTH):
        mod = c_act @ w_ada[layer] + b_ada[layer]
        shift, scale, gate = jnp.split(mod, 3, axis=-1)
        h = rms_norm(x, norm_in_gain[layer]) * (1.0 + scale[:, None, :]) + shift[:, None, :]

        proj = h @ w_in[layer]
        q, k, v, z_attn, xbc, dt_raw, z_ssm = jnp.split(proj, splits, axis=-1)

        o = stick_breaking_attention(
            q.reshape(bsz, seq, SB_HEADS, SB_HEAD_DIM),
            k.reshape(bsz, seq, SB_HEADS, SB_HEAD_DIM),
            v.reshape(bsz, seq, SB_HEADS, SB_HEAD_DIM)).reshape(bsz, seq, D_ATTN)
        y_attn = rms_norm(o, sb_norm_gain[layer]) * jax.nn.silu(z_attn)

        xbc = jax.nn.silu(causal_depthwise_conv(xbc, conv_w[layer], conv_b[layer]))
        xs, b_ssm, c_ssm = jnp.split(xbc, [D_SSM, D_SSM + SSM_GROUPS * SSM_STATE], axis=-1)
        dt = jax.nn.softplus((dt_raw + dt_bias[layer]).astype(jnp.float32))
        a = -jnp.exp(a_log[layer].astype(jnp.float32))
        y = ssd_scan(xs.reshape(bsz, seq, SSM_HEADS, SSM_HEAD_DIM), dt, a,
                     b_ssm.reshape(bsz, seq, SSM_GROUPS, SSM_STATE),
                     c_ssm.reshape(bsz, seq, SSM_GROUPS, SSM_STATE), d_skip[layer])
        y = y.reshape(bsz, seq, D_SSM).astype(x.dtype)
        y_ssm = rms_norm(y * jax.nn.silu(z_ssm), ssm_norm_gain[layer])

        mixed = jnp.concatenate([y_attn, y_ssm], axis=-1) @ w_out[layer]
        x = x + gate[:, None, :] * mixed
    return rms_norm(x, norm_f_gain)


DEPTH_2 = 2

ROPE_THETA = 500000.0
D_FF = 4 * D_MODEL
N_EVEN = (DEPTH_2 + 1) // 2
N_ODD = DEPTH_2 // 2
A_HEADS = 8
A_HEAD_DIM = 64
A_WIDTH = A_HEADS * A_HEAD_DIM
A_ROT_DIM = A_HEAD_DIM // 4
IDX_HEADS = 16
IDX_DIM = 64
TOPK_MAX = 256
B_GROUPS = 8
B_GROUP_DIM = 64
B_WIDTH = B_GROUPS * B_GROUP_DIM
CONV_WIDTH_2 = 3
EVEN_COLS = (A_WIDTH, A_WIDTH, A_WIDTH,
             IDX_HEADS * IDX_DIM, IDX_DIM, IDX_HEADS,
             B_WIDTH, B_WIDTH, B_WIDTH)
EVEN_IN_WIDTH = sum(EVEN_COLS)
EVEN_OUT_WIDTH = A_WIDTH + B_WIDTH
C_HEADS = 16
C_NOPE_DIM = 64
C_ROPE_DIM = 32
C_V_DIM = 64
C_Q_RANK = 384
C_KV_RANK = 256


def _rms_norm(x, gain):
    xf = x.astype(jnp.float32)
    xf = xf * lax.rsqrt(jnp.mean(xf * xf, axis=-1, keepdims=True) + NORM_EPS)
    return xf.astype(x.dtype) * gain

def _rope_cos_sin(positions, rot_dim):
    inv_freq = ROPE_THETA ** (-jnp.arange(0, rot_dim, 2, dtype=jnp.float32) / rot_dim)
    ang = positions.astype(jnp.float32)[..., None] * inv_freq
    return jnp.cos(ang)[:, :, None, :], jnp.sin(ang)[:, :, None, :]

def _rotate(x, cos, sin):
    xf = x.astype(jnp.float32)
    x1, x2 = jnp.split(xf, 2, axis=-1)
    return jnp.concatenate([x1 * cos - x2 * sin, x2 * cos + x1 * sin], axis=-1).astype(x.dtype)

def _partial_rope(x, cos, sin):
    rot = 2 * cos.shape[-1]
    return jnp.concatenate([_rotate(x[..., :rot], cos, sin), x[..., rot:]], axis=-1)

def _to_blocks(a):
    b, s = a.shape[:2]
    return jnp.moveaxis(a.reshape(b, s // Q_BLOCK, Q_BLOCK, *a.shape[2:]), 1, 0)

def _from_blocks(o):
    nb, b, qb = o.shape[:3]
    return jnp.moveaxis(o, 0, 1).reshape(b, nb * qb, *o.shape[3:])

def _dsa_attention(q, k, v, q_idx, k_idx, w_idx):
    bsz, s, h, dh = q.shape
    n_blocks = s // Q_BLOCK
    top_k = min(TOPK_MAX, s // 4)
    key_pos = jnp.arange(s, dtype=jnp.int32)
    gather = jax.vmap(lambda kb, ib: kb[ib])

    def block(args):
        qb, qib, wib, start = args
        q_pos = start + jnp.arange(Q_BLOCK, dtype=jnp.int32)
        causal = key_pos[None, :] <= q_pos[:, None]
        rel = jax.nn.relu(jnp.einsum('bqhd,bsd->bqhs', qib, k_idx).astype(jnp.float32))
        score = jnp.einsum('bqhs,bqh->bqs', rel, wib)
        score = jnp.where(causal[None], score, -jnp.inf)
        _, sel = lax.top_k(score, top_k)
        valid = sel <= q_pos[None, :, None]
        k_sel = gather(k, sel)
        v_sel = gather(v, sel)
        logits = jnp.einsum('bqhd,bqkhd->bhqk', qb, k_sel).astype(jnp.float32) * (dh ** -0.5)
        logits = jnp.where(valid[:, None], logits, -jnp.inf)
        p = jax.nn.softmax(logits, axis=-1).astype(v.dtype)
        return jnp.einsum('bhqk,bqkhd->bqhd', p, v_sel).reshape(bsz, Q_BLOCK, h * dh)

    starts = jnp.arange(n_blocks, dtype=jnp.int32) * Q_BLOCK
    out = lax.map(block, (_to_blocks(q), _to_blocks(q_idx), _to_blocks(w_idx), starts))
    return _from_blocks(out)

def _short_conv(x_in, gate_b, gate_c, conv_w):
    u = gate_c * x_in
    y = lax.conv_general_dilated(u, conv_w[:, None, :].astype(u.dtype), window_strides=(1,),
                                 padding=[(CONV_WIDTH_2 - 1, 0)],
                                 dimension_numbers=('NWC', 'WIO', 'NWC'),
                                 feature_group_count=u.shape[-1])
    return gate_b * y

def _sparse_attn_conv_mixer(h, rope_quarter, w_in, conv_w, w_out):
    cos, sin = rope_quarter
    bsz, s, _ = h.shape
    proj = h @ w_in
    offsets = np.cumsum(EVEN_COLS)[:-1].tolist()
    q, k, v, q_idx, k_idx, w_idx, gate_b, gate_c, x_in = jnp.split(proj, offsets, axis=-1)
    q = _partial_rope(q.reshape(bsz, s, A_HEADS, A_HEAD_DIM), cos, sin)
    k = _partial_rope(k.reshape(bsz, s, A_HEADS, A_HEAD_DIM), cos, sin)
    v = v.reshape(bsz, s, A_HEADS, A_HEAD_DIM)
    q_idx = _partial_rope(q_idx.reshape(bsz, s, IDX_HEADS, IDX_DIM), cos, sin)
    k_idx = _partial_rope(k_idx[:, :, None, :], cos, sin)[:, :, 0, :]
    w_idx = w_idx.astype(jnp.float32) * (IDX_HEADS ** -0.5 * IDX_DIM ** -0.5)
    attn = _dsa_attention(q, k, v, q_idx, k_idx, w_idx)
    conv = _short_conv(x_in, gate_b, gate_c, conv_w)
    return jnp.concatenate([attn, conv], axis=-1) @ w_out

def _mla_mixer(h, rope_mla, w_dq, q_norm, w_uq, w_dkv, kv_norm, w_ukv, w_o):
    cos, sin = rope_mla
    bsz, s, _ = h.shape
    q = (_rms_norm(h @ w_dq, q_norm) @ w_uq).reshape(bsz, s, C_HEADS, C_NOPE_DIM + C_ROPE_DIM)
    q_nope = q[..., :C_NOPE_DIM]
    q_rope = _rotate(q[..., C_NOPE_DIM:], cos, sin)
    kv_a = h @ w_dkv
    c_kv = _rms_norm(kv_a[..., :C_KV_RANK], kv_norm)
    k_rope = _rotate(kv_a[..., C_KV_RANK:][:, :, None, :], cos, sin)[:, :, 0, :]
    kv = (c_kv @ w_ukv).reshape(bsz, s, C_HEADS, C_NOPE_DIM + C_V_DIM)
    k_nope, v = kv[..., :C_NOPE_DIM], kv[..., C_NOPE_DIM:]
    scale = (C_NOPE_DIM + C_ROPE_DIM) ** -0.5
    key_pos = jnp.arange(s, dtype=jnp.int32)

    def block(args):
        qnb, qrb, start = args
        q_pos = start + jnp.arange(Q_BLOCK, dtype=jnp.int32)
        causal = key_pos[None, :] <= q_pos[:, None]
        logits = (jnp.einsum('bqhd,bshd->bhqs', qnb, k_nope)
                  + jnp.einsum('bqhr,bsr->bhqs', qrb, k_rope)).astype(jnp.float32) * scale
        logits = jnp.where(causal[None, None], logits, -jnp.inf)
        p = jax.nn.softmax(logits, axis=-1).astype(v.dtype)
        return jnp.einsum('bhqs,bshd->bqhd', p, v).reshape(bsz, Q_BLOCK, C_HEADS * C_V_DIM)

    starts = jnp.arange(s // Q_BLOCK, dtype=jnp.int32) * Q_BLOCK
    out = lax.map(block, (_to_blocks(q_nope), _to_blocks(q_rope), starts))
    return _from_blocks(out) @ w_o

def _squared_relu_mlp(h, w1, w2):
    return jnp.square(jax.nn.relu(h @ w1)) @ w2

def second_inputs(seed: int = 0) -> dict:
    key = jax.random.key(seed)
    ks = jax.random.split(key, 20)

    def dense(k, shape, fan_in):
        return jax.random.normal(k, shape, jnp.float32) * (fan_in ** -0.5)

    def gain(k, shape):
        return 1.0 + 0.02 * jax.random.normal(k, shape, jnp.float32)

    return {
        'x': jax.random.normal(ks[0], (BATCH, SEQ, D_MODEL), jnp.float32),
        'positions': jnp.broadcast_to(jnp.arange(SEQ, dtype=jnp.int32), (BATCH, SEQ)),
        'norm_mix_pre': gain(ks[1], (DEPTH_2, D_MODEL)),
        'norm_mix_post': gain(ks[2], (DEPTH_2, D_MODEL)),
        'norm_ffn_pre': gain(ks[3], (DEPTH_2, D_MODEL)),
        'norm_ffn_post': gain(ks[4], (DEPTH_2, D_MODEL)),
        'even_w_in': dense(ks[5], (N_EVEN, D_MODEL, EVEN_IN_WIDTH), D_MODEL),
        'even_conv_w': dense(ks[6], (N_EVEN, CONV_WIDTH_2, B_WIDTH), CONV_WIDTH_2),
        'even_w_out': dense(ks[7], (N_EVEN, EVEN_OUT_WIDTH, D_MODEL), EVEN_OUT_WIDTH),
        'odd_w_dq': dense(ks[8], (N_ODD, D_MODEL, C_Q_RANK), D_MODEL),
        'odd_q_norm': gain(ks[9], (N_ODD, C_Q_RANK)),
        'odd_w_uq': dense(ks[10], (N_ODD, C_Q_RANK, C_HEADS * (C_NOPE_DIM + C_ROPE_DIM)), C_Q_RANK),
        'odd_w_dkv': dense(ks[11], (N_ODD, D_MODEL, C_KV_RANK + C_ROPE_DIM), D_MODEL),
        'odd_kv_norm': gain(ks[12], (N_ODD, C_KV_RANK)),
        'odd_w_ukv': dense(ks[13], (N_ODD, C_KV_RANK, C_HEADS * (C_NOPE_DIM + C_V_DIM)), C_KV_RANK),
        'odd_w_o': dense(ks[14], (N_ODD, C_HEADS * C_V_DIM, D_MODEL), C_HEADS * C_V_DIM),
        'mlp_w1': dense(ks[15], (DEPTH_2, D_MODEL, D_FF), D_MODEL),
        'mlp_w2': dense(ks[16], (DEPTH_2, D_FF, D_MODEL), D_FF),
    }

def second_block(x, positions, norm_mix_pre, norm_mix_post, norm_ffn_pre, norm_ffn_post,
              even_w_in, even_conv_w, even_w_out,
              odd_w_dq, odd_q_norm, odd_w_uq, odd_w_dkv, odd_kv_norm, odd_w_ukv, odd_w_o,
              mlp_w1, mlp_w2):
    rope_quarter = _rope_cos_sin(positions, A_ROT_DIM)
    rope_mla = _rope_cos_sin(positions, C_ROPE_DIM)
    for layer in range(DEPTH_2):
        j = layer // 2
        hn = _rms_norm(x, norm_mix_pre[layer])
        if layer % 2 == 0:
            mix = _sparse_attn_conv_mixer(hn, rope_quarter, even_w_in[j], even_conv_w[j], even_w_out[j])
        else:
            mix = _mla_mixer(hn, rope_mla, odd_w_dq[j], odd_q_norm[j], odd_w_uq[j],
                             odd_w_dkv[j], odd_kv_norm[j], odd_w_ukv[j], odd_w_o[j])
        x = x + _rms_norm(mix, norm_mix_post[layer])
        hn = _rms_norm(x, norm_ffn_pre[layer])
        x = x + _rms_norm(_squared_relu_mlp(hn, mlp_w1[layer], mlp_w2[layer]), norm_ffn_post[layer])
    return x


def setup_inputs(seed=0):
    out = dict(first_inputs(seed))
    for name, value in second_inputs(seed + 1).items():
        if name != "x":
            out[name + "_2"] = value
    return out


def reference(
    x, c, w_ada, b_ada, norm_in_gain, w_in, conv_w, conv_b, dt_bias, a_log, d_skip,
    sb_norm_gain, ssm_norm_gain, w_out, norm_f_gain, positions_2, norm_mix_pre_2,
    norm_mix_post_2, norm_ffn_pre_2, norm_ffn_post_2, even_w_in_2, even_conv_w_2, even_w_out_2,
    odd_w_dq_2, odd_q_norm_2, odd_w_uq_2, odd_w_dkv_2, odd_kv_norm_2, odd_w_ukv_2, odd_w_o_2,
    mlp_w1_2, mlp_w2_2,
):
    x = first_block(
        x, c, w_ada, b_ada, norm_in_gain, w_in, conv_w, conv_b, dt_bias, a_log, d_skip,
        sb_norm_gain, ssm_norm_gain, w_out, norm_f_gain,
    )
    return second_block(
        x, positions_2, norm_mix_pre_2, norm_mix_post_2, norm_ffn_pre_2, norm_ffn_post_2,
        even_w_in_2, even_conv_w_2, even_w_out_2, odd_w_dq_2, odd_q_norm_2, odd_w_uq_2,
        odd_w_dkv_2, odd_kv_norm_2, odd_w_ukv_2, odd_w_o_2, mlp_w1_2, mlp_w2_2,
    )


_drawn_inputs = setup_inputs


def setup_inputs(seed=0):
    import zlib

    import numpy as np

    out = dict(_drawn_inputs(seed))
    spreads = {}
    factors = {'conv_b': 4.149,
     'norm_mix_post_2': 3.173,
     'norm_ffn_pre_2': 3.345,
     'norm_ffn_post_2': 3.465,
     'odd_q_norm_2': 8.0,
     'odd_kv_norm_2': 4.819}
    for name, (base, spread) in spreads.items():
        noise = np.random.default_rng([zlib.crc32(name.encode()), seed]).standard_normal(out[name].shape)
        drawn = base * np.exp(spread * noise) if base else spread * noise
        out[name] = jnp.asarray(drawn.astype(out[name].dtype))
    for name, factor in factors.items():
        out[name] = (out[name] * factor).astype(out[name].dtype)
    return out
```

```python
import math
from contextlib import ExitStack

import concourse.bass as bass
from concourse import mybir

F32 = mybir.dt.float32
F32R = mybir.dt.float32r
I32 = mybir.dt.int32
ACT = mybir.ActivationFunctionType
ALU = mybir.AluOpType
AX = mybir.AxisListType.X

P = 128
SEQ = 512
DM = 1024
TT = SEQ // P
KT = DM // P
UNIT = 2048
NEG = -1e30
DROPPED = -3e38
CHOSEN = -2e38
EPS = 1e-6
H1 = 16
HD = 64
GROUPS = 2
HG = H1 // GROUPS
XBC_T = 12
A_H = 8
TOPK = 128
C_H = 16
C_QK = 96
C_NOPE = 64
Q_RANK = 384
KV_RANK = 256
D_FF = 4096
THETA = 500000.0
N_PARAMS = 16
ROUNDER = 1.5 * 2.0 ** 23
TWO_PI = [6.28125, 1014 / 2.0 ** 19, 2 * math.pi - 6.28125 - 1014 / 2.0 ** 19]
PI_BELOW = 3.1415925
CLAMP = 20.0
IDX_AT = {1: 0, 2: 256, 3: 640}


def phase_table():
    def rounds(n):
        return [n] * 4, [n, n, n, 0]

    rows = [
        ("ada_ss", 8, ([1] * 4, [0] * 4)), ("q", 4, rounds(2)), ("k", 4, rounds(2)), ("v", 4, rounds(2)),
        ("xbc", 6, rounds(3)), ("dt", 1, ([1, 0, 0, 0], [0] * 4)), ("z_ssm", 4, rounds(2)),
        ("z_attn", 4, rounds(2)), ("ada_g", 4, ([1, 1, 0, 0], [0] * 4)), ("wout_a", 4, rounds(2)),
        ("wout_s", 4, rounds(2)), ("qi", 4, rounds(2)), ("kiw", 1, rounds(1)), ("qk2", 4, rounds(2)),
        ("v2", 2, rounds(1)), ("gates", 6, rounds(3)), ("wo2", 4, rounds(2)), ("mlp0", 32, rounds(24)),
        ("dq", 2, rounds(1)), ("dkv", 2, rounds(1)), ("uq", 3, rounds(3)),
        ("ukv", 2, ([4] * 4, [4, 4, 4, 2])), ("wo3", 4, rounds(2)), ("mlp1", 32, rounds(24)),
    ]
    unit, free, full, table = 0, [0] * 4, [0] * 4, {}
    for name, units, (f, g) in rows:
        table[name] = (unit, list(free), list(full), units)
        unit += units
        free = [a + b for a, b in zip(free, f)]
        full = [a + b for a, b in zip(full, g)]
    table["end"] = (unit, list(free), list(full), 0)
    return table


def transpose_table():
    rows = [("params", 2, 0), ("h", 8, 1), ("y_attn", 8, 1), ("scan", 10, 0), ("y_ssm", 8, 1), ("mix0", 8, 1),
            ("qi", 8, 0), ("ki", 1, 0), ("qk", 8, 0), ("attn", 4, 1), ("ffn0", 8, 1), ("mix1", 8, 1),
            ("cq", 3, 1), ("ckv", 2, 1), ("heads", 2 * C_H, 0), ("lat", 8, 1), ("ffn1", 8, 1)]
    n, split, table = 0, 0, {}
    for name, groups, is_split in rows:
        table[name] = (n, split)
        n += groups
        split += groups * is_split
    return table


def build_program(nc, x, c, w_ada, b_ada, norm_in_gain, w_in, conv_w, conv_b, dt_bias, a_log, d_skip,
                  sb_norm_gain, ssm_norm_gain, w_out, norm_f_gain, positions_2, norm_mix_pre_2,
                  norm_mix_post_2, norm_ffn_pre_2, norm_ffn_post_2, even_w_in_2, even_conv_w_2,
                  even_w_out_2, odd_w_dq_2, odd_q_norm_2, odd_w_uq_2, odd_w_dkv_2, odd_kv_norm_2,
                  odd_w_ukv_2, odd_w_o_2, mlp_w1_2, mlp_w2_2, out):
    PH = phase_table()
    TR = transpose_table()
    ctx = ExitStack()
    sems = {}

    def S(name):
        if name not in sems:
            sems[name] = ctx.enter_context(nc.semaphore(name))
        return sems[name]

    cursor = [(nc.sbuf_base + 63) // 64 * 64]

    def at(name, shape, dtype=F32, offset=None):
        size = 4
        for n in shape[1:]:
            size *= n
        if offset is None:
            offset = cursor[0]
            cursor[0] += (size + 31) // 32 * 32
        return nc.alloc_sbuf_tensor_at(name, shape, dtype, offset=offset)

    wraw = [at(f"wraw{s}", [P, UNIT]) for s in range(2)]
    whi = [at(f"whi{s}", [P, UNIT], F32R) for s in range(2)]
    wlo = [at(f"wlo{s}", [P, UNIT], F32R) for s in range(2)]
    hhi = at("hhi", [P, KT, SEQ], F32R)
    hlo = at("hlo", [P, KT, SEQ], F32R)
    xres = at("xres", [P, TT, DM])
    ident = at("ident", [P, P])
    identr = at("identr", [P, P], F32R)
    ones = at("ones", [P, P])
    tri_le = at("tri_le", [P, P])
    tri_gt = at("tri_gt", [P, P])
    neg_ge = at("neg_ge", [P, P], F32R)
    neg_one = at("neg_one", [P, P], F32R)
    mask_t = at("mask_t", [P, P], F32R)
    mask_q = at("mask_q", [P, P], F32R)
    scratch = at("scratch", [P, P])
    scratch1 = at("scratch1", [P, P])
    junk = at("junk", [P, 2, DM], mybir.dt.bfloat16)
    sinall = at("sinall", [P, TT, 24])
    col_a = at("col_a", [P, P])
    col_b = at("col_b", [P, 32])
    stat = at("stat", [P, 16, TT])
    rstd = at("rstd", [P, 16, TT])
    mhalf = at("mhalf", [P, TT])
    cact = at("cact", [P, KT])
    small = at("small", [P, 64])
    cosq = at("cosq", [P, TT, 8])
    sinq = at("sinq", [P, TT, 8])
    cosm = at("cosm", [P, TT, 16])
    sinm = at("sinm", [P, TT, 16])
    row_a = at("row_a", [P, DM])
    row_b = at("row_b", [P, DM])
    A0 = cursor[0]
    KB = 1024

    def arena(name, shape, kb, dtype=F32):
        return at(name, shape, dtype, offset=A0 + int(kb * KB))

    xn = arena("xn", [P, TT, DM], 0)
    b_row = arena("b_row", [P, 2 * DM], 40)
    mod = arena("mod", [P, 2 * DM], 48)
    prm_a = arena("prm_a", [P, P], 60)
    prm_b = arena("prm_b", [32, P], 60.5)
    pos_i = arena("pos_i", [P, TT], 64, I32)
    pos_f = arena("pos_f", [P, TT], 64.25)
    freq = arena("freq", [P, 24], 64.5)
    ang = arena("ang", [P, TT, 24], 65)
    ang_n = arena("ang_n", [P, TT, 24], 66)
    ang_s = arena("ang_s", [P, TT, 24], 67)
    chi = arena("chi", [P, KT, P], 70, F32R)
    clo = arena("clo", [P, KT, P], 74, F32R)
    gate = arena("gate", [P, DM], 98)
    chi2 = arena("chi2", [P, KT, P], 16, F32R)
    clo2 = arena("clo2", [P, KT, P], 20, F32R)
    qt = arena("qt", [P, KT, SEQ], 0)
    kt = arena("kt", [P, KT, SEQ], 16)
    vo = arena("vo", [P, TT, DM], 32)
    sb_l = arena("sb_l", [P, 1280], 48)
    sb_hi = arena("sb_hi", [P, 1280], 53, F32R)
    sb_lo = arena("sb_lo", [P, 1280], 58, F32R)
    sb_w = arena("sb_w", [P, 1280], 63)
    za = arena("za", [P, TT, DM], 0)
    xn_a = arena("xn_a", [P, TT, DM], 16)
    mix = arena("mix", [P, TT, DM], 48)
    xbc = arena("xbc", [P, XBC_T, SEQ + 3], 68)
    dts = arena("dts", [P, 6, TT * H1], 92.5)
    conv_acc = arena("conv_acc", [P, 2, SEQ], 94)
    zs = xres
    yt = arena("yt", [P, TT, DM], 0)
    xdt = arena("xdt", [P, DM], 16)
    xdte = arena("xdte", [P, DM], 20)
    hst = arena("hst", [P, DM], 24)
    b_tm = arena("b_tm", [P, TT, 2 * P], 28)
    cbm = arena("cbm", [P, 8, P], 32)
    ldm = arena("ldm", [P, H1, P], 36)
    dec = arena("dec", [P, HG, P], 44)
    off = arena("off", [P, SEQ], 64)
    xd = arena("xd", [P, SEQ], 66)
    qi_tm = arena("qi_tm", [P, TT, DM], 0)
    qk_tm = arena("qk_tm", [P, TT, DM], 16)
    kiw = arena("kiw", [P, TT, 144], 32)
    v2 = arena("v2", [P, TT, 512], 34.5)
    qit = arena("qit", [P, KT, SEQ], 42.5)
    kit = arena("kit", [P, SEQ], 58.5)
    score = arena("score", [P, TT, SEQ], 60.5)
    relu_s = arena("relu_s", [P, 2, 1152], 68.5)
    top8 = arena("top8", [P, TT, 8], 77.5)
    qkt = arena("qkt", [P, KT, SEQ], 78)
    rt = arena("rt", [P, 4, TT * H1 * 8], 94)
    bias_q = arena("bias_q", [P, TT, SEQ], 0, F32R)
    pr = [arena("pr0", [P, 1280], 8), arena("pr1", [P, 1280], 13)]
    prt = [arena("prt0", [P, 1280], 18), arena("prt1", [P, 1280], 23)]
    mx = arena("mx", [P, 2, TT], 77.625)
    den = arena("den", [P, 2, TT], 77.75)
    gb = arena("gb", [P, TT, SEQ], 42.5)
    gc = arena("gc", [P, TT, SEQ + 2], 50.5)
    xi = arena("xi", [P, TT, SEQ], 68.5)
    ca = arena("ca", [P, TT, SEQ], 94)
    mix2 = arena("mix2", [P, TT, DM], 58.75)
    mh_hi = [arena(f"mh_hi{s}", [P, 4, SEQ], 16 + 16 * s, F32R) for s in range(2)]
    mh_lo = [arena(f"mh_lo{s}", [P, 4, SEQ], 24 + 16 * s, F32R) for s in range(2)]
    mh_r = arena("mh_r", [P, 2, SEQ], 48)
    mixm = arena("mixm", [P, TT, DM], 56)
    kva = arena("kva", [P, TT, 288], 16)
    cq = arena("cq", [P, TT, Q_RANK], 21)
    q_tm = arena("q_tm", [P, TT, C_H * C_QK], 27)
    k_tm = arena("k_tm", [P, TT, C_H, C_QK], 51)
    v3 = arena("v3", [P, TT, DM], 75)
    rtm = arena("rtm", [P, 4, TT * C_H * 16], 0)
    qth = [arena(f"qth{s}", [P, SEQ], 2 * s) for s in range(2)]
    kth = [arena(f"kth{s}", [P, SEQ], 4 + 2 * s) for s in range(2)]
    pr3 = [arena("pr30", [P, 1280], 8), arena("pr31", [P, 1280], 16)]
    prt3 = [arena("prt30", [P, 1280], 21), arena("prt31", [P, 1280], 91)]
    mx3 = arena("mx3", [P, 2, TT], 14)
    den3 = arena("den3", [P, 2, TT], 14.5)
    mix3 = arena("mix3", [P, TT, DM], 27)
    assert A0 + 102 * KB <= nc.sbuf_usable_end, (A0, nc.sbuf_usable_end)

    PDT = ctx.enter_context(nc.psum_tensor("PDT", [P, 4, SEQ], F32))
    PM = ctx.enter_context(nc.psum_tensor("PM", [P, 4, SEQ], F32))
    PD = [PDT[:, b, :] for b in range(4)]
    PX = [PM, PDT]

    C_C, C_CW, C_CB, C_SBG, C_SSG, C_MIX, C_FFN = 0, 8, 56, 68, 76, 84, 100
    C_QN, C_KN, C_CW2 = 0, 3, 5
    ROWS_A, ROWS_B = 116, 17

    SB_CHUNKS = [[(1, 0), (3, 384)], [(2, 0)], [(0, 0)]]
    SB_FIRST = [0, 512, 768]
    SB_WIDE = [512, 256, 512]
    SB_AT = {1: (0, 0), 3: (0, 384), 2: (1, 0), 0: (2, 0)}
    QB_AT = {3: (0, 0), 2: (1, 0), 0: (1, 384), 1: (2, 0)}
    QB_FIRST = {3: 0, 2: 512, 0: 896, 1: 1024}

    def kmajor(w):
        return w.rearrange("(k p) n -> p k n", p=P)

    w_ada_v, w_in_v, w_out_v = kmajor(w_ada[0]), kmajor(w_in[0]), kmajor(w_out[0])
    w_even_v, w_eo_v = kmajor(even_w_in_2[0]), kmajor(even_w_out_2[0])
    w_dq_v, w_uq_v, w_dkv_v = kmajor(odd_w_dq_2[0]), kmajor(odd_w_uq_2[0]), kmajor(odd_w_dkv_2[0])
    w_ukv_v, w_oo_v = kmajor(odd_w_ukv_2[0]), kmajor(odd_w_o_2[0])
    w1_v = [kmajor(mlp_w1_2[j]) for j in range(2)]
    w2_v = [kmajor(mlp_w2_2[j]) for j in range(2)]

    def wview(t, kn, n):
        return t[:, 0:kn * n].rearrange("p (k n) -> p k n", k=kn)

    def fl(ap):
        return ap.bitcast(F32)

    def loop(eng, n, body):
        if n == 1:
            body(0)
        else:
            with eng.Fori(0, n) as i:
                body(i)

    def dyn(t, i, b):
        return t[:, bass.ds(i * 4 + b, 1), :]

    def phase_done(eng, name):
        names = list(PH)
        after = PH[names[names.index(name) + 1]][1]
        for b in range(4):
            if after[b] > PH[name][1][b]:
                eng.wait_ge(S(f"bank_free{b}"), after[b])

    def full_wait(eng, name, b, r, unit):
        if b < 3:
            eng.wait_ge(S(f"bank_full{b}"), r + (PH[name][2][b] + 1))
        else:
            eng.wait_ge(S("w_used"), unit + 1)

    block = ctx.enter_context(nc.Block())

    @block.sync
    def _(sp):
        def load(dst, src, sem="params"):
            sp.dma_start(dst, src).then_inc(S(sem), 16)

        def unit(u, par, kn, n, src):
            if not isinstance(u, int) or u >= 2:
                sp.wait_ge(S("w_split"), u - 1)
            sp.dma_start(wview(wraw[par], kn, n), src).then_inc(S(f"w_loaded{par}"), 16)

        def columns(name, w, n_chunks, c0, k0=0):
            u0 = PH[name][0]

            def body(i):
                cc = c0 + i * 512 if isinstance(i, int) else sp.snap(i * 512 + c0)
                for h in range(2):
                    par = (u0 + h) % 2
                    unit(i * 2 + (u0 + h), par, 4, 512,
                         w[:, k0 + 4 * h:k0 + 4 * h + 4, bass.ds(cc, 512)])
            loop(sp, n_chunks, body)

        def mlp(name, j):
            u0 = PH[name][0]

            def up(i, d):
                cc = i * 1024 + 512 * d if isinstance(i, int) else sp.snap(i * 1024 + 512 * d)
                return [w1_v[j][:, 4 * h:4 * h + 4, bass.ds(cc, 512)] for h in range(2)]

            def down(i, d):
                kk = i * 8 + 4 * d if isinstance(i, int) else sp.snap(i * 8 + 4 * d)
                return [w2_v[j][:, bass.ds(kk, 4), 512 * h:512 * h + 512] for h in range(2)]

            def four(i, first, srcs):
                for n, s in enumerate(srcs):
                    unit(i * 8 + (u0 + first + n), (u0 + first + n) % 2, 4, 512, s)

            four(0, 0, up(0, 0))
            with sp.Fori(0, 3) as i:
                four(i, 2, up(i, 1))
                four(i, 4, down(i, 0))
                four(i, 6, up(i, 2))
                four(i, 8, down(i, 1))
            four(3, 2, up(3, 1))
            four(3, 4, down(3, 0))
            four(3, 6, down(3, 1))

        load(prm_a[C_C:C_C + 8, :], c.rearrange("a (k p) -> (a k) p", p=P), "params_c")
        for u in range(2):
            unit(u, u % 2, 4, 512, w_ada_v[:, 4 * u:4 * u + 4, DM:DM + 512])
        load(xres[:, :, :], x[0].rearrange("(t p) n -> p t n", p=P), "x_loaded")
        load(prm_a[C_CW:C_CW + 48, :], conv_w[0].rearrange("j (k p) -> (j k) p", p=P))
        load(prm_a[C_CB:C_CB + 12, :], conv_b[0].rearrange("(k p) -> k p", p=P))
        load(prm_a[C_SBG:C_SBG + 8, :], sb_norm_gain[0].rearrange("(k p) -> k p", p=P))
        load(prm_a[C_SSG:C_SSG + 8, :], ssm_norm_gain[0].rearrange("(k p) -> k p", p=P))
        load(prm_a[C_MIX:C_MIX + 16, :], norm_mix_pre_2.rearrange("j (k p) -> (j k) p", p=P))
        load(prm_a[C_FFN:C_FFN + 16, :], norm_ffn_pre_2.rearrange("j (k p) -> (j k) p", p=P))
        load(prm_b[C_QN:C_QN + 3, :], odd_q_norm_2[0].rearrange("(k p) -> k p", p=P))
        load(prm_b[C_KN:C_KN + 2, :], odd_kv_norm_2[0].rearrange("(k p) -> k p", p=P))
        load(prm_b[C_CW2:C_CW2 + 12, :], even_conv_w_2[0].rearrange("j (k p) -> (j k) p", p=P))
        with nc.allow_non_contiguous_dma(reason="512 positions"):
            load(pos_i[:, :], positions_2[0].rearrange("(t p) -> p t", p=P))
        load(row_a[:, :], norm_in_gain[0].partition_broadcast(P))
        load(b_row[:, :], b_ada[0][0:2 * DM].partition_broadcast(P))
        load(small[:, 0:16], dt_bias[0].partition_broadcast(P))
        load(small[:, 16:32], a_log[0].partition_broadcast(P))
        load(small[:, 32:48], d_skip[0].partition_broadcast(P))
        load(row_b[:, :], b_ada[0][2 * DM:3 * DM].partition_broadcast(P))
        for u in range(2, 8):
            cc = [DM, DM + 512, 0, 512][u // 2]
            unit(u, u % 2, 4, 512, w_ada_v[:, 4 * (u % 2):4 * (u % 2) + 4, cc:cc + 512])
        columns("q", w_in_v, 2, 0)
        columns("k", w_in_v, 2, DM)
        columns("v", w_in_v, 2, 2 * DM)
        sp.wait_ge(S("h_made"), TT)
        load(row_a[:, :], norm_f_gain.partition_broadcast(P), "row_f")
        columns("xbc", w_in_v, 3, 4 * DM)
        u0 = PH["dt"][0]
        unit(u0, u0 % 2, 8, 16, w_in_v[:, :, 4 * DM + 1536:4 * DM + 1552])
        columns("z_ssm", w_in_v, 2, 4 * DM + 1552)
        columns("z_attn", w_in_v, 2, 3 * DM)
        columns("ada_g", w_ada_v, 2, 2 * DM)
        columns("wout_a", w_out_v, 2, 0)
        columns("wout_s", w_out_v, 2, 0, k0=8)
        sp.wait_ge(S("y_gated"), TT)
        load(xres[:, :, :], x[0].rearrange("(t p) n -> p t n", p=P), "x_again")
        columns("qi", w_even_v, 2, 1536)
        u0 = PH["kiw"][0]
        unit(u0, u0 % 2, 8, 80, w_even_v[:, :, 2560:2640])
        phase_done(sp, "ada_g")
        load(row_b[:, :], norm_mix_post_2[0].partition_broadcast(P), "row_mix0")
        columns("qk2", w_even_v, 2, 0)
        columns("v2", w_even_v, 1, DM)
        columns("gates", w_even_v, 3, 2640)
        sp.wait_ge(S("first_out"), TT)
        load(row_a[:, :], norm_ffn_post_2[0].partition_broadcast(P), "row_ffn0")
        columns("wo2", w_eo_v, 2, 0)
        mlp("mlp0", 0)
        sp.wait_ge(S("post_mix0"), TT)
        load(row_b[:, :], norm_mix_post_2[1].partition_broadcast(P), "row_mix1")
        u0 = PH["dq"][0]
        for h in range(2):
            unit(u0 + h, (u0 + h) % 2, 4, Q_RANK, w_dq_v[:, 4 * h:4 * h + 4, :])
        u0 = PH["dkv"][0]
        for h in range(2):
            unit(u0 + h, (u0 + h) % 2, 4, 288, w_dkv_v[:, 4 * h:4 * h + 4, :])
        u0 = PH["uq"][0]
        for n in range(3):
            unit(u0 + n, (u0 + n) % 2, 3, 512, w_uq_v[:, :, 512 * n:512 * n + 512])
        u0 = PH["ukv"][0]
        for n in range(2):
            unit(u0 + n, (u0 + n) % 2, 2, 1024, w_ukv_v[:, :, 1024 * n:1024 * n + 1024])
        columns("wo3", w_oo_v, 2, 0)
        mlp("mlp1", 1)
        sp.wait_ge(S("post_ffn0"), TT)
        load(row_a[:, :], norm_ffn_post_2[1].partition_broadcast(P), "row_ffn1")
        for t in range(TT):
            sp.wait_ge(S("post_ffn1"), t + 1)
            sp.dma_start(out[0, t * P:(t + 1) * P, :], xres[:, t, :]).then_inc(S("stored"), 16)
        sp.wait_ge(S("stored"), 16 * TT)

    @block.tensor
    def _(pe):
        mm = nc.tensor.matmul

        def bank_wait(name, b, r):
            pe.wait_ge(S(f"bank_free{b}"), r + PH[name][1][b])

        def unit_wait(u):
            pe.wait_ge(S("w_split"), u + 1)

        def tm(bank, n, act, k0, ws, kn, nn, c0, start, stop, t):
            hi, lo = act
            wh, wl = wview(whi[ws], kn, nn), wview(wlo[ws], kn, nn)
            for k in range(kn):
                sth, stl = hi[:, k0 + k, t * P:t * P + P], lo[:, k0 + k, t * P:t * P + P]
                mm(bank, sth, wh[:, k, c0:c0 + n], start=start and k == 0, stop=False)
                mm(bank, sth, wl[:, k, c0:c0 + n], start=False, stop=False)
                last = mm(bank, stl, wh[:, k, c0:c0 + n], start=False, stop=stop and k == kn - 1)
            return last

        def fm(bank, act, k0, ws, f, start, stop):
            hi, lo = act
            wh, wl = wview(whi[ws], 4, 512), wview(wlo[ws], 4, 512)
            for k in range(4):
                sth, stl = wh[:, k, f * P:f * P + P], wl[:, k, f * P:f * P + P]
                mm(bank, sth, hi[:, k0 + k, :], start=start and k == 0, stop=False)
                mm(bank, sth, lo[:, k0 + k, :], start=False, stop=False)
                last = mm(bank, stl, hi[:, k0 + k, :], start=False, stop=stop and k == 3)
            return last

        def full(last, b):
            last.then_inc(S("w_used" if b == 3 else f"bank_full{b}"), 1)

        def two_units(name, first, r, i, stride, feature_major, n=512):
            u0 = PH[name][0] + first
            for h in range(2):
                unit_wait(i * stride + (u0 + h))
                for b in range(4):
                    if h == 0:
                        bank_wait(name, b, r)
                    if feature_major:
                        last = fm(PD[b], (hhi, hlo), 4 * h, (u0 + h) % 2, b, h == 0, h == 1)
                    else:
                        last = tm(PD[b][:, 0:n], n, (hhi, hlo), 4 * h, (u0 + h) % 2, 4, n, 0, h == 0, h == 1, b)
                    if h == 1:
                        full(last, b)
                if h == 0:
                    last.then_inc(S("w_used"), 1)

        def chunks(name, n, feature_major):
            loop(pe, n, lambda i: two_units(name, 0, i, i, 2, feature_major))

        def transposes(name, nk, src):
            for k in range(nk):
                n = TR[name][0] + k
                pe.wait_ge(S("tr_read"), max(TR[name][0], n - 3))
                for t in range(TT):
                    last = nc.tensor.transpose(PM[:, k % 4, t * P:t * P + P], src(t, k), ident[:, :])
                last.then_inc(S("tr_done"), 1)

        def transposed(name, nk):
            pe.wait_ge(S("tr_read"), TR[name][0] + nk)

        def mlp(name, layer):
            u0 = PH[name][0]

            def up(first, r, i):
                two_units(name, first, r, i, 8, True)

            def down(par, first, r, i, m):
                pe.wait_ge(S("hidden_ready"), m * 4 + (32 * layer + 4))
                for h in range(2):
                    unit_wait(i * 8 + (u0 + first + h))
                    for b in range(4):
                        bank_wait(name, b, r + h)
                        full(tm(PD[b], 512, (mh_hi[par], mh_lo[par]), 0, (u0 + first + h) % 2, 4, 512,
                                0, True, True, b), b)

            up(0, 0, 0)
            with pe.Fori(0, 3) as i:
                up(2, i * 6 + 1, i)
                down(0, 4, i * 6 + 2, i, i * 2)
                up(6, i * 6 + 4, i)
                down(1, 8, i * 6 + 5, i, i * 2 + 1)
            up(2, 19, 3)
            down(0, 4, 20, 3, 6)
            down(1, 6, 22, 3, 7)

        pe.wait_ge(S("masks"), 1)
        pe.wait_ge(S("params_c"), 16)
        nc.tensor.transpose(PM[:, 3, 0:8], prm_a[0:8, :], ident[0:8, 0:8]).then_inc(S("tr_done"), 1)
        pe.wait_ge(S("c_split"), 1)

        def ada(name, j, first, chi, clo):
            for h in range(2):
                u = PH[name][0] + first + h
                unit_wait(u)
                if h == 0:
                    bank_wait(name, j, 0)
                wh, wl = wview(whi[u % 2], 4, 512), wview(wlo[u % 2], 4, 512)
                for k in range(4):
                    ch, cl = chi[:, 4 * h + k, :], clo[:, 4 * h + k, :]
                    mm(PD[j], ch, wh[:, k, :], start=h == 0 and k == 0, stop=False)
                    mm(PD[j], ch, wl[:, k, :], start=False, stop=False)
                    last = mm(PD[j], cl, wh[:, k, :], start=False, stop=h == 1 and k == 3)
                last.then_inc(S("w_used"), 1)

        ada("ada_ss", 0, 0, chi, clo)
        pe.wait_ge(S("params"), 16 * N_PARAMS)
        nc.tensor.transpose(PM[:, 2, 0:ROWS_A], prm_a[0:ROWS_A, :], ident[0:ROWS_A, 0:ROWS_A])
        nc.tensor.transpose(PM[:, 2, P:P + ROWS_B], prm_b[0:ROWS_B, :], ident[0:ROWS_B, 0:ROWS_B]).then_inc(S("tr_done"), 1)
        for j in range(1, 4):
            ada("ada_ss", j, 2 * j, chi, clo)
        pe.wait_ge(S("h_made"), TT)
        transposes("h", 8, lambda t, k: xn[:, t, k * P:k * P + P])
        transposed("h", 8)
        chunks("q", 2, True)
        chunks("k", 2, True)
        chunks("v", 2, False)

        def sb_scores(h):
            p0, ft = HD * (h % 2), h // 2
            for n, blocks in enumerate(SB_CHUNKS):
                if h:
                    pe.wait_ge(S("sb_weights"), 3 * (h - 1) + n + 1)
                for m, (s, c0) in enumerate(blocks):
                    w = SEQ - s * P
                    mm(PM[:, n, c0:c0 + w], kt[p0:p0 + HD, ft, s * P:s * P + P], qt[p0:p0 + HD, ft, s * P:SEQ],
                       start=m == 0, stop=False, skip_group_check=True)
                    last = mm(PM[:, n, c0:c0 + P], identr[:, :], mask_t[:, :], start=False, stop=False,
                              skip_group_check=True)
                last.then_inc(S("sb_z"), 1)

        def sb_tails(h):
            for n, blocks in enumerate(SB_CHUNKS):
                pe.wait_ge(S("sb_split"), 3 * h + max(n + 1, 2))
                for m, (s, c0) in enumerate(blocks):
                    for j in range(s, TT):
                        cj, cc = SB_AT[j]
                        a = SB_FIRST[cj] + cc
                        w = SEQ - j * P
                        st = neg_ge if j == s else neg_one
                        o = PM[:, n, c0 + (j - s) * P:c0 + (j - s) * P + w]
                        for part in (sb_hi, sb_lo):
                            last = mm(o, st[:, :], part[:, a:a + w], start=False,
                                      stop=m == len(blocks) - 1 and j == TT - 1 and part is sb_lo,
                                      skip_group_check=True)
                last.then_inc(S("sb_tail"), 1)

        def sb_values(h):
            if h >= 2:
                pe.wait_ge(S("sb_out"), h - 1)
            pe.wait_ge(S("sb_weights"), 3 * h + 3)
            for t in range(TT):
                for s in range(t + 1):
                    cj, cc = SB_AT[s]
                    a = SB_FIRST[cj] + cc + (t - s) * P
                    last = mm(PM[:, 3, (h % 2) * 256 + t * HD:(h % 2) * 256 + t * HD + HD], sb_w[:, a:a + P],
                              vo[:, s, h * HD:h * HD + HD], start=s == 0, stop=s == t)
            last.then_inc(S("sb_pv"), 1)

        for name in ("q", "k", "v"):
            phase_done(pe, name)
        sb_scores(0)
        sb_tails(0)
        for h in range(1, H1):
            sb_scores(h)
            sb_values(h - 1)
            sb_tails(h)
        sb_values(H1 - 1)

        chunks("xbc", 3, True)
        unit_wait(PH["dt"][0])
        bank_wait("dt", 0, 0)
        for t in range(TT):
            last = tm(PD[0][:, 16 * t:16 * t + 16], 16, (hhi, hlo), 0, PH["dt"][0] % 2, 8, 16, 0, True, True, t)
        last.then_inc(S("w_used"), 1)
        chunks("z_ssm", 2, False)
        chunks("z_attn", 2, False)
        pe.wait_ge(S("c_split"), 2)
        ada("ada_g", 0, 0, chi2, clo2)
        ada("ada_g", 1, 2, chi2, clo2)
        pe.wait_ge(S("y_attn_made"), TT)
        transposes("y_attn", 8, lambda t, k: xn_a[:, t, k * P:k * P + P])
        transposed("y_attn", 8)
        chunks("wout_a", 2, False)

        pe.wait_ge(S("conv_done"), XBC_T)
        transposes("scan", 10, lambda t, k: xbc[:, k, t * P:t * P + P])
        transposed("scan", 10)
        pe.wait_ge(S("ld_made"), 1)
        mm(PM[:, 3, 0:64], tri_le[:, :], dts[:, 1, :], start=True, stop=True)
        mm(PM[:, 3, 64:128], tri_gt[:, :], dts[:, 1, :], start=True, stop=True)
        mm(PM[:, 3, 128:192], ones[:, :], dts[:, 1, :], start=True, stop=True).then_inc(S("scan_cum"), 1)
        for g in range(GROUPS):
            for t in range(TT):
                last = mm(PM[:, g, t * P:t * P + P], xbc[:, 8 + g, t * P:t * P + P], xbc[:, 10 + g, t * P:t * P + P],
                          start=True, stop=True)
        last.then_inc(S("scan_cb"), 1)
        pe.wait_ge(S("scan_exps"), 1)
        pe.wait_ge(S("cbm_made"), 1)
        for t in range(TT):
            pe.wait_ge(S("ldm_made"), t + 1)
            for g in range(GROUPS):
                n = 2 * t + g
                if n:
                    pe.wait_ge(S("scan_dec"), n)
                for h in range(HG):
                    last = mm(PM[:, h // 4, (h % 4) * P:(h % 4) * P + P], ldm[:, g * HG + h, :], tri_le[:, :],
                              start=True, stop=True)
                last.then_inc(S("scan_seg"), 1)
                if t:
                    pe.wait_ge(S("hst_made"), min(n, 2 * (TT - 1)))
                    if n == 2 * TT - 1:
                        pe.wait_ge(S("off_read"), n - 2)
                    mm(PM[:, 3, :], xbc[:, 10 + g, t * P:t * P + P], hst[:, g * 512:g * 512 + 512],
                       start=True, stop=True).then_inc(S("scan_off"), 1)
                pe.wait_ge(S("scan_m"), n + 1)
                if n:
                    pe.wait_ge(S("scan_y"), n)
                for h in range(HG):
                    a = (g * HG + h) * HD
                    last = mm(PM[:, 2, h * HD:h * HD + HD], dec[:, h, :], xdt[:, a:a + HD], start=True, stop=True)
                last.then_inc(S("scan_diag"), 1)
                if t < TT - 1:
                    pe.wait_ge(S("xdte_made"), t + 1)
                    if t:
                        pe.wait_ge(S("off_read"), n - 1)
                    elif g:
                        pe.wait_ge(S("hst_made"), 1)
                    mm(PM[:, 3, :], b_tm[:, t, g * P:g * P + P], xdte[:, g * 512:g * 512 + 512],
                       start=True, stop=True).then_inc(S("scan_st"), 1)
        pe.wait_ge(S("y_ssm_made"), TT)
        transposes("y_ssm", 8, lambda t, k: yt[:, t, k * P:k * P + P])
        transposed("y_ssm", 8)
        chunks("wout_s", 2, False)

        pe.wait_ge(S("mix0_made"), TT)
        transposes("mix0", 8, lambda t, k: xn[:, t, k * P:k * P + P])
        transposed("mix0", 8)
        chunks("qi", 2, False)
        u0 = PH["kiw"][0]
        unit_wait(u0)
        for t in range(TT):
            bank_wait("kiw", t, 0)
            full(tm(PD[t][:, 0:80], 80, (hhi, hlo), 0, u0 % 2, 8, 80, 0, True, True, t), t)
        pe.wait_ge(S("qi_roped"), 1)
        transposes("qi", 8, lambda t, k: qi_tm[:, t, k * P:k * P + P])
        transposes("ki", 1, lambda t, k: kiw[:, t, 0:P])
        transposed("ki", 1)
        for h in range(H1):
            p0 = HD * (h % 2)
            for t in range(1, TT):
                if h:
                    pe.wait_ge(S("idx_relu"), 3 * (h - 1) + t)
                mm(PM[:, t - 1, 0:(t + 1) * P], qit[p0:p0 + HD, h // 2, t * P:t * P + P],
                   kit[p0:p0 + HD, 0:(t + 1) * P], start=True, stop=True).then_inc(S("idx_dots"), 1)
        chunks("qk2", 2, False)
        two_units("v2", 0, 0, 0, 2, False)
        chunks("gates", 3, True)
        pe.wait_ge(S("qk_roped"), 1)
        transposes("qk", 8, lambda t, k: qk_tm[:, t, k * P:k * P + P])
        transposed("qk", 8)

        def logits(base, h, q, k, bias, need):
            s = h % 2
            X = PX[s]
            for t in (3, 2, 0, 1):
                b, c0 = QB_AT[t]
                w = (t + 1) * P
                mm(X[:, b, c0:c0 + w], q(t), k(w), start=t != 0, stop=False, skip_group_check=True)
                bw = bias(t)
                last = mm(X[:, b, c0 + w - bw.shape[1]:c0 + w], identr[:, :], bw, start=False, stop=t != 2,
                          skip_group_check=True)
                if t != 2:
                    last.then_inc(S("att_logits"), 1)

        def probs_out(base, h, p, pt, v):
            s = h % 2
            X = PX[s]
            n = base + h
            pe.wait_ge(S("att_exps"), 4 * n + 4)
            at_block = 0
            for t in (3, 2, 0, 1):
                for j in range(t + 1):
                    last = nc.tensor.transpose(X[:, at_block // 4, (at_block % 4) * P:(at_block % 4) * P + P],
                                               p[s][:, QB_FIRST[t] + j * P:QB_FIRST[t] + j * P + P], ident[:, :])
                    at_block += 1
            last.then_inc(S("att_turned"), 1)

        def values(base, h, pt, v):
            s = h % 2
            n = base + h
            pe.wait_ge(S("att_pt"), 2 * n + 2)
            if n >= 2:
                pe.wait_ge(S("att_out"), n - 1)
            for t in range(TT):
                for j in range(t + 1):
                    a = QB_FIRST[t] + j * P
                    last = mm(PX[s][:, 3, t * HD:t * HD + HD], pt[s][:, a:a + P], v(j, h), start=j == 0, stop=j == t)
            last.then_inc(S("att_pv"), 1)

        def sparse_logits(h):
            if h >= 2:
                pe.wait_ge(S("att_pt"), 2 * (h - 1))
            p0, f = HD * (h % 2), h // 2
            logits(0, h, lambda t: qkt[p0:p0 + HD, f, t * P:t * P + P], lambda w: qkt[p0:p0 + HD, 4 + f, 0:w],
                   lambda t: bias_q[:, t, 0:(t + 1) * P] if t else mask_q[:, :], None)

        pe.wait_ge(S("bias_made"), 3)
        phase_done(pe, "gates")
        for h in range(A_H + 1):
            if h < A_H:
                sparse_logits(h)
            if h:
                probs_out(0, h - 1, pr, prt, None)
                values(0, h - 1, prt, lambda j, hh: v2[:, j, hh * HD:hh * HD + HD])
        pe.wait_ge(S("att_out"), A_H)
        transposes("attn", 4, lambda t, k: v2[:, t, k * P:k * P + P])
        transposed("attn", 4)
        pe.wait_ge(S("conv2_done"), 4)
        chunks("wo2", 2, False)
        pe.wait_ge(S("ffn0_made"), TT)
        transposes("ffn0", 8, lambda t, k: xn[:, t, k * P:k * P + P])
        transposed("ffn0", 8)
        mlp("mlp0", 0)

        pe.wait_ge(S("mix1_made"), TT)
        transposes("mix1", 8, lambda t, k: xn[:, t, k * P:k * P + P])
        transposed("mix1", 8)
        two_units("dq", 0, 0, 0, 2, False, Q_RANK)
        two_units("dkv", 0, 0, 0, 2, False, KV_RANK + 32)
        pe.wait_ge(S("cq_made"), TT)
        transposes("cq", 3, lambda t, k: cq[:, t, k * P:k * P + P])
        pe.wait_ge(S("ckv_made"), TT)
        transposes("ckv", 2, lambda t, k: kva[:, t, k * P:k * P + P])
        transposed("ckv", 2)
        u0 = PH["uq"][0]
        for n in range(3):
            unit_wait(u0 + n)
            for t in range(TT):
                bank_wait("uq", t, n)
                full(tm(PD[t], 512, (hhi, hlo), 0, (u0 + n) % 2, 3, 512, 0, True, True, t), t)
        u0 = PH["ukv"][0]
        for n in range(2):
            unit_wait(u0 + n)
            for r in range(2):
                for t in range(TT):
                    bank_wait("ukv", t, 2 * n + r)
                    last = tm(PD[t], 512, (hhi, hlo), 3, (u0 + n) % 2, 2, 1024, 512 * r, True, True, t)
                    if t == 3 and r == 0:
                        last.then_inc(S("bank_full3"), 1)
                    else:
                        full(last, t)
        pe.wait_ge(S("mla_roped"), 1)
        phase_done(pe, "ukv")

        def latent_logits(h):
            s = h % 2
            if h >= 2:
                pe.wait_ge(S("att_pt"), 2 * (A_H + h - 1))
            for m, src in enumerate((lambda t: q_tm[:, t, h * C_QK:h * C_QK + C_QK], lambda t: k_tm[:, t, h, :])):
                for t in range(TT):
                    last = nc.tensor.transpose(PX[s][0:C_QK, m, t * P:t * P + P], src(t), ident[:, :])
                last.then_inc(S("tr_done"), 1)
            pe.wait_ge(S("tr_read"), TR["heads"][0] + 2 * h + 2)
            logits(A_H, h, lambda t: qth[s][0:C_QK, t * P:t * P + P], lambda w: kth[s][0:C_QK, 0:w],
                   lambda t: mask_q[:, :], None)

        for h in range(C_H + 1):
            if h < C_H:
                latent_logits(h)
            if h:
                probs_out(A_H, h - 1, pr3, prt3, None)
                values(A_H, h - 1, prt3, lambda j, hh: v3[:, j, hh * HD:hh * HD + HD])
        pe.wait_ge(S("att_out"), A_H + C_H)
        transposes("lat", 8, lambda t, k: v3[:, t, k * P:k * P + P])
        transposed("lat", 8)
        chunks("wo3", 2, False)
        pe.wait_ge(S("ffn1_made"), TT)
        transposes("ffn1", 8, lambda t, k: xn[:, t, k * P:k * P + P])
        transposed("ffn1", 8)
        mlp("mlp1", 1)

    @block.scalar
    def _(act):
        def hi(i, base, stride):
            if isinstance(i, int) and i * stride + base >= PH["end"][0]:
                return
            act.wait_ge(S(f"w_loaded{base % 2}"), i * (8 * stride) + 16 * (base // 2 + 1))
            if base >= 2:
                act.wait_ge(S("w_used"), i * stride + (base - 1))
            nc.scalar.activation(whi[base % 2][:, :], wraw[base % 2][:, :], ACT.Copy).then_inc(S("w_hi"), 1)

        def rounds(name, n, dst=None, func=ACT.Copy, scale=1.0, unrolled=False):
            u0 = PH[name][0]

            def body(i):
                hi(i, u0 + 1, 2)
                hi(i, u0 + 2, 2)
                for b in range(4):
                    if dst is not None:
                        full_wait(act, name, b, i, i * 2 + (u0 + 1))
                        nc.scalar.activation(dst(i, b), PD[b], func, scale=scale).then_inc(S(f"bank_free{b}"), 1)
            if unrolled:
                for i in range(n):
                    body(i)
            else:
                loop(act, n, body)

        def split_tiles(name, nk, gain, k0, after):
            act.wait_ge(S("w_used"), PH[after][0])
            for k in range(nk):
                act.wait_ge(S("tr_done"), TR[name][0] + k + 1)
                nc.scalar.activation(hhi[:, k0 + k, :], PM[:, k % 4, :], ACT.Copy, scale=gain(k))\
                    .then_inc(S("tr_hi"), 1)

        def copy_tiles(name, nk, dst):
            for k in range(nk):
                act.wait_ge(S("tr_done"), TR[name][0] + k + 1)
                nc.scalar.activation(dst(k), PM[:, k % 4, :], ACT.Copy).then_inc(S("tr_read"), 1)

        def squares(s, src, sem, need, d=DM):
            for t in range(TT):
                if sem is not None:
                    act.wait_ge(S(sem), need(t))
                if t or s:
                    act.wait_ge(S("squares"), TT * s + t - 1)
                nc.scalar.activation(junk[:, t % 2, 0:d], src(t), ACT.Square, accum_out=stat[:, s, t:t + 1])\
                    .then_inc(S("squares"), 1)

        def mlp(name, layer):
            u0 = PH[name][0]

            def up(first, r, i, m):
                hi(i, u0 + first + 1, 8)
                hi(i, u0 + first + 2, 8)
                base = m * 4 + 32 * layer

                def relu(b):
                    full_wait(act, name, b, r, i * 8 + (u0 + first + 1))
                    if b >= 2:
                        act.wait_ge(S("hidden_ready"), base + (b - 1))
                    nc.scalar.activation(mh_r[:, b % 2, :], PD[b], ACT.Relu).then_inc(S(f"bank_free{b}"), 1)

                def part(b):
                    act.wait_ge(S("hidden_sq"), base + (b + 1))
                    nc.scalar.activation(mh_hi[MPAR[first]][:, b, :], mh_r[:, b % 2, :], ACT.Copy)\
                        .then_inc(S("hidden_hi"), 1)
                if not (isinstance(m, int) and m == 0):
                    act.wait_ge(S("hidden_ready"), base)
                relu(0)
                relu(1)
                part(0)
                relu(2)
                part(1)
                relu(3)
                part(2)
                part(3)

            def down(first, i):
                hi(i, u0 + first + 1, 8)
                hi(i, u0 + first + 2, 8)

            MPAR = {0: 0, 2: 1, 6: 0}
            up(0, 0, 0, 0)
            with act.Fori(0, 3) as i:
                up(2, i * 6 + 1, i, i * 2 + 1)
                down(4, i)
                up(6, i * 6 + 4, i, i * 2 + 2)
                down(8, i)
            up(2, 19, 3, 7)
            down(4, 3)
            down(6, 3)

        hi(0, 0, 0)
        act.wait_ge(S("tr_done"), 1)
        nc.scalar.activation(cact[:, :], PM[:, 3, 0:8], ACT.Silu).then_inc(S("tr_read"), 1)
        act.wait_ge(S("tr_read"), 1)
        nc.scalar.activation(chi[:, :, :], cact[:, :].unsqueeze(2).to_broadcast([P, KT, P]), ACT.Copy)\
            .then_inc(S("c_hi"), 1)
        act.wait_ge(S("x_loaded"), 16)
        squares(0, lambda t: xres[:, t, :], None, None)
        for u in range(1, 9):
            hi(0, u, 0)
        act.wait_ge(S("angles"), 1)
        nc.scalar.activation(sinall[:, :, :], ang[:, :, :], ACT.Sin).then_inc(S("sines"), 1)
        nc.scalar.activation(ang_s[:, :, :], ang[:, :, :], ACT.Sin, scale=0.5).then_inc(S("sines"), 1)
        split_tiles("h", 8, lambda k: 1.0, 0, "ada_ss")
        rounds("q", 2, lambda i, b: dyn(qt, i, b), scale=HD ** -0.5)
        rounds("k", 2, lambda i, b: dyn(kt, i, b))
        rounds("v", 2, lambda i, b: vo[:, b, bass.ds(i * 512, 512)])

        def sb_head(h):
            for n in range(3):
                a = slice(SB_FIRST[n], SB_FIRST[n] + SB_WIDE[n])
                act.wait_ge(S("sb_clamped"), 3 * h + n + 1)
                nc.scalar.activation(sb_l[:, a], sb_l[:, a], ACT.Exp).then_inc(S("sb_exp"), 1)
                act.wait_ge(S("sb_exp"), 3 * h + n + 1)
                nc.scalar.activation(sb_l[:, a], sb_l[:, a], ACT.Ln, bias=1.0).then_inc(S("sb_ln"), 1)
            if h:
                act.wait_ge(S("sb_tail"), 3 * h)
            for n in range(3):
                a = slice(SB_FIRST[n], SB_FIRST[n] + SB_WIDE[n])
                act.wait_ge(S("sb_softplus"), 3 * h + n + 1)
                nc.scalar.activation(sb_hi[:, a], sb_l[:, a], ACT.Copy).then_inc(S("sb_high"), 1)
            if h:
                act.wait_ge(S("sb_pv"), h)
            for n in range(3):
                a = slice(SB_FIRST[n], SB_FIRST[n] + SB_WIDE[n])
                act.wait_ge(S("sb_tail"), 3 * h + n + 1)
                nc.scalar.activation(sb_w[:, a], PM[:, n, 0:SB_WIDE[n]], ACT.Exp).then_inc(S("sb_weights"), 1)

        nc.scalar.preload_act_table_set("natural_log_exp_and_others")
        for h in range(H1):
            sb_head(h)
        act.wait_ge(S("sb_tail"), 3 * H1)
        nc.scalar.activation(chi2[:, :, :], cact[:, :].unsqueeze(2).to_broadcast([P, KT, P]), ACT.Copy)\
            .then_inc(S("c_hi"), 1)
        rounds("xbc", 3, lambda i, b: xbc[:, bass.ds(i * 4 + b, 1), 3:SEQ + 3])
        hi(0, PH["dt"][0] + 1, 0)
        rounds("z_ssm", 2, lambda i, b: zs[:, b, bass.ds(i * 512, 512)])
        rounds("z_attn", 2, lambda i, b: za[:, b, bass.ds(i * 512, 512)])
        act.wait_ge(S("dt_clamped"), 1)
        nc.scalar.activation(dts[:, 0, :], dts[:, 0, :], ACT.Exp).then_inc(S("dt_exp"), 1)
        nc.scalar.activation(small[:, 16:32], small[:, 16:32], ACT.Exp).then_inc(S("dt_exp"), 1)
        act.wait_ge(S("dt_exp"), 2)
        nc.scalar.activation(dts[:, 0, :], dts[:, 0, :], ACT.Ln, bias=1.0).then_inc(S("dt_ln"), 1)
        for u in range(1, 5):
            hi(0, PH["ada_g"][0] + u, 0)
        for ct in range(XBC_T):
            act.wait_ge(S("conv_sum"), ct + 1)
            nc.scalar.activation(xbc[:, ct, 0:SEQ], conv_acc[:, ct % 2, :], ACT.Silu).then_inc(S("conv_done"), 1)
        phase_done(act, "z_attn")
        for t in range(TT):
            nc.scalar.activation(za[:, t, :], za[:, t, :], ACT.Silu).then_inc(S("za_silu"), 1)
        squares(1, lambda t: vo[:, t, :], "sb_out", lambda t: H1)
        split_tiles("y_attn", 8, lambda k: col_a[:, C_SBG + k:C_SBG + k + 1], 0, "wout_a")
        rounds("wout_a", 2, lambda i, b: mix[:, b, bass.ds(i * 512, 512)])
        phase_done(act, "z_ssm")
        for t in range(TT):
            nc.scalar.activation(zs[:, t, :], zs[:, t, :], ACT.Silu).then_inc(S("zs_silu"), 1)
        copy_tiles("scan", 10, lambda k: yt[:, :, k * P:k * P + P] if k < 8 else b_tm[:, :, (k - 8) * P:(k - 7) * P])
        act.wait_ge(S("scan_cum"), 1)
        nc.scalar.activation(dts[:, 2:5, :], PM[:, 3, 0:192].rearrange("p (a b) -> p a b", a=3), ACT.Exp)\
            .then_inc(S("scan_exps"), 1)
        for n in range(2 * TT):
            act.wait_ge(S("scan_seg"), n + 1)
            if n:
                act.wait_ge(S("scan_diag"), n)
            nc.scalar.activation(dec[:, :, :].rearrange("p h l -> p (h l)"), PM[:, 0:2, :].rearrange("p a b -> p (a b)"),
                                 ACT.Exp).then_inc(S("scan_dec"), 1)
        squares(2, lambda t: yt[:, t, :], "y_gated", lambda t: t + 1)
        split_tiles("y_ssm", 8, lambda k: col_a[:, C_SSG + k:C_SSG + k + 1], 0, "wout_s")
        rounds("wout_s", 2)
        squares(3, lambda t: xres[:, t, :], "x2_made", lambda t: t + 1)
        squares(4, lambda t: xres[:, t, :], "first_out", lambda t: t + 1)
        split_tiles("mix0", 8, lambda k: col_a[:, C_MIX + k:C_MIX + k + 1], 0, "qi")
        rounds("qi", 2, lambda i, b: qi_tm[:, b, bass.ds(i * 512, 512)])
        hi(0, PH["kiw"][0] + 1, 0)
        copy_tiles("qi", 8, lambda k: qit[:, k, :])
        copy_tiles("ki", 1, lambda k: kit[:, :])
        for h in range(H1):
            if h >= 2:
                act.wait_ge(S("idx_sum"), 3 * (h - 1))
            for t in range(1, TT):
                act.wait_ge(S("idx_dots"), 3 * h + t)
                nc.scalar.activation(relu_s[:, h % 2, IDX_AT[t]:IDX_AT[t] + (t + 1) * P], PM[:, t - 1, 0:(t + 1) * P],
                                     ACT.Relu).then_inc(S("idx_relu"), 1)
        rounds("qk2", 2, lambda i, b: qk_tm[:, b, bass.ds(i * 512, 512)])
        rounds("v2", 1, lambda i, b: v2[:, b, :])
        act.wait_ge(S("idx_sum"), 3 * H1)
        rounds("gates", 3, lambda i, b: [gb[:, b, :], gc[:, b, 2:SEQ + 2], xi[:, b, :]][i], unrolled=True)
        copy_tiles("qk", 8, lambda k: qkt[:, k, :])
        act.wait_ge(S("w_used"), PH["wo2"][0])
        for f in range(4):
            act.wait_ge(S("conv2_out"), f + 1)
            nc.scalar.activation(hhi[:, 4 + f, :], ca[:, f, :], ACT.Copy).then_inc(S("conv2_hi"), 1)

        def exps(base, h, p, m, d, scale):
            n, s = base + h, h % 2
            act.wait_ge(S("att_max"), n + 1)
            if h >= 2:
                act.wait_ge(S("att_turned"), n - 1)
                act.wait_ge(S("att_out"), n - 1)
            for t in (3, 2, 0, 1):
                b, c0 = QB_AT[t]
                w = (t + 1) * P
                nc.scalar.activation(p[s][:, QB_FIRST[t]:QB_FIRST[t] + w], PX[s][:, b, c0:c0 + w], ACT.Exp,
                                     bias=m[:, s, t:t + 1], scale=scale, accum_out=d[:, s, t:t + 1])\
                    .then_inc(S("att_exps"), 1)

        def turned(base, h, pt):
            n, s = base + h, h % 2
            act.wait_ge(S("att_turned"), n + 1)
            if h >= 2:
                act.wait_ge(S("att_pv"), n - 1)
            nc.scalar.activation(pt[s][:, 0:SEQ], PX[s][:, 0, :], ACT.Copy)\
                .then_inc(S("att_pt"), 1)

        for h in range(A_H + 1):
            if h < A_H:
                exps(0, h, pr, mx, den, HD ** -0.5)
            if h:
                turned(0, h - 1, prt)
        split_tiles("attn", 4, lambda k: 1.0, 0, "wo2")
        rounds("wo2", 2, lambda i, b: mix2[:, b, bass.ds(i * 512, 512)])
        phase_done(act, "wo2")
        squares(5, lambda t: mix2[:, t, :], None, None)
        squares(6, lambda t: xres[:, t, :], "post_mix0", lambda t: t + 1)
        split_tiles("ffn0", 8, lambda k: col_a[:, C_FFN + k:C_FFN + k + 1], 0, "mlp0")
        mlp("mlp0", 0)
        phase_done(act, "mlp0")
        squares(7, lambda t: mixm[:, t, :], None, None)
        squares(8, lambda t: xres[:, t, :], "post_ffn0", lambda t: t + 1)
        split_tiles("mix1", 8, lambda k: col_a[:, C_MIX + 8 + k:C_MIX + 9 + k], 0, "dq")
        for name, dst, n in (("dq", cq, Q_RANK), ("dkv", kva, KV_RANK + 32)):
            u0 = PH[name][0]
            hi(0, u0 + 1, 0)
            hi(0, u0 + 2, 0)
            for b in range(4):
                full_wait(act, name, b, 0, u0 + 1)
                nc.scalar.activation(dst[:, b, :], PD[b][:, 0:n], ACT.Copy).then_inc(S(f"bank_free{b}"), 1)
        phase_done(act, "dkv")
        squares(9, lambda t: cq[:, t, :], None, None, Q_RANK)
        squares(10, lambda t: kva[:, t, 0:KV_RANK], None, None, KV_RANK)
        split_tiles("cq", 3, lambda k: col_b[:, C_QN + k:C_QN + k + 1], 0, "uq")
        split_tiles("ckv", 2, lambda k: col_b[:, C_KN + k:C_KN + k + 1], 3, "uq")
        u0 = PH["uq"][0]
        for n in range(3):
            hi(0, u0 + n + 1, 0)
            for t in range(TT):
                full_wait(act, "uq", t, n, u0 + n)
                nc.scalar.activation(q_tm[:, t, 512 * n:512 * n + 512], PD[t], ACT.Copy)\
                    .then_inc(S(f"bank_free{t}"), 1)
        u0 = PH["ukv"][0]
        hi(0, u0 + 1, 0)
        hi(0, u0 + 2, 0)

        def turn_q(h):
            s = h % 2
            act.wait_ge(S("tr_done"), TR["heads"][0] + 2 * h + 1)
            nc.scalar.activation(qth[s][0:C_QK, :], PX[s][0:C_QK, 0, :], ACT.Copy).then_inc(S("tr_read"), 1)

        for h in range(C_H + 1):
            if h < C_H:
                turn_q(h)
                exps(A_H, h, pr3, mx3, den3, C_QK ** -0.5)
            if h:
                turned(A_H, h - 1, prt3)
        split_tiles("lat", 8, lambda k: 1.0, 0, "wo3")
        rounds("wo3", 2, lambda i, b: mix3[:, b, bass.ds(i * 512, 512)])
        phase_done(act, "wo3")
        squares(11, lambda t: mix3[:, t, :], None, None)
        squares(12, lambda t: xres[:, t, :], "post_mix1", lambda t: t + 1)
        split_tiles("ffn1", 8, lambda k: col_a[:, C_FFN + 8 + k:C_FFN + 9 + k], 0, "mlp1")
        mlp("mlp1", 1)
        phase_done(act, "mlp1")
        squares(13, lambda t: mixm[:, t, :], None, None)

    @block.gpsimd
    def _(pool):
        g = nc.gpsimd

        def lo(i, base, stride):
            if base >= PH["end"][0]:
                return
            pool.wait_ge(S("w_hi"), i * stride + (base + 1))
            g.tensor_tensor(wlo[base % 2][:, :], wraw[base % 2][:, :], fl(whi[base % 2][:, :]), ALU.subtract)\
                .then_inc(S("w_split"), 1)

        def units(name, to):
            for u in range(PH[name][0] + 1, PH[to][0] + 1):
                lo(0, u, 0)

        def pairs(name, n):
            u0 = PH[name][0]

            def body(i):
                lo(i, u0 + 1, 2)
                lo(i, u0 + 2, 2)
            loop(pool, n, body)

        def rsqrt(s, n=1):
            for m in range(s, s + n):
                pool.wait_ge(S("mean_sq"), m + 1)
                g.tensor_tensor(rstd[:, m, :], stat[:, m, :], mhalf[:, :], ALU.pow).then_inc(S("rstd_done"), 1)

        g.memset(ident[:, :], 0.0).then_inc(S("filled"), 1)
        g.memset(ones[:, :], 1.0).then_inc(S("filled"), 1)
        g.memset(scratch[:, :], 0.0).then_inc(S("filled"), 1)
        g.memset(scratch1[:, :], -1.0).then_inc(S("filled"), 1)
        g.memset(mhalf[:, :], -0.5).then_inc(S("filled"), 1)
        pool.wait_ge(S("filled"), 5)
        g.affine_select(out=ident[:, :], in_=ident[:, :], compare_op=ALU.not_equal, fill=1.0, base=0,
                        pattern=[[-1, P]], channel_multiplier=1).then_inc(S("masks"), 1)
        lo(0, 0, 0)
        g.affine_select(out=identr[:, :], in_=scratch[:, :], compare_op=ALU.not_equal, fill=1.0, base=0,
                        pattern=[[-1, P]], channel_multiplier=1)
        g.affine_select(out=tri_le[:, :], in_=ones[:, :], compare_op=ALU.is_ge, fill=0.0, base=0,
                        pattern=[[1, P]], channel_multiplier=-1)
        g.affine_select(out=tri_gt[:, :], in_=ones[:, :], compare_op=ALU.is_gt, fill=0.0, base=0,
                        pattern=[[-1, P]], channel_multiplier=1)
        g.affine_select(out=neg_ge[:, :], in_=scratch1[:, :], compare_op=ALU.is_ge, fill=0.0, base=0,
                        pattern=[[-1, P]], channel_multiplier=1)
        g.affine_select(out=mask_t[:, :], in_=scratch[:, :], compare_op=ALU.is_gt, fill=NEG, base=0,
                        pattern=[[1, P]], channel_multiplier=-1)
        g.affine_select(out=mask_q[:, :], in_=scratch[:, :], compare_op=ALU.is_ge, fill=NEG, base=0,
                        pattern=[[-1, P]], channel_multiplier=1)
        g.tensor_copy(neg_one[:, :], scratch1[:, :]).then_inc(S("masks"), 1)
        for j in range(8):
            g.memset(freq[:, j:j + 1], THETA ** (-2.0 * j / 16))
        for j in range(16):
            g.memset(freq[:, 8 + j:9 + j], THETA ** (-2.0 * j / 32)).then_inc(S("freqs"), 1)
        lo(0, 1, 0)
        lo(0, 2, 0)
        rsqrt(0)
        for u in range(3, 9):
            lo(0, u, 0)
        pairs("q", 2)
        pairs("k", 2)
        pairs("v", 2)
        g.memset(xbc[:, :, 0:3], 0.0).then_inc(S("pads"), 1)
        pairs("xbc", 3)
        lo(0, PH["dt"][0] + 1, 0)
        pairs("z_ssm", 2)
        pairs("z_attn", 2)
        units("ada_g", "wout_a")
        rsqrt(1)
        pairs("wout_a", 2)
        rsqrt(2)
        pairs("wout_s", 2)
        rsqrt(3, 2)
        pairs("qi", 2)
        lo(0, PH["kiw"][0] + 1, 0)
        for t in range(1, TT):
            pool.wait_ge(S("idx_sum"), 3 * H1)
            g.affine_select(out=score[:, t, t * P:t * P + P], in_=score[:, t, t * P:t * P + P], compare_op=ALU.is_ge,
                            fill=DROPPED, base=0, pattern=[[-1, P]], channel_multiplier=1)\
                .then_inc(S("score_masked"), 1)
        pairs("qk2", 2)
        pairs("v2", 1)
        g.memset(gc[:, :, 0:2], 0.0).then_inc(S("pads"), 1)
        pairs("gates", 3)
        pairs("wo2", 2)
        rsqrt(5, 2)

        def mlp(name, layer):
            u0 = PH[name][0]
            pool.wait_ge(S(f"post_mix{layer}"), TT)
            g.memset(mixm[:, :, :], 0.0).then_inc(S("acc_zero"), 1)
            for u in (1, 2):
                lo(0, u0 + u, 0)
            with pool.Fori(0, 3) as i:
                for u in range(3, 11):
                    lo(i, u0 + u, 8)
            for u in range(27, 33):
                lo(0, u0 + u, 0)

        mlp("mlp0", 0)
        rsqrt(7, 2)
        units("dq", "uq")
        rsqrt(9, 2)
        units("uq", "wo3")
        pairs("wo3", 2)
        rsqrt(11, 2)
        mlp("mlp1", 1)
        rsqrt(13)

    @block.vector
    def _(dve):
        v = nc.vector
        chained = [0]

        def link(ins):
            chained[0] += 1
            ins.then_inc(S("dve_chain"), 1)
            dve.wait_ge(S("dve_chain"), chained[0])

        def split_tiles(name, nk, gain, k0):
            for k in range(nk):
                dve.wait_ge(S("tr_hi"), TR[name][1] + k + 1)
                v.scalar_tensor_tensor(out=hlo[:, k0 + k, :], in0=PM[:, k % 4, :], scalar=gain(k),
                                       in1=fl(hhi[:, k0 + k, :]), op0=ALU.mult, op1=ALU.subtract)\
                    .then_inc(S("tr_read"), 1)

        def mean_square(s, d=DM):
            dve.wait_ge(S("squares"), TT * (s + 1))
            v.tensor_scalar(stat[:, s, :], stat[:, s, :], 1.0 / d, EPS, ALU.mult, ALU.add).then_inc(S("mean_sq"), 1)
            dve.wait_ge(S("rstd_done"), s + 1)

        def rope(view, heads, half, c, s, tmp):
            n = TT * heads * half
            shape = [P, TT, heads, half]
            cb = c[:, :, :].unsqueeze(2).to_broadcast(shape)
            sb = s[:, :, :].unsqueeze(2).to_broadcast(shape)
            x1, x2 = view[:, :, :, 0:half], view[:, :, :, half:2 * half]
            t = [tmp[:, j, 0:n].rearrange("p (a h d) -> p a h d", a=TT, h=heads) for j in range(4)]
            v.tensor_tensor(t[0], x1, cb, ALU.mult)
            v.tensor_tensor(t[1], x2, sb, ALU.mult)
            v.tensor_tensor(t[2], x2, cb, ALU.mult)
            link(v.tensor_tensor(t[3], x1, sb, ALU.mult))
            v.tensor_tensor(x1, t[0], t[1], ALU.subtract)
            link(v.tensor_tensor(x2, t[2], t[3], ALU.add))

        dve.wait_ge(S("c_hi"), 1)
        v.tensor_tensor(clo[:, :, :], cact[:, :].unsqueeze(2).to_broadcast([P, KT, P]), fl(chi[:, :, :]),
                        ALU.subtract).then_inc(S("c_split"), 1)
        dve.wait_ge(S("tr_done"), 2)
        v.tensor_copy(col_a[:, 0:ROWS_A], PM[:, 2, 0:ROWS_A])
        v.tensor_copy(col_b[:, 0:ROWS_B], PM[:, 2, P:P + ROWS_B]).then_inc(S("tr_read"), 1)
        dve.wait_ge(S("params"), 16 * N_PARAMS)
        dve.wait_ge(S("freqs"), 16)
        link(v.tensor_copy(pos_f[:, :], pos_i[:, :]))
        link(v.tensor_tensor(ang[:, :, :], pos_f[:, :].unsqueeze(2).to_broadcast([P, TT, 24]),
                             freq[:, :].unsqueeze(1).to_broadcast([P, TT, 24]), ALU.mult))
        link(v.tensor_scalar(ang_n[:, :, :], ang[:, :, :], 1.0 / (2 * math.pi), ROUNDER, ALU.mult, ALU.add))
        link(v.tensor_scalar(ang_n[:, :, :], ang_n[:, :, :], -ROUNDER, None, ALU.add))
        for part in TWO_PI:
            link(v.scalar_tensor_tensor(out=ang[:, :, :], in0=ang_n[:, :, :], scalar=-part, in1=ang[:, :, :],
                                        op0=ALU.mult, op1=ALU.add))
        v.tensor_scalar(ang[:, :, :], ang[:, :, :], PI_BELOW, -PI_BELOW, ALU.min, ALU.max).then_inc(S("angles"), 1)
        mean_square(0)
        for j, c0 in enumerate((DM, DM + 512, 0, 512)):
            full_unit = PH["ada_ss"][0] + 2 * j + 2
            dve.wait_ge(S("w_used"), full_unit)
            v.tensor_tensor(mod[:, c0:c0 + 512], PD[j], b_row[:, c0:c0 + 512], ALU.add).then_inc(S(f"bank_free{j}"), 1)
            if j < 2:
                dve.wait_ge(S(f"bank_free{j}"), 1)
                v.scalar_tensor_tensor(out=mod[:, c0:c0 + 512], in0=mod[:, c0:c0 + 512], scalar=1.0,
                                       in1=row_a[:, c0 - DM:c0 - DM + 512], op0=ALU.add, op1=ALU.mult)
        dve.wait_ge(S("sines"), 2)
        link(v.tensor_tensor(ang_s[:, :, :], ang_s[:, :, :], ang_s[:, :, :], ALU.mult))
        v.tensor_scalar(cosq[:, :, :], ang_s[:, :, 0:8], -2.0, 1.0, ALU.mult, ALU.add)
        v.tensor_scalar(cosm[:, :, :], ang_s[:, :, 8:24], -2.0, 1.0, ALU.mult, ALU.add)
        v.tensor_copy(sinq[:, :, :], sinall[:, :, 0:8])
        link(v.tensor_copy(sinm[:, :, :], sinall[:, :, 8:24]))
        for t in range(TT):
            v.scalar_tensor_tensor(out=xn[:, t, :], in0=xres[:, t, :], scalar=rstd[:, 0, t:t + 1],
                                   in1=mod[:, DM:2 * DM], op0=ALU.mult, op1=ALU.mult).then_inc(S("h_scaled"), 1)
        for t in range(TT):
            dve.wait_ge(S("h_scaled"), t + 1)
            v.tensor_tensor(xn[:, t, :], xn[:, t, :], mod[:, 0:DM], ALU.add).then_inc(S("h_made"), 1)
        split_tiles("h", 8, lambda k: 1.0, 0)

        def sb_emit(h):
            dve.wait_ge(S("sb_pv"), h + 1)
            v.tensor_copy(vo[:, :, h * HD:h * HD + HD],
                          PM[:, 3, (h % 2) * 256:(h % 2) * 256 + 256].rearrange("p (t d) -> p t d", t=TT))\
                .then_inc(S("sb_out"), 1)

        for h in range(H1):
            for n in range(3):
                a = slice(SB_FIRST[n], SB_FIRST[n] + SB_WIDE[n])
                dve.wait_ge(S("sb_z"), 3 * h + n + 1)
                if h:
                    dve.wait_ge(S("sb_split"), 3 * (h - 1) + n + 1)
                v.tensor_scalar(sb_l[:, a], PM[:, n, 0:SB_WIDE[n]], CLAMP, None, ALU.min).then_inc(S("sb_clamped"), 1)
            if h:
                sb_emit(h - 1)
            for n in range(3):
                a = slice(SB_FIRST[n], SB_FIRST[n] + SB_WIDE[n])
                dve.wait_ge(S("sb_ln"), 3 * h + n + 1)
                v.tensor_tensor(sb_l[:, a], PM[:, n, 0:SB_WIDE[n]], sb_l[:, a], ALU.max).then_inc(S("sb_softplus"), 1)
            for n in range(3):
                a = slice(SB_FIRST[n], SB_FIRST[n] + SB_WIDE[n])
                dve.wait_ge(S("sb_high"), 3 * h + n + 1)
                v.tensor_tensor(sb_lo[:, a], sb_l[:, a], fl(sb_hi[:, a]), ALU.subtract).then_inc(S("sb_split"), 1)
        sb_emit(H1 - 1)
        dve.wait_ge(S("c_hi"), 2)
        v.tensor_tensor(clo2[:, :, :], cact[:, :].unsqueeze(2).to_broadcast([P, KT, P]), fl(chi2[:, :, :]),
                        ALU.subtract).then_inc(S("c_split"), 1)

        u0 = PH["dt"][0]
        dve.wait_ge(S("w_used"), u0 + 1)
        rows4 = [P, TT, H1]
        v.tensor_tensor(dts[:, 5, :].rearrange("p (t h) -> p t h", t=TT), PD[0][:, 0:64].rearrange("p (t h) -> p t h", t=TT),
                        small[:, 0:16].unsqueeze(1).to_broadcast(rows4), ALU.add).then_inc(S("bank_free0"), 1)
        dve.wait_ge(S("bank_free0"), PH["z_ssm"][1][0])
        v.tensor_scalar(dts[:, 0, :], dts[:, 5, :], CLAMP, None, ALU.min).then_inc(S("dt_clamped"), 1)
        phase_done(dve, "xbc")
        dve.wait_ge(S("pads"), 1)
        for ct in range(XBC_T):
            acc = conv_acc[:, ct % 2, :]
            if ct >= 2:
                dve.wait_ge(S("conv_done"), ct - 1)
            col = [col_a[:, C_CW + 12 * j + ct:C_CW + 12 * j + ct + 1] for j in range(4)]
            link(v.tensor_scalar(acc, xbc[:, ct, 0:SEQ], col[0], col_a[:, C_CB + ct:C_CB + ct + 1], ALU.mult, ALU.add))
            for j in range(1, 4):
                op = v.scalar_tensor_tensor(out=acc, in0=xbc[:, ct, j:j + SEQ], scalar=col[j], in1=acc,
                                            op0=ALU.mult, op1=ALU.add)
                if j < 3:
                    link(op)
                else:
                    op.then_inc(S("conv_sum"), 1)
        dve.wait_ge(S("dt_ln"), 1)
        link(v.tensor_tensor(dts[:, 0, :], dts[:, 5, :], dts[:, 0, :], ALU.max))
        v.scalar_tensor_tensor(out=dts[:, 1, :].rearrange("p (t h) -> p t h", t=TT),
                               in0=dts[:, 0, :].rearrange("p (t h) -> p t h", t=TT), scalar=-1.0,
                               in1=small[:, 16:32].unsqueeze(1).to_broadcast(rows4), op0=ALU.mult, op1=ALU.mult)\
            .then_inc(S("ld_made"), 1)
        for j in range(2):
            dve.wait_ge(S("w_used"), PH["ada_g"][0] + 2 * j + 2)
            v.tensor_tensor(gate[:, 512 * j:512 * j + 512], PD[j], row_b[:, 512 * j:512 * j + 512], ALU.add)\
                .then_inc(S(f"bank_free{j}"), 1)
        mean_square(1)
        dve.wait_ge(S("za_silu"), TT)
        for t in range(TT):
            v.scalar_tensor_tensor(out=xn_a[:, t, :], in0=vo[:, t, :], scalar=rstd[:, 1, t:t + 1], in1=za[:, t, :],
                                   op0=ALU.mult, op1=ALU.mult).then_inc(S("y_attn_made"), 1)
        split_tiles("y_attn", 8, lambda k: col_a[:, C_SBG + k:C_SBG + k + 1], 0)

        dve.wait_ge(S("scan_cb"), 1)
        for g in range(GROUPS):
            op = v.tensor_tensor(cbm[:, 4 * g:4 * g + 4, :], PM[:, g, :].rearrange("p (t l) -> p t l", t=TT),
                                 tri_le[:, :].unsqueeze(1).to_broadcast([P, TT, P]), ALU.mult)
        op.then_inc(S("cbm_made"), 1)
        dve.wait_ge(S("cbm_made"), 1)
        dve.wait_ge(S("scan_exps"), 1)
        dve.wait_ge(S("zs_silu"), TT)

        def per_head(row, t, g, n=HG):
            a = t * H1 + g * HG
            return dts[:, row, a:a + n].unsqueeze(2).to_broadcast([P, n, HD])

        def heads(ap):
            return ap.rearrange("p (h d) -> p h d", d=HD)

        for t in range(TT):
            if t:
                dve.wait_ge(S("scan_seg"), 2 * t)
            v.tensor_tensor(ldm[:, :, :], tri_gt[:, :].unsqueeze(1).to_broadcast([P, H1, P]),
                            dts[:, 1, t * H1:t * H1 + H1].unsqueeze(2).to_broadcast([P, H1, P]), ALU.mult)\
                .then_inc(S("ldm_made"), 1)
            if t:
                dve.wait_ge(S("scan_diag"), 2 * t)
                dve.wait_ge(S("xdte_made"), t)
            link(v.tensor_tensor(heads(xdt[:, :]), heads(yt[:, t, :]), per_head(0, t, 0, H1), ALU.mult))
            if t < TT - 1:
                if t:
                    dve.wait_ge(S("scan_st"), 2 * t)
                v.tensor_tensor(heads(xdte[:, :]), heads(xdt[:, :]), per_head(3, t, 0, H1), ALU.mult)\
                    .then_inc(S("xdte_made"), 1)
            for g in range(GROUPS):
                n = 2 * t + g
                cols = slice(g * 512, g * 512 + 512)
                dve.wait_ge(S("scan_dec"), n + 1)
                v.tensor_tensor(dec[:, :, :], dec[:, :, :],
                                cbm[:, 4 * g + t, :].unsqueeze(1).to_broadcast([P, HG, P]), ALU.mult)\
                    .then_inc(S("scan_m"), 1)
                if n:
                    dve.wait_ge(S("scan_y"), n)
                link(v.tensor_tensor(heads(xd[:, :]), heads(yt[:, t, cols]),
                                     small[:, 32 + g * HG:32 + g * HG + HG].unsqueeze(2).to_broadcast([P, HG, HD]),
                                     ALU.mult))
                if t:
                    dve.wait_ge(S("scan_off"), n - 1)
                    v.tensor_tensor(heads(off[:, :]), heads(PM[:, 3, :]), per_head(2, t, g), ALU.mult)\
                        .then_inc(S("off_read"), 1)
                    dve.wait_ge(S("off_read"), n - 1)
                    link(v.tensor_tensor(xd[:, :], xd[:, :], off[:, :], ALU.add))
                dve.wait_ge(S("scan_diag"), n + 1)
                v.tensor_tensor(yt[:, t, cols], PM[:, 2, :], xd[:, :], ALU.add).then_inc(S("scan_y"), 1)
                if t < TT - 1:
                    if t:
                        link(v.tensor_tensor(heads(hst[:, cols]), heads(hst[:, cols]), per_head(4, t, g), ALU.mult))
                    dve.wait_ge(S("scan_st"), n + 1)
                    if t:
                        v.tensor_tensor(hst[:, cols], hst[:, cols], PM[:, 3, :], ALU.add).then_inc(S("hst_made"), 1)
                    else:
                        v.tensor_copy(hst[:, cols], PM[:, 3, :]).then_inc(S("hst_made"), 1)
            dve.wait_ge(S("scan_y"), 2 * t + 2)
            v.tensor_tensor(yt[:, t, :], yt[:, t, :], zs[:, t, :], ALU.mult).then_inc(S("y_gated"), 1)
        mean_square(2)
        for t in range(TT):
            v.tensor_scalar(yt[:, t, :], yt[:, t, :], rstd[:, 2, t:t + 1], None, ALU.mult).then_inc(S("y_ssm_made"), 1)
        split_tiles("y_ssm", 8, lambda k: col_a[:, C_SSG + k:C_SSG + k + 1], 0)
        u0 = PH["wout_s"][0]

        def add_mix(i):
            for b in range(4):
                full_wait(dve, "wout_s", b, i, i * 2 + (u0 + 1))
                m = mix[:, b, bass.ds(i * 512, 512)]
                v.tensor_tensor(m, PD[b], m, ALU.add).then_inc(S(f"bank_free{b}"), 1)
        loop(dve, 2, add_mix)
        phase_done(dve, "wout_s")
        dve.wait_ge(S("x_again"), 16)
        for t in range(TT):
            link(v.tensor_tensor(mix[:, t, :], mix[:, t, :], gate[:, :], ALU.mult))
            v.tensor_tensor(xres[:, t, :], xres[:, t, :], mix[:, t, :], ALU.add).then_inc(S("x2_made"), 1)
        mean_square(3)
        dve.wait_ge(S("row_f"), 16)
        for t in range(TT):
            v.scalar_tensor_tensor(out=xres[:, t, :], in0=xres[:, t, :], scalar=rstd[:, 3, t:t + 1], in1=row_a[:, :],
                                   op0=ALU.mult, op1=ALU.mult).then_inc(S("first_out"), 1)

        def normed(s, sem):
            mean_square(s)
            for t in range(TT):
                v.tensor_scalar(xn[:, t, :], xres[:, t, :], rstd[:, s, t:t + 1], None, ALU.mult).then_inc(S(sem), 1)

        def post_norm(s, m, row, sem):
            mean_square(s)
            for t in range(TT):
                link(v.scalar_tensor_tensor(out=m[:, t, :], in0=m[:, t, :], scalar=rstd[:, s, t:t + 1], in1=row[:, :],
                                            op0=ALU.mult, op1=ALU.mult))
                v.tensor_tensor(xres[:, t, :], xres[:, t, :], m[:, t, :], ALU.add).then_inc(S(sem), 1)

        normed(4, "mix0_made")
        split_tiles("mix0", 8, lambda k: col_a[:, C_MIX + k:C_MIX + k + 1], 0)

        for t in range(TT):
            full_wait(dve, "kiw", t, 0, PH["kiw"][0])
            v.tensor_copy(kiw[:, t, 0:64], PD[t][:, 0:64])
            v.tensor_scalar(kiw[:, t, 128:144], PD[t][:, 64:80], H1 ** -0.5 * HD ** -0.5, None, ALU.mult)\
                .then_inc(S(f"bank_free{t}"), 1)
        phase_done(dve, "qi")
        phase_done(dve, "kiw")
        rope(qi_tm[:, :, :].rearrange("p t (h d) -> p t h d", d=HD), H1, 8, cosq, sinq, rt)
        rope(kiw[:, :, 0:64].rearrange("p t (h d) -> p t h d", d=HD), 1, 8, cosq, sinq, rt)
        v.tensor_copy(kiw[:, :, 64:128], kiw[:, :, 0:64]).then_inc(S("qi_roped"), 1)
        for h in range(H1):
            for t in range(1, TT):
                dve.wait_ge(S("idx_relu"), 3 * h + t)
                r = relu_s[:, h % 2, IDX_AT[t]:IDX_AT[t] + (t + 1) * P]
                sc = score[:, t, 0:(t + 1) * P]
                w = kiw[:, t, 128 + h:129 + h]
                if h:
                    dve.wait_ge(S("idx_sum"), 3 * (h - 1) + t)
                    v.scalar_tensor_tensor(out=sc, in0=r, scalar=w, in1=sc, op0=ALU.mult, op1=ALU.add)\
                        .then_inc(S("idx_sum"), 1)
                else:
                    v.tensor_scalar(sc, r, w, None, ALU.mult).then_inc(S("idx_sum"), 1)
        for r in range(TOPK // 8):
            for t in range(1, TT):
                if r == 0:
                    dve.wait_ge(S("score_masked"), t)
                else:
                    dve.wait_ge(S("top_taken"), 3 * (r - 1) + t)
                v.max(top8[:, t, :], score[:, t, 0:(t + 1) * P]).then_inc(S("top_found"), 1)
            for t in range(1, TT):
                dve.wait_ge(S("top_found"), 3 * r + t)
                v.match_replace(score[:, t, 0:(t + 1) * P], top8[:, t, :], score[:, t, 0:(t + 1) * P], CHOSEN)\
                    .then_inc(S("top_taken"), 1)
        for t in range(1, TT):
            dve.wait_ge(S("top_taken"), 3 * (TOPK // 8 - 1) + t)
            v.tensor_scalar(bias_q[:, t, 0:(t + 1) * P], score[:, t, 0:(t + 1) * P], CHOSEN, NEG, ALU.not_equal,
                            ALU.mult).then_inc(S("bias_made"), 1)
        phase_done(dve, "qk2")
        rope(qk_tm[:, :, :].rearrange("p t (h d) -> p t h d", d=HD), H1, 8, cosq, sinq, rt)
        v.tensor_copy(kiw[:, :, 64:128], kiw[:, :, 0:64]).then_inc(S("qk_roped"), 1)
        phase_done(dve, "gates")
        dve.wait_ge(S("pads"), 2)
        dve.wait_ge(S("tr_read"), TR["qk"][0] + 8)
        link(v.tensor_tensor(gc[:, :, 2:SEQ + 2], gc[:, :, 2:SEQ + 2], xi[:, :, :], ALU.mult))
        for f in range(4):
            col = [col_b[:, C_CW2 + 4 * j + f:C_CW2 + 4 * j + f + 1] for j in range(3)]
            link(v.tensor_scalar(ca[:, f, :], gc[:, f, 0:SEQ], col[0], None, ALU.mult))
            for j in (1, 2):
                link(v.scalar_tensor_tensor(out=ca[:, f, :], in0=gc[:, f, j:j + SEQ], scalar=col[j], in1=ca[:, f, :],
                                            op0=ALU.mult, op1=ALU.add))
            v.tensor_tensor(ca[:, f, :], ca[:, f, :], gb[:, f, :], ALU.mult).then_inc(S("conv2_out"), 1)
        for f in range(4):
            dve.wait_ge(S("conv2_hi"), f + 1)
            v.tensor_tensor(hlo[:, 4 + f, :], ca[:, f, :], fl(hhi[:, 4 + f, :]), ALU.subtract)\
                .then_inc(S("conv2_done"), 1)

        def row_max(base, h, m, scale):
            n, s = base + h, h % 2
            if h >= 2:
                dve.wait_ge(S("att_exps"), 4 * (n - 1))
            for q, t in enumerate((3, 2, 0, 1)):
                b, c0 = QB_AT[t]
                dve.wait_ge(S("att_logits"), 3 * n + [1, 2, 2, 3][q])
                op = v.reduce_max(m[:, s, t:t + 1], PX[s][:, b, c0:c0 + (t + 1) * P], AX, negate=True)
            link(op)
            v.tensor_scalar(m[:, s, :], m[:, s, :], scale, None, ALU.mult).then_inc(S("att_max"), 1)

        def emit(base, h, pt, d, dst):
            n, s = base + h, h % 2
            dve.wait_ge(S("att_turned"), n + 1)
            if h >= 2:
                dve.wait_ge(S("att_pv"), n - 1)
            v.tensor_copy(pt[s][:, SEQ:1280], PX[s][:, :, :].rearrange("p a b -> p (a b)")[:, SEQ:1280])\
                .then_inc(S("att_pt"), 1)
            dve.wait_ge(S("att_exps"), 4 * n + 4)
            link(v.reciprocal(d[:, s, :], d[:, s, :]))
            dve.wait_ge(S("att_pv"), n + 1)
            v.tensor_tensor(dst, PX[s][:, 3, 0:256].rearrange("p (t d) -> p t d", t=TT),
                            d[:, s, :].unsqueeze(2).to_broadcast([P, TT, HD]), ALU.mult).then_inc(S("att_out"), 1)

        for h in range(A_H + 1):
            if h < A_H:
                row_max(0, h, mx, HD ** -0.5)
            if h:
                emit(0, h - 1, prt, den, v2[:, :, (h - 1) * HD:h * HD])
        split_tiles("attn", 4, lambda k: 1.0, 0)
        dve.wait_ge(S("row_mix0"), 16)
        post_norm(5, mix2, row_b, "post_mix0")
        normed(6, "ffn0_made")
        split_tiles("ffn0", 8, lambda k: col_a[:, C_FFN + k:C_FFN + k + 1], 0)

        def mlp(name, layer):
            u0 = PH[name][0]
            MPAR = {0: 0, 2: 1, 6: 0}

            def up(first, i, m):
                base = m * 4 + 32 * layer

                def square(b, r):
                    dve.wait_ge(S(f"bank_free{b}"), r + (PH[name][1][b] + 1))
                    v.tensor_tensor(mh_r[:, b % 2, :], mh_r[:, b % 2, :], mh_r[:, b % 2, :], ALU.mult)\
                        .then_inc(S("hidden_sq"), 1)

                def low(b):
                    dve.wait_ge(S("hidden_hi"), base + (b + 1))
                    v.tensor_tensor(mh_lo[MPAR[first]][:, b, :], mh_r[:, b % 2, :], fl(mh_hi[MPAR[first]][:, b, :]),
                                    ALU.subtract).then_inc(S("hidden_ready"), 1)
                r = {0: 0, 2: i * 6 + 1, 6: i * 6 + 4}[first]
                square(0, r)
                square(1, r)
                low(0)
                square(2, r)
                low(1)
                square(3, r)
                low(2)
                low(3)

            def down(first, r, i):
                for h in range(2):
                    for b in range(4):
                        full_wait(dve, name, b, r + h, i * 8 + (u0 + first + h))
                        m = mixm[:, b, 512 * h:512 * h + 512]
                        v.tensor_tensor(m, PD[b], m, ALU.add).then_inc(S(f"bank_free{b}"), 1)

            dve.wait_ge(S("acc_zero"), layer + 1)
            up(0, 0, 0)
            with dve.Fori(0, 3) as i:
                up(2, i, i * 2 + 1)
                down(4, i * 6 + 2, i)
                up(6, i, i * 2 + 2)
                down(8, i * 6 + 5, i)
            up(2, 3, 7)
            down(4, 20, 3)
            down(6, 22, 3)

        mlp("mlp0", 0)
        dve.wait_ge(S("row_ffn0"), 16)
        post_norm(7, mixm, row_a, "post_ffn0")
        normed(8, "mix1_made")
        split_tiles("mix1", 8, lambda k: col_a[:, C_MIX + 8 + k:C_MIX + 9 + k], 0)
        mean_square(9, Q_RANK)
        for t in range(TT):
            v.tensor_scalar(cq[:, t, :], cq[:, t, :], rstd[:, 9, t:t + 1], None, ALU.mult).then_inc(S("cq_made"), 1)
        mean_square(10, KV_RANK)
        for t in range(TT):
            v.tensor_scalar(kva[:, t, 0:KV_RANK], kva[:, t, 0:KV_RANK], rstd[:, 10, t:t + 1], None, ALU.mult)\
                .then_inc(S("ckv_made"), 1)
        split_tiles("cq", 3, lambda k: col_b[:, C_QN + k:C_QN + k + 1], 0)
        split_tiles("ckv", 2, lambda k: col_b[:, C_KN + k:C_KN + k + 1], 3)
        rope(kva[:, :, 256:288].rearrange("p t (h d) -> p t h d", h=1), 1, 16, cosm, sinm, rtm)
        v.tensor_copy(k_tm[:, :, :, C_NOPE:C_QK], kva[:, :, 256:288].unsqueeze(2).to_broadcast([P, TT, C_H, 32]))
        u0 = PH["ukv"][0]
        for n in range(2):
            for r in range(2):
                for t in range(TT):
                    if t == 3 and r == 0:
                        dve.wait_ge(S("bank_full3"), PH["ukv"][2][3] + n + 1)
                    else:
                        full_wait(dve, "ukv", t, 2 * n + r, u0 + n)
                    h0 = 8 * n + 4 * r
                    kv = PD[t].rearrange("p (h d) -> p h d", h=4)
                    v.tensor_copy(k_tm[:, t, h0:h0 + 4, 0:C_NOPE], kv[:, :, 0:64])
                    v.tensor_copy(heads(v3[:, t, h0 * HD:(h0 + 4) * HD]), kv[:, :, 64:128])\
                        .then_inc(S(f"bank_free{t}"), 1)
        phase_done(dve, "uq")
        q4 = q_tm[:, :, :].rearrange("p t (h d) -> p t h d", d=C_QK)
        rope(q4[:, :, :, C_NOPE:C_QK], C_H, 16, cosm, sinm, rtm)
        v.tensor_copy(kva[:, 0, 0:8], kva[:, 0, 8:16]).then_inc(S("mla_roped"), 1)

        def turn_k(h):
            s = h % 2
            dve.wait_ge(S("tr_done"), TR["heads"][0] + 2 * h + 2)
            v.tensor_copy(kth[s][0:C_QK, :], PX[s][0:C_QK, 1, :]).then_inc(S("tr_read"), 1)

        for h in range(C_H + 1):
            if h < C_H:
                turn_k(h)
                row_max(A_H, h, mx3, C_QK ** -0.5)
            if h:
                emit(A_H, h - 1, prt3, den3, v3[:, :, (h - 1) * HD:h * HD])
        split_tiles("lat", 8, lambda k: 1.0, 0)
        dve.wait_ge(S("row_mix1"), 16)
        post_norm(11, mix3, row_b, "post_mix1")
        normed(12, "ffn1_made")
        split_tiles("ffn1", 8, lambda k: col_a[:, C_FFN + 8 + k:C_FFN + 9 + k], 0)
        mlp("mlp1", 1)
        dve.wait_ge(S("row_ffn1"), 16)
        post_norm(13, mixm, row_a, "post_ffn1")

    ctx.close()


NAMES = ["x", "c", "w_ada", "b_ada", "norm_in_gain", "w_in", "conv_w", "conv_b", "dt_bias", "a_log", "d_skip",
         "sb_norm_gain", "ssm_norm_gain", "w_out", "norm_f_gain", "positions_2", "norm_mix_pre_2",
         "norm_mix_post_2", "norm_ffn_pre_2", "norm_ffn_post_2", "even_w_in_2", "even_conv_w_2", "even_w_out_2",
         "odd_w_dq_2", "odd_q_norm_2", "odd_w_uq_2", "odd_w_dkv_2", "odd_kv_norm_2", "odd_w_ukv_2", "odd_w_o_2",
         "mlp_w1_2", "mlp_w2_2"]


def kernel(**inputs):
    import numpy as np
    import concourse.bacc as bacc
    from concourse.bass_utils import run_bass_kernel_spmd

    nc = bacc.Bacc("TRN2", target_bir_lowering=False, num_devices=1, dynamic_dma_scratch_size=1024)
    arrays, args = {}, []
    for name in NAMES:
        a = np.ascontiguousarray(inputs[name])
        arrays[f"in_{name}"] = a
        args.append(nc.dram_tensor(f"in_{name}", a.shape, mybir.dt.from_np(a.dtype), kind="ExternalInput").ap())
    args.append(nc.dram_tensor("out_0", (1, SEQ, DM), F32, kind="ExternalOutput").ap())
    build_program(nc, *args)
    r = run_bass_kernel_spmd(nc, [arrays], core_ids=[0])
    return r.results[0]["out_0"]
```

```python
import math
from contextlib import ExitStack

import concourse.bass as bass
from concourse import mybir

F32 = mybir.dt.float32
F32R = mybir.dt.float32r
I32 = mybir.dt.int32
ACT = mybir.ActivationFunctionType
ALU = mybir.AluOpType
AX = mybir.AxisListType.X

P = 128
SEQ = 512
DM = 1024
TT = SEQ // P
KT = DM // P
UNIT = 2048
NEG = -1e30
DROPPED = -3e38
CHOSEN = -2e38
EPS = 1e-6
H1 = 16
HD = 64
GROUPS = 2
HG = H1 // GROUPS
XBC_T = 12
A_H = 8
TOPK = 128
C_H = 16
C_QK = 96
C_NOPE = 64
Q_RANK = 384
KV_RANK = 256
D_FF = 4096
THETA = 500000.0
N_PARAMS = 16
ROUNDER = 1.5 * 2.0 ** 23
TWO_PI = [6.28125, 1014 / 2.0 ** 19, 2 * math.pi - 6.28125 - 1014 / 2.0 ** 19]
PI_BELOW = 3.1415925
CLAMP = 20.0
IDX_AT = {1: 0, 2: 256, 3: 640}


def phase_table():
    def rounds(n):
        return [n] * 4, [n, n, n, 0]

    rows = [
        ("ada_ss", 8, ([1] * 4, [0] * 4)), ("ada_g", 4, ([1, 1, 0, 0], [0] * 4)), ("q", 4, rounds(2)), ("k", 4, rounds(2)), ("v", 4, rounds(2)),
        ("xbc", 6, rounds(3)), ("z_ssm", 4, rounds(2)), ("dt", 1, ([1, 0, 0, 0], [0] * 4)),
        ("z_attn", 4, rounds(2)), ("wout_a", 4, rounds(2)),
        ("wout_s", 4, rounds(2)), ("qi", 4, rounds(2)), ("kiw", 1, rounds(1)), ("qk2", 4, rounds(2)),
        ("v2", 2, rounds(1)), ("gates", 6, rounds(3)), ("wo2", 4, rounds(2)), ("mlp0", 32, rounds(24)),
        ("dq", 2, rounds(1)), ("dkv", 2, rounds(1)), ("uq", 3, rounds(3)),
        ("ukv", 2, ([4] * 4, [4, 4, 4, 2])), ("wo3", 4, rounds(2)), ("mlp1", 32, rounds(24)),
    ]
    unit, free, full, table = 0, [0] * 4, [0] * 4, {}
    for name, units, (f, g) in rows:
        table[name] = (unit, list(free), list(full), units)
        unit += units
        free = [a + b for a, b in zip(free, f)]
        full = [a + b for a, b in zip(full, g)]
    table["end"] = (unit, list(free), list(full), 0)
    return table


def transpose_table():
    rows = [("params", 2, 0), ("h", 8, 1), ("scan", 10, 0), ("y_attn", 8, 1), ("y_ssm", 8, 1), ("mix0", 8, 1),
            ("qi", 8, 0), ("ki", 1, 0), ("qk", 8, 0), ("attn", 4, 1), ("ffn0", 8, 1), ("mix1", 8, 1),
            ("cq", 3, 1), ("ckv", 2, 1), ("heads", 2 * C_H, 0), ("lat", 8, 1), ("ffn1", 8, 1)]
    n, split, table = 0, 0, {}
    for name, groups, is_split in rows:
        table[name] = (n, split)
        n += groups
        split += groups * is_split
    return table


def build_program(nc, x, c, w_ada, b_ada, norm_in_gain, w_in, conv_w, conv_b, dt_bias, a_log, d_skip,
                  sb_norm_gain, ssm_norm_gain, w_out, norm_f_gain, positions_2, norm_mix_pre_2,
                  norm_mix_post_2, norm_ffn_pre_2, norm_ffn_post_2, even_w_in_2, even_conv_w_2,
                  even_w_out_2, odd_w_dq_2, odd_q_norm_2, odd_w_uq_2, odd_w_dkv_2, odd_kv_norm_2,
                  odd_w_ukv_2, odd_w_o_2, mlp_w1_2, mlp_w2_2, out):
    PH = phase_table()
    TR = transpose_table()
    ctx = ExitStack()
    sems = {}

    def S(name):
        if name not in sems:
            sems[name] = ctx.enter_context(nc.semaphore(name))
        return sems[name]

    cursor = [(nc.sbuf_base + 63) // 64 * 64]

    def at(name, shape, dtype=F32, offset=None):
        size = 4
        for n in shape[1:]:
            size *= n
        if offset is None:
            offset = cursor[0]
            cursor[0] += (size + 31) // 32 * 32
        return nc.alloc_sbuf_tensor_at(name, shape, dtype, offset=offset)

    wraw = [at(f"wraw{s}", [P, UNIT]) for s in range(2)]
    whi = [at(f"whi{s}", [P, UNIT], F32R) for s in range(2)]
    wlo = [at(f"wlo{s}", [P, UNIT], F32R) for s in range(2)]
    hhi = at("hhi", [P, KT, SEQ], F32R)
    hlo = at("hlo", [P, KT, SEQ], F32R)
    xres = at("xres", [P, TT, DM])
    ident = at("ident", [P, P])
    identr = at("identr", [P, P], F32R)
    ones = at("ones", [P, P])
    tri_le = at("tri_le", [P, P])
    tri_gt = at("tri_gt", [P, P])
    neg_ge = at("neg_ge", [P, P], F32R)
    neg_one = at("neg_one", [P, P], F32R)
    mask_t = at("mask_t", [P, P], F32R)
    mask_q = at("mask_q", [P, P], F32R)
    scratch = at("scratch", [P, P])
    scratch1 = at("scratch1", [P, P])
    junk = at("junk", [P, 2, DM], mybir.dt.bfloat16)
    sinall = at("sinall", [P, TT, 24])
    col_a = at("col_a", [P, P])
    col_b = at("col_b", [P, 32])
    stat = at("stat", [P, 16, TT])
    rstd = at("rstd", [P, 16, TT])
    mhalf = at("mhalf", [P, TT])
    cact = at("cact", [P, KT])
    small = at("small", [P, 64])
    cosq = at("cosq", [P, TT, 8])
    sinq = at("sinq", [P, TT, 8])
    cosm = at("cosm", [P, TT, 16])
    sinm = at("sinm", [P, TT, 16])
    row_a = at("row_a", [P, DM])
    row_b = at("row_b", [P, DM])
    A0 = cursor[0]
    KB = 1024

    def arena(name, shape, kb, dtype=F32):
        return at(name, shape, dtype, offset=A0 + int(kb * KB))

    xn = arena("xn", [P, TT, DM], 0)
    b_row = arena("b_row", [P, 2 * DM], 40)
    mod = arena("mod", [P, 2 * DM], 48)
    prm_a = arena("prm_a", [P, P], 60)
    prm_b = arena("prm_b", [32, P], 60.5)
    pos_i = arena("pos_i", [P, TT], 64, I32)
    pos_f = arena("pos_f", [P, TT], 64.25)
    freq = arena("freq", [P, 24], 64.5)
    ang = arena("ang", [P, TT, 24], 65)
    ang_n = arena("ang_n", [P, TT, 24], 66)
    ang_s = arena("ang_s", [P, TT, 24], 67)
    chi = arena("chi", [P, KT, P], 70, F32R)
    clo = arena("clo", [P, KT, P], 74, F32R)
    gate = arena("gate", [P, DM], 98)
    qt = arena("qt", [P, KT, SEQ], 0)
    kt = arena("kt", [P, KT, SEQ], 16)
    vo = arena("vo", [P, TT, DM], 32)
    sb_l = arena("sb_l", [P, 1280], 48)
    sb_hi = arena("sb_hi", [P, 1280], 53, F32R)
    sb_lo = arena("sb_lo", [P, 1280], 58, F32R)
    sb_w = arena("sb_w", [P, 1280], 63)
    za = arena("za", [P, TT, DM], 16)
    mix = arena("mix", [P, TT, DM], 16)
    xbc = arena("xbc", [P, XBC_T, SEQ + 3], 68)
    dts = arena("dts", [P, 6, TT * H1], 92.5)
    conv_acc = arena("conv_acc", [P, 2, SEQ], 94)
    zs = xres
    yt = arena("yt", [P, TT, DM], 0)
    xdt = arena("xdt", [P, DM], 48)
    xdte = arena("xdte", [P, DM], 52)
    hst = arena("hst", [P, DM], 56)
    b_tm = arena("b_tm", [P, TT, 2 * P], 60)
    cbm = arena("cbm", [P, 8, P], 64)
    ldm = arena("ldm", [P, H1, P], 68)
    dec = [arena(f"dec{s}", [P, HG, P], 76 + 4 * s) for s in range(2)]
    off = arena("off", [P, SEQ], 94)
    xd = arena("xd", [P, SEQ], 96)
    qi_tm = arena("qi_tm", [P, TT, DM], 0)
    qk_tm = arena("qk_tm", [P, TT, DM], 16)
    kiw = arena("kiw", [P, TT, 144], 32)
    v2 = arena("v2", [P, TT, 512], 34.5)
    qit = arena("qit", [P, KT, SEQ], 42.5)
    kit = arena("kit", [P, SEQ], 58.5)
    score = arena("score", [P, TT, SEQ], 60.5)
    relu_s = arena("relu_s", [P, 2, 1152], 68.5)
    top8 = arena("top8", [P, TT, 8], 77.5)
    qkt = arena("qkt", [P, KT, SEQ], 78)
    rt = arena("rt", [P, 4, TT * H1 * 8], 94)
    bias_q = arena("bias_q", [P, TT, SEQ], 0, F32R)
    pr = [arena("pr0", [P, 1280], 8), arena("pr1", [P, 1280], 13)]
    prt = [arena("prt0", [P, 1280], 18), arena("prt1", [P, 1280], 23)]
    mx = arena("mx", [P, 2, TT], 77.625)
    den = arena("den", [P, 2, TT], 77.75)
    gb = arena("gb", [P, TT, SEQ], 42.5)
    gc = arena("gc", [P, TT, SEQ + 2], 50.5)
    xi = arena("xi", [P, TT, SEQ], 68.5)
    ca = arena("ca", [P, TT, SEQ], 94)
    mix2 = arena("mix2", [P, TT, DM], 58.75)
    mh_hi = [arena(f"mh_hi{s}", [P, 4, SEQ], 16 + 16 * s, F32R) for s in range(2)]
    mh_lo = [arena(f"mh_lo{s}", [P, 4, SEQ], 24 + 16 * s, F32R) for s in range(2)]
    mh_r = arena("mh_r", [P, 2, SEQ], 48)
    mixm = arena("mixm", [P, TT, DM], 56)
    kva = arena("kva", [P, TT, 288], 16)
    cq = arena("cq", [P, TT, Q_RANK], 21)
    q_tm = arena("q_tm", [P, TT, C_H * C_QK], 27)
    k_tm = arena("k_tm", [P, TT, C_H, C_QK], 51)
    v3 = arena("v3", [P, TT, DM], 75)
    rtm = arena("rtm", [P, 4, TT * C_H * 16], 0)
    qth = [arena(f"qth{s}", [P, SEQ], 2 * s) for s in range(2)]
    kth = [arena(f"kth{s}", [P, SEQ], 4 + 2 * s) for s in range(2)]
    pr3 = [arena("pr30", [P, 1280], 8), arena("pr31", [P, 1280], 16)]
    prt3 = [arena("prt30", [P, 1280], 21), arena("prt31", [P, 1280], 91)]
    mx3 = arena("mx3", [P, 2, TT], 14)
    den3 = arena("den3", [P, 2, TT], 14.5)
    mix3 = arena("mix3", [P, TT, DM], 27)
    assert A0 + 102 * KB <= nc.sbuf_usable_end, (A0, nc.sbuf_usable_end)

    PDT = ctx.enter_context(nc.psum_tensor("PDT", [P, 4, SEQ], F32))
    PM = ctx.enter_context(nc.psum_tensor("PM", [P, 4, SEQ], F32))
    PD = [PDT[:, b, :] for b in range(4)]
    PX = [PM, PDT]

    C_C, C_CW, C_CB, C_SBG, C_SSG, C_MIX, C_FFN = 0, 8, 56, 68, 76, 84, 100
    C_QN, C_KN, C_CW2 = 0, 3, 5
    ROWS_A, ROWS_B = 116, 17

    SB_CHUNKS = [[(1, 0), (3, 384)], [(2, 0)], [(0, 0)]]
    SB_FIRST = [0, 512, 768]
    SB_WIDE = [512, 256, 512]
    SB_AT = {1: (0, 0), 3: (0, 384), 2: (1, 0), 0: (2, 0)}
    QB_AT = {3: (0, 0), 2: (1, 0), 0: (1, 384), 1: (2, 0)}
    QB_FIRST = {3: 0, 2: 512, 0: 896, 1: 1024}

    def kmajor(w):
        return w.rearrange("(k p) n -> p k n", p=P)

    w_ada_v, w_in_v, w_out_v = kmajor(w_ada[0]), kmajor(w_in[0]), kmajor(w_out[0])
    w_even_v, w_eo_v = kmajor(even_w_in_2[0]), kmajor(even_w_out_2[0])
    w_dq_v, w_uq_v, w_dkv_v = kmajor(odd_w_dq_2[0]), kmajor(odd_w_uq_2[0]), kmajor(odd_w_dkv_2[0])
    w_ukv_v, w_oo_v = kmajor(odd_w_ukv_2[0]), kmajor(odd_w_o_2[0])
    w1_v = [kmajor(mlp_w1_2[j]) for j in range(2)]
    w2_v = [kmajor(mlp_w2_2[j]) for j in range(2)]

    def wview(t, kn, n):
        return t[:, 0:kn * n].rearrange("p (k n) -> p k n", k=kn)

    def fl(ap):
        return ap.bitcast(F32)

    def loop(eng, n, body):
        if n == 1:
            body(0)
        else:
            with eng.Fori(0, n) as i:
                body(i)

    def dyn(t, i, b):
        return t[:, bass.ds(i * 4 + b, 1), :]

    def phase_done(eng, name):
        names = list(PH)
        after = PH[names[names.index(name) + 1]][1]
        for b in range(4):
            if after[b] > PH[name][1][b]:
                eng.wait_ge(S(f"bank_free{b}"), after[b])

    def full_wait(eng, name, b, r, unit):
        if b < 3:
            eng.wait_ge(S(f"bank_full{b}"), r + (PH[name][2][b] + 1))
        else:
            eng.wait_ge(S("w_used"), unit + 1)

    def pieces(name, rounds):
        return [(name, r, h, b) for r in range(rounds) for h in range(2) for b in range(4)]

    SB_PIECES = pieces("xbc", 3) + pieces("z_ssm", 2) + [("dt", 0, 0, 0)] + pieces("z_attn", 1)
    SCAN_PIECES = pieces("wout_a", 2)

    def step_pieces(n):
        return SCAN_PIECES[(3 * n + 1) // 2:(3 * n + 4) // 2]

    block = ctx.enter_context(nc.Block())

    @block.sync
    def _(sp):
        def load(dst, src, sem="params"):
            sp.dma_start(dst, src).then_inc(S(sem), 16)

        def unit(u, par, kn, n, src):
            if not isinstance(u, int) or u >= 2:
                sp.wait_ge(S("w_split"), u - 1)
            sp.dma_start(wview(wraw[par], kn, n), src).then_inc(S(f"w_loaded{par}"), 16)

        def columns(name, w, n_chunks, c0, k0=0):
            u0 = PH[name][0]

            def body(i):
                cc = c0 + i * 512 if isinstance(i, int) else sp.snap(i * 512 + c0)
                for h in range(2):
                    par = (u0 + h) % 2
                    unit(i * 2 + (u0 + h), par, 4, 512,
                         w[:, k0 + 4 * h:k0 + 4 * h + 4, bass.ds(cc, 512)])
            loop(sp, n_chunks, body)

        def mlp(name, j):
            u0 = PH[name][0]

            def up(i, d):
                cc = i * 1024 + 512 * d if isinstance(i, int) else sp.snap(i * 1024 + 512 * d)
                return [w1_v[j][:, 4 * h:4 * h + 4, bass.ds(cc, 512)] for h in range(2)]

            def down(i, d):
                kk = i * 8 + 4 * d if isinstance(i, int) else sp.snap(i * 8 + 4 * d)
                return [w2_v[j][:, bass.ds(kk, 4), 512 * h:512 * h + 512] for h in range(2)]

            def four(i, first, srcs):
                for n, s in enumerate(srcs):
                    unit(i * 8 + (u0 + first + n), (u0 + first + n) % 2, 4, 512, s)

            four(0, 0, up(0, 0))
            with sp.Fori(0, 3) as i:
                four(i, 2, up(i, 1))
                four(i, 4, down(i, 0))
                four(i, 6, up(i, 2))
                four(i, 8, down(i, 1))
            four(3, 2, up(3, 1))
            four(3, 4, down(3, 0))
            four(3, 6, down(3, 1))

        load(prm_a[C_C:C_C + 8, :], c.rearrange("a (k p) -> (a k) p", p=P), "params_c")
        for u in range(2):
            unit(u, u % 2, 4, 512, w_ada_v[:, 4 * u:4 * u + 4, DM:DM + 512])
        load(xres[:, :, :], x[0].rearrange("(t p) n -> p t n", p=P), "x_loaded")
        load(prm_a[C_CW:C_CW + 48, :], conv_w[0].rearrange("j (k p) -> (j k) p", p=P))
        load(prm_a[C_CB:C_CB + 12, :], conv_b[0].rearrange("(k p) -> k p", p=P))
        load(prm_a[C_SBG:C_SBG + 8, :], sb_norm_gain[0].rearrange("(k p) -> k p", p=P))
        load(prm_a[C_SSG:C_SSG + 8, :], ssm_norm_gain[0].rearrange("(k p) -> k p", p=P))
        load(prm_a[C_MIX:C_MIX + 16, :], norm_mix_pre_2.rearrange("j (k p) -> (j k) p", p=P))
        load(prm_a[C_FFN:C_FFN + 16, :], norm_ffn_pre_2.rearrange("j (k p) -> (j k) p", p=P))
        load(prm_b[C_QN:C_QN + 3, :], odd_q_norm_2[0].rearrange("(k p) -> k p", p=P))
        load(prm_b[C_KN:C_KN + 2, :], odd_kv_norm_2[0].rearrange("(k p) -> k p", p=P))
        load(prm_b[C_CW2:C_CW2 + 12, :], even_conv_w_2[0].rearrange("j (k p) -> (j k) p", p=P))
        with nc.allow_non_contiguous_dma(reason="512 positions"):
            load(pos_i[:, :], positions_2[0].rearrange("(t p) -> p t", p=P))
        load(row_a[:, :], norm_in_gain[0].partition_broadcast(P))
        load(b_row[:, :], b_ada[0][0:2 * DM].partition_broadcast(P))
        load(small[:, 0:16], dt_bias[0].partition_broadcast(P))
        load(small[:, 16:32], a_log[0].partition_broadcast(P))
        load(small[:, 32:48], d_skip[0].partition_broadcast(P))
        load(row_b[:, :], b_ada[0][2 * DM:3 * DM].partition_broadcast(P))
        for u in range(2, 8):
            cc = [DM, DM + 512, 0, 512][u // 2]
            unit(u, u % 2, 4, 512, w_ada_v[:, 4 * (u % 2):4 * (u % 2) + 4, cc:cc + 512])
        columns("ada_g", w_ada_v, 2, 2 * DM)
        columns("q", w_in_v, 2, 0)
        columns("k", w_in_v, 2, DM)
        columns("v", w_in_v, 2, 2 * DM)
        sp.wait_ge(S("h_made"), TT)
        load(row_a[:, :], norm_f_gain.partition_broadcast(P), "row_f")
        columns("xbc", w_in_v, 3, 4 * DM)
        columns("z_ssm", w_in_v, 2, 4 * DM + 1552)
        u0 = PH["dt"][0]
        unit(u0, u0 % 2, 8, 16, w_in_v[:, :, 4 * DM + 1536:4 * DM + 1552])
        columns("z_attn", w_in_v, 2, 3 * DM)
        columns("wout_a", w_out_v, 2, 0)
        columns("wout_s", w_out_v, 2, 0, k0=8)
        sp.wait_ge(S("y_gated"), TT)
        load(xres[:, :, :], x[0].rearrange("(t p) n -> p t n", p=P), "x_again")
        columns("qi", w_even_v, 2, 1536)
        u0 = PH["kiw"][0]
        unit(u0, u0 % 2, 8, 80, w_even_v[:, :, 2560:2640])
        phase_done(sp, "ada_g")
        load(row_b[:, :], norm_mix_post_2[0].partition_broadcast(P), "row_mix0")
        columns("qk2", w_even_v, 2, 0)
        columns("v2", w_even_v, 1, DM)
        columns("gates", w_even_v, 3, 2640)
        sp.wait_ge(S("first_out"), TT)
        load(row_a[:, :], norm_ffn_post_2[0].partition_broadcast(P), "row_ffn0")
        columns("wo2", w_eo_v, 2, 0)
        mlp("mlp0", 0)
        sp.wait_ge(S("post_mix0"), TT)
        load(row_b[:, :], norm_mix_post_2[1].partition_broadcast(P), "row_mix1")
        u0 = PH["dq"][0]
        for h in range(2):
            unit(u0 + h, (u0 + h) % 2, 4, Q_RANK, w_dq_v[:, 4 * h:4 * h + 4, :])
        u0 = PH["dkv"][0]
        for h in range(2):
            unit(u0 + h, (u0 + h) % 2, 4, 288, w_dkv_v[:, 4 * h:4 * h + 4, :])
        u0 = PH["uq"][0]
        for n in range(3):
            unit(u0 + n, (u0 + n) % 2, 3, 512, w_uq_v[:, :, 512 * n:512 * n + 512])
        u0 = PH["ukv"][0]
        for n in range(2):
            unit(u0 + n, (u0 + n) % 2, 2, 1024, w_ukv_v[:, :, 1024 * n:1024 * n + 1024])
        columns("wo3", w_oo_v, 2, 0)
        mlp("mlp1", 1)
        sp.wait_ge(S("post_ffn0"), TT)
        load(row_a[:, :], norm_ffn_post_2[1].partition_broadcast(P), "row_ffn1")
        for t in range(TT):
            sp.wait_ge(S("post_ffn1"), t + 1)
            sp.dma_start(out[0, t * P:(t + 1) * P, :], xres[:, t, :]).then_inc(S("stored"), 16)
        sp.wait_ge(S("stored"), 16 * TT)

    @block.tensor
    def _(pe):
        mm = nc.tensor.matmul

        def bank_wait(name, b, r):
            pe.wait_ge(S(f"bank_free{b}"), r + PH[name][1][b])

        def unit_wait(u):
            pe.wait_ge(S("w_split"), u + 1)

        def tm(bank, n, act, k0, ws, kn, nn, c0, start, stop, t):
            hi, lo = act
            wh, wl = wview(whi[ws], kn, nn), wview(wlo[ws], kn, nn)
            for k in range(kn):
                sth, stl = hi[:, k0 + k, t * P:t * P + P], lo[:, k0 + k, t * P:t * P + P]
                mm(bank, sth, wh[:, k, c0:c0 + n], start=start and k == 0, stop=False)
                mm(bank, sth, wl[:, k, c0:c0 + n], start=False, stop=False)
                last = mm(bank, stl, wh[:, k, c0:c0 + n], start=False, stop=stop and k == kn - 1)
            return last

        def fm(bank, act, k0, ws, f, start, stop):
            hi, lo = act
            wh, wl = wview(whi[ws], 4, 512), wview(wlo[ws], 4, 512)
            for k in range(4):
                sth, stl = wh[:, k, f * P:f * P + P], wl[:, k, f * P:f * P + P]
                mm(bank, sth, hi[:, k0 + k, :], start=start and k == 0, stop=False)
                mm(bank, sth, lo[:, k0 + k, :], start=False, stop=False)
                last = mm(bank, stl, hi[:, k0 + k, :], start=False, stop=stop and k == 3)
            return last

        def full(last, b):
            last.then_inc(S("w_used" if b == 3 else f"bank_full{b}"), 1)

        def two_units(name, first, r, i, stride, feature_major, n=512):
            u0 = PH[name][0] + first
            for h in range(2):
                unit_wait(i * stride + (u0 + h))
                for b in range(4):
                    if h == 0:
                        bank_wait(name, b, r)
                    if feature_major:
                        last = fm(PD[b], (hhi, hlo), 4 * h, (u0 + h) % 2, b, h == 0, h == 1)
                    else:
                        last = tm(PD[b][:, 0:n], n, (hhi, hlo), 4 * h, (u0 + h) % 2, 4, n, 0, h == 0, h == 1, b)
                    if h == 1:
                        full(last, b)
                if h == 0:
                    last.then_inc(S("w_used"), 1)

        def chunks(name, n, feature_major):
            loop(pe, n, lambda i: two_units(name, 0, i, i, 2, feature_major))

        def transposes(name, nk, src):
            for k in range(nk):
                n = TR[name][0] + k
                pe.wait_ge(S("tr_read"), max(TR[name][0], n - 3))
                for t in range(TT):
                    last = nc.tensor.transpose(PM[:, k % 4, t * P:t * P + P], src(t, k), ident[:, :])
                last.then_inc(S("tr_done"), 1)

        def transposed(name, nk):
            pe.wait_ge(S("tr_read"), TR[name][0] + nk)

        def mlp(name, layer):
            u0 = PH[name][0]

            def up(first, r, i):
                two_units(name, first, r, i, 8, True)

            def down(par, first, r, i, m):
                pe.wait_ge(S("hidden_ready"), m * 4 + (32 * layer + 4))
                for h in range(2):
                    unit_wait(i * 8 + (u0 + first + h))
                    for b in range(4):
                        bank_wait(name, b, r + h)
                        full(tm(PD[b], 512, (mh_hi[par], mh_lo[par]), 0, (u0 + first + h) % 2, 4, 512,
                                0, True, True, b), b)

            up(0, 0, 0)
            with pe.Fori(0, 3) as i:
                up(2, i * 6 + 1, i)
                down(0, 4, i * 6 + 2, i, i * 2)
                up(6, i * 6 + 4, i)
                down(1, 8, i * 6 + 5, i, i * 2 + 1)
            up(2, 19, 3)
            down(0, 4, 20, 3, 6)
            down(1, 6, 22, 3, 7)

        pe.wait_ge(S("masks"), 1)
        pe.wait_ge(S("params_c"), 16)
        nc.tensor.transpose(PM[:, 3, 0:8], prm_a[0:8, :], ident[0:8, 0:8]).then_inc(S("tr_done"), 1)
        pe.wait_ge(S("c_split"), 1)

        def ada(name, j, first, chi, clo):
            for h in range(2):
                u = PH[name][0] + first + h
                unit_wait(u)
                if h == 0:
                    bank_wait(name, j, 0)
                wh, wl = wview(whi[u % 2], 4, 512), wview(wlo[u % 2], 4, 512)
                for k in range(4):
                    ch, cl = chi[:, 4 * h + k, :], clo[:, 4 * h + k, :]
                    mm(PD[j], ch, wh[:, k, :], start=h == 0 and k == 0, stop=False)
                    mm(PD[j], ch, wl[:, k, :], start=False, stop=False)
                    last = mm(PD[j], cl, wh[:, k, :], start=False, stop=h == 1 and k == 3)
                last.then_inc(S("w_used"), 1)

        ada("ada_ss", 0, 0, chi, clo)
        pe.wait_ge(S("params"), 16 * N_PARAMS)
        nc.tensor.transpose(PM[:, 2, 0:ROWS_A], prm_a[0:ROWS_A, :], ident[0:ROWS_A, 0:ROWS_A])
        nc.tensor.transpose(PM[:, 2, P:P + ROWS_B], prm_b[0:ROWS_B, :], ident[0:ROWS_B, 0:ROWS_B]).then_inc(S("tr_done"), 1)
        for j in range(1, 4):
            ada("ada_ss", j, 2 * j, chi, clo)
        for j in range(2):
            ada("ada_g", j, 2 * j, chi, clo)
        pe.wait_ge(S("h_made"), TT)
        transposes("h", 8, lambda t, k: xn[:, t, k * P:k * P + P])
        transposed("h", 8)
        chunks("q", 2, True)
        chunks("k", 2, True)
        chunks("v", 2, False)

        def sb_scores(h):
            p0, ft = HD * (h % 2), h // 2
            for n, blocks in enumerate(SB_CHUNKS):
                if h:
                    pe.wait_ge(S("sb_weights"), 3 * (h - 1) + n + 1)
                for m, (s, c0) in enumerate(blocks):
                    w = SEQ - s * P
                    mm(PM[:, n, c0:c0 + w], kt[p0:p0 + HD, ft, s * P:s * P + P], qt[p0:p0 + HD, ft, s * P:SEQ],
                       start=m == 0, stop=False, skip_group_check=True)
                    last = mm(PM[:, n, c0:c0 + P], identr[:, :], mask_t[:, :], start=False, stop=False,
                              skip_group_check=True)
                last.then_inc(S("sb_z"), 1)

        def sb_tails(h):
            for n, blocks in enumerate(SB_CHUNKS):
                pe.wait_ge(S("sb_split"), 3 * h + max(n + 1, 2))
                for m, (s, c0) in enumerate(blocks):
                    for j in range(s, TT):
                        cj, cc = SB_AT[j]
                        a = SB_FIRST[cj] + cc
                        w = SEQ - j * P
                        st = neg_ge if j == s else neg_one
                        o = PM[:, n, c0 + (j - s) * P:c0 + (j - s) * P + w]
                        for part in (sb_hi, sb_lo):
                            last = mm(o, st[:, :], part[:, a:a + w], start=False,
                                      stop=m == len(blocks) - 1 and j == TT - 1 and part is sb_lo,
                                      skip_group_check=True)
                last.then_inc(S("sb_tail"), 1)

        def sb_values(h):
            if h >= 2:
                pe.wait_ge(S("sb_out"), h - 1)
            pe.wait_ge(S("sb_weights"), 3 * h + 3)
            for t in range(TT):
                for s in range(t + 1):
                    cj, cc = SB_AT[s]
                    a = SB_FIRST[cj] + cc + (t - s) * P
                    last = mm(PM[:, 3, (h % 2) * 256 + t * HD:(h % 2) * 256 + t * HD + HD], sb_w[:, a:a + P],
                              vo[:, s, h * HD:h * HD + HD], start=s == 0, stop=s == t)
            last.then_inc(S("sb_pv"), 1)

        for name in ("q", "k", "v"):
            phase_done(pe, name)
        def piece(name, r, h, b):
            u = PH[name][0] + 2 * r + h
            if b == 0:
                unit_wait(u)
            if h == 0:
                bank_wait(name, b, r)
            if name == "dt":
                for t in range(TT):
                    last = tm(PD[0][:, 16 * t:16 * t + 16], 16, (hhi, hlo), 0, u % 2, 8, 16, 0, True, True, t)
                last.then_inc(S("w_used"), 1)
                return
            if name == "xbc":
                last = fm(PD[b], (hhi, hlo), 4 * h, u % 2, b, h == 0, h == 1)
            else:
                last = tm(PD[b], 512, (hhi, hlo), 4 * h, u % 2, 4, 512, 0, h == 0, h == 1, b)
            if h == 1:
                full(last, b)
            elif b == 3:
                last.then_inc(S("w_used"), 1)

        for h in range(H1):
            sb_scores(h)
            if h:
                sb_values(h - 1)
            piece(*SB_PIECES[3 * h])
            piece(*SB_PIECES[3 * h + 1])
            sb_tails(h)
            piece(*SB_PIECES[3 * h + 2])
        sb_values(H1 - 1)
        for p in SB_PIECES[3 * H1:]:
            piece(*p)
        two_units("z_attn", 2, 1, 0, 2, False)

        pe.wait_ge(S("conv_done"), XBC_T)
        transposes("scan", 10, lambda t, k: xbc[:, k, t * P:t * P + P])
        transposed("scan", 10)
        pe.wait_ge(S("ld_made"), 1)
        mm(PM[:, 3, 0:64], tri_le[:, :], dts[:, 1, :], start=True, stop=True)
        mm(PM[:, 3, 64:128], tri_gt[:, :], dts[:, 1, :], start=True, stop=True)
        mm(PM[:, 3, 128:192], ones[:, :], dts[:, 1, :], start=True, stop=True).then_inc(S("scan_cum"), 1)
        for g in range(GROUPS):
            for t in range(TT):
                last = mm(PM[:, g, t * P:t * P + P], xbc[:, 8 + g, t * P:t * P + P], xbc[:, 10 + g, t * P:t * P + P],
                          start=True, stop=True)
        last.then_inc(S("scan_cb"), 1)
        pe.wait_ge(S("scan_exps"), 1)
        pe.wait_ge(S("cbm_made"), 1)
        pe.wait_ge(S("y_attn_made"), TT)
        transposes("y_attn", 8, lambda t, k: vo[:, t, k * P:k * P + P])
        transposed("y_attn", 8)

        def segment(n):
            t, g = n // 2, n % 2
            pe.wait_ge(S("ldm_made"), t + 1)
            if n:
                pe.wait_ge(S("scan_dec"), n)
            for h in range(HG):
                last = mm(PM[:, h // 4, (h % 4) * P:(h % 4) * P + P], ldm[:, g * HG + h, :], tri_le[:, :],
                          start=True, stop=True)
            last.then_inc(S("scan_seg"), 1)

        segment(0)
        for n in range(2 * TT):
            t, g = n // 2, n % 2
            first, *rest = step_pieces(n)
            piece(*first)
            if t:
                pe.wait_ge(S("hst_made"), min(n, 2 * (TT - 1)))
                if n == 2 * TT - 1:
                    pe.wait_ge(S("off_read"), n - 2)
                mm(PM[:, 3, :], xbc[:, 10 + g, t * P:t * P + P], hst[:, g * 512:g * 512 + 512],
                   start=True, stop=True).then_inc(S("scan_off"), 1)
            for p in rest:
                piece(*p)
            pe.wait_ge(S("scan_m"), n + 1)
            if n:
                pe.wait_ge(S("scan_y"), n)
            for h in range(HG):
                a = (g * HG + h) * HD
                last = mm(PM[:, 2, h * HD:h * HD + HD], dec[g][:, h, :], xdt[:, a:a + HD], start=True, stop=True)
            last.then_inc(S("scan_diag"), 1)
            if t < TT - 1:
                pe.wait_ge(S("xdte_made"), t + 1)
                if t:
                    pe.wait_ge(S("off_read"), n - 1)
                elif g:
                    pe.wait_ge(S("hst_made"), 1)
                mm(PM[:, 3, :], b_tm[:, t, g * P:g * P + P], xdte[:, g * 512:g * 512 + 512],
                   start=True, stop=True).then_inc(S("scan_st"), 1)
            if n < 2 * TT - 1:
                segment(n + 1)
        for p in SCAN_PIECES[3 * TT:]:
            piece(*p)
        pe.wait_ge(S("y_ssm_made"), TT)
        transposes("y_ssm", 8, lambda t, k: yt[:, t, k * P:k * P + P])
        transposed("y_ssm", 8)
        chunks("wout_s", 2, False)

        pe.wait_ge(S("mix0_made"), TT)
        transposes("mix0", 8, lambda t, k: xn[:, t, k * P:k * P + P])
        transposed("mix0", 8)
        chunks("qi", 2, False)
        u0 = PH["kiw"][0]
        unit_wait(u0)
        for t in range(TT):
            bank_wait("kiw", t, 0)
            full(tm(PD[t][:, 0:80], 80, (hhi, hlo), 0, u0 % 2, 8, 80, 0, True, True, t), t)
        pe.wait_ge(S("qi_roped"), 1)
        transposes("qi", 8, lambda t, k: qi_tm[:, t, k * P:k * P + P])
        transposes("ki", 1, lambda t, k: kiw[:, t, 0:P])
        transposed("ki", 1)
        for h in range(H1):
            p0 = HD * (h % 2)
            for t in range(1, TT):
                if h:
                    pe.wait_ge(S("idx_relu"), 3 * (h - 1) + t)
                mm(PM[:, t - 1, 0:(t + 1) * P], qit[p0:p0 + HD, h // 2, t * P:t * P + P],
                   kit[p0:p0 + HD, 0:(t + 1) * P], start=True, stop=True).then_inc(S("idx_dots"), 1)
        chunks("qk2", 2, False)
        two_units("v2", 0, 0, 0, 2, False)
        chunks("gates", 3, True)
        pe.wait_ge(S("qk_roped"), 1)
        transposes("qk", 8, lambda t, k: qk_tm[:, t, k * P:k * P + P])
        transposed("qk", 8)

        def logits(n, q, k, bias):
            X = PX[n % 2]
            for t in (3, 2, 0, 1):
                b, c0 = QB_AT[t]
                w = (t + 1) * P
                mm(X[:, b, c0:c0 + w], q(t), k(w), start=t != 0, stop=False, skip_group_check=True)
                bw = bias(t)
                last = mm(X[:, b, c0 + w - bw.shape[1]:c0 + w], identr[:, :], bw, start=False, stop=t != 2,
                          skip_group_check=True)
                if t != 2:
                    last.then_inc(S("att_logits"), 1)

        def turn_probs(n, p):
            X = PX[n % 2]
            pe.wait_ge(S("att_exps"), 4 * n + 4)
            at_block = 0
            for t in (3, 2, 0, 1):
                for j in range(t + 1):
                    last = nc.tensor.transpose(X[:, at_block // 4, (at_block % 4) * P:(at_block % 4) * P + P],
                                               p[n % 2][:, QB_FIRST[t] + j * P:QB_FIRST[t] + j * P + P], ident[:, :])
                    at_block += 1
            last.then_inc(S("att_turned"), 1)

        def values(n, pt, v):
            c0 = 256 * (n % 2)
            pe.wait_ge(S("att_pt"), 2 * n + 2)
            if n >= 2:
                pe.wait_ge(S("att_out"), n - 1)
            for t in range(TT):
                for j in range(t + 1):
                    a = QB_FIRST[t] + j * P
                    last = mm(PM[:, 3, c0 + t * HD:c0 + t * HD + HD], pt[n % 2][:, a:a + P], v(j),
                              start=j == 0, stop=j == t)
            last.then_inc(S("att_pv"), 1)

        pe.wait_ge(S("bias_made"), 3)
        phase_done(pe, "gates")
        for h in range(A_H + 1):
            if h < A_H:
                if h >= 2:
                    pe.wait_ge(S("att_pt"), 2 * (h - 1))
                p0, f = HD * (h % 2), h // 2
                logits(h, lambda t: qkt[p0:p0 + HD, f, t * P:t * P + P], lambda w: qkt[p0:p0 + HD, 4 + f, 0:w],
                       lambda t: bias_q[:, t, 0:(t + 1) * P] if t else mask_q[:, :])
            if h:
                turn_probs(h - 1, pr)
                values(h - 1, prt, lambda j: v2[:, j, (h - 1) * HD:h * HD])
        pe.wait_ge(S("att_out"), A_H)
        transposes("attn", 4, lambda t, k: v2[:, t, k * P:k * P + P])
        transposed("attn", 4)
        pe.wait_ge(S("conv2_done"), 4)
        chunks("wo2", 2, False)
        pe.wait_ge(S("ffn0_made"), TT)
        transposes("ffn0", 8, lambda t, k: xn[:, t, k * P:k * P + P])
        transposed("ffn0", 8)
        mlp("mlp0", 0)

        pe.wait_ge(S("mix1_made"), TT)
        transposes("mix1", 8, lambda t, k: xn[:, t, k * P:k * P + P])
        transposed("mix1", 8)
        two_units("dq", 0, 0, 0, 2, False, Q_RANK)
        two_units("dkv", 0, 0, 0, 2, False, KV_RANK + 32)
        pe.wait_ge(S("cq_made"), TT)
        transposes("cq", 3, lambda t, k: cq[:, t, k * P:k * P + P])
        pe.wait_ge(S("ckv_made"), TT)
        transposes("ckv", 2, lambda t, k: kva[:, t, k * P:k * P + P])
        transposed("ckv", 2)
        u0 = PH["uq"][0]
        for n in range(3):
            unit_wait(u0 + n)
            for t in range(TT):
                bank_wait("uq", t, n)
                full(tm(PD[t], 512, (hhi, hlo), 0, (u0 + n) % 2, 3, 512, 0, True, True, t), t)
        u0 = PH["ukv"][0]
        for n in range(2):
            unit_wait(u0 + n)
            for r in range(2):
                for t in range(TT):
                    bank_wait("ukv", t, 2 * n + r)
                    last = tm(PD[t], 512, (hhi, hlo), 3, (u0 + n) % 2, 2, 1024, 512 * r, True, True, t)
                    if t == 3 and r == 0:
                        last.then_inc(S("bank_full3"), 1)
                    else:
                        full(last, t)
        pe.wait_ge(S("mla_roped"), 1)
        phase_done(pe, "ukv")

        def turn_qk(h, m):
            pe.wait_ge(S("tr_read"), TR["heads"][0] + 2 * h + m)
            for t in range(TT):
                src = k_tm[:, t, h, :] if m else q_tm[:, t, h * C_QK:h * C_QK + C_QK]
                last = nc.tensor.transpose(PDT[0:C_QK, 3, t * P:t * P + P], src, ident[:, :])
            last.then_inc(S("tr_done"), 1)

        turn_qk(0, 0)
        turn_qk(0, 1)
        for h in range(C_H + 1):
            n = A_H + h
            if h < C_H:
                pe.wait_ge(S("att_pt"), 2 * (n - 1))
                pe.wait_ge(S("tr_read"), TR["heads"][0] + 2 * h + 2)
                qh, kh = qth[h % 2], kth[h % 2]
                logits(n, lambda t: qh[0:C_QK, t * P:t * P + P], lambda w: kh[0:C_QK, 0:w], lambda t: mask_q[:, :])
            if h + 1 < C_H:
                turn_qk(h + 1, 0)
            if h:
                turn_probs(n - 1, pr3)
            if h + 1 < C_H:
                turn_qk(h + 1, 1)
            if h:
                values(n - 1, prt3, lambda j: v3[:, j, (h - 1) * HD:h * HD])
        pe.wait_ge(S("att_out"), A_H + C_H)
        transposes("lat", 8, lambda t, k: v3[:, t, k * P:k * P + P])
        transposed("lat", 8)
        chunks("wo3", 2, False)
        pe.wait_ge(S("ffn1_made"), TT)
        transposes("ffn1", 8, lambda t, k: xn[:, t, k * P:k * P + P])
        transposed("ffn1", 8)
        mlp("mlp1", 1)

    @block.scalar
    def _(act):
        def hi(i, base, stride):
            if isinstance(i, int) and i * stride + base >= PH["end"][0]:
                return
            act.wait_ge(S(f"w_loaded{base % 2}"), i * (8 * stride) + 16 * (base // 2 + 1))
            if base >= 2:
                act.wait_ge(S("w_used"), i * stride + (base - 1))
            nc.scalar.activation(whi[base % 2][:, :], wraw[base % 2][:, :], ACT.Copy).then_inc(S("w_hi"), 1)

        def rounds(name, n, dst=None, func=ACT.Copy, scale=1.0, unrolled=False):
            u0 = PH[name][0]

            def body(i):
                hi(i, u0 + 1, 2)
                hi(i, u0 + 2, 2)
                for b in range(4):
                    if dst is not None:
                        full_wait(act, name, b, i, i * 2 + (u0 + 1))
                        nc.scalar.activation(dst(i, b), PD[b], func, scale=scale).then_inc(S(f"bank_free{b}"), 1)
            if unrolled:
                for i in range(n):
                    body(i)
            else:
                loop(act, n, body)

        def split_tiles(name, nk, gain, k0, after):
            act.wait_ge(S("w_used"), PH[after][0])
            for k in range(nk):
                act.wait_ge(S("tr_done"), TR[name][0] + k + 1)
                nc.scalar.activation(hhi[:, k0 + k, :], PM[:, k % 4, :], ACT.Copy, scale=gain(k))\
                    .then_inc(S("tr_hi"), 1)

        def copy_tiles(name, nk, dst, scale=lambda k: 1.0):
            for k in range(nk):
                act.wait_ge(S("tr_done"), TR[name][0] + k + 1)
                nc.scalar.activation(dst(k), PM[:, k % 4, :], ACT.Copy, scale=scale(k)).then_inc(S("tr_read"), 1)

        def squares(s, src, sem, need, d=DM):
            for t in range(TT):
                if sem is not None:
                    act.wait_ge(S(sem), need(t))
                if t or s:
                    act.wait_ge(S("squares"), TT * s + t - 1)
                nc.scalar.activation(junk[:, t % 2, 0:d], src(t), ACT.Square, accum_out=stat[:, s, t:t + 1])\
                    .then_inc(S("squares"), 1)

        def mlp(name, layer):
            u0 = PH[name][0]

            def up(first, r, i, m):
                hi(i, u0 + first + 1, 8)
                hi(i, u0 + first + 2, 8)
                base = m * 4 + 32 * layer

                def relu(b):
                    full_wait(act, name, b, r, i * 8 + (u0 + first + 1))
                    if b >= 2:
                        act.wait_ge(S("hidden_ready"), base + (b - 1))
                    nc.scalar.activation(mh_r[:, b % 2, :], PD[b], ACT.Relu).then_inc(S(f"bank_free{b}"), 1)

                def part(b):
                    act.wait_ge(S("hidden_sq"), base + (b + 1))
                    nc.scalar.activation(mh_hi[MPAR[first]][:, b, :], mh_r[:, b % 2, :], ACT.Copy)\
                        .then_inc(S("hidden_hi"), 1)
                if not (isinstance(m, int) and m == 0):
                    act.wait_ge(S("hidden_ready"), base)
                relu(0)
                relu(1)
                part(0)
                relu(2)
                part(1)
                relu(3)
                part(2)
                part(3)

            def down(first, i):
                hi(i, u0 + first + 1, 8)
                hi(i, u0 + first + 2, 8)

            MPAR = {0: 0, 2: 1, 6: 0}
            up(0, 0, 0, 0)
            with act.Fori(0, 3) as i:
                up(2, i * 6 + 1, i, i * 2 + 1)
                down(4, i)
                up(6, i * 6 + 4, i, i * 2 + 2)
                down(8, i)
            up(2, 19, 3, 7)
            down(4, 3)
            down(6, 3)

        hi(0, 0, 0)
        act.wait_ge(S("tr_done"), 1)
        nc.scalar.activation(cact[:, :], PM[:, 3, 0:8], ACT.Silu).then_inc(S("tr_read"), 1)
        act.wait_ge(S("tr_read"), 1)
        nc.scalar.activation(chi[:, :, :], cact[:, :].unsqueeze(2).to_broadcast([P, KT, P]), ACT.Copy)\
            .then_inc(S("c_hi"), 1)
        act.wait_ge(S("x_loaded"), 16)
        squares(0, lambda t: xres[:, t, :], None, None)
        for u in range(1, 9):
            hi(0, u, 0)
        act.wait_ge(S("angles"), 1)
        nc.scalar.activation(sinall[:, :, :], ang[:, :, :], ACT.Sin).then_inc(S("sines"), 1)
        nc.scalar.activation(ang_s[:, :, :], ang[:, :, :], ACT.Sin, scale=0.5).then_inc(S("sines"), 1)
        for u in range(1, 5):
            hi(0, PH["ada_g"][0] + u, 0)
        split_tiles("h", 8, lambda k: 1.0, 0, "ada_ss")
        rounds("q", 2, lambda i, b: dyn(qt, i, b), scale=HD ** -0.5)
        rounds("k", 2, lambda i, b: dyn(kt, i, b))
        rounds("v", 2, lambda i, b: vo[:, b, bass.ds(i * 512, 512)])

        def sb_head(h):
            for n in range(3):
                a = slice(SB_FIRST[n], SB_FIRST[n] + SB_WIDE[n])
                act.wait_ge(S("sb_clamped"), 3 * h + n + 1)
                nc.scalar.activation(sb_l[:, a], sb_l[:, a], ACT.Exp).then_inc(S("sb_exp"), 1)
                act.wait_ge(S("sb_exp"), 3 * h + n + 1)
                nc.scalar.activation(sb_l[:, a], sb_l[:, a], ACT.Ln, bias=1.0).then_inc(S("sb_ln"), 1)
            if h:
                act.wait_ge(S("sb_tail"), 3 * h)
            for n in range(3):
                a = slice(SB_FIRST[n], SB_FIRST[n] + SB_WIDE[n])
                act.wait_ge(S("sb_softplus"), 3 * h + n + 1)
                nc.scalar.activation(sb_hi[:, a], sb_l[:, a], ACT.Copy).then_inc(S("sb_high"), 1)
            after_piece(*SB_PIECES[3 * h])
            after_piece(*SB_PIECES[3 * h + 1])
            if h:
                act.wait_ge(S("sb_pv"), h)
            for n in range(3):
                a = slice(SB_FIRST[n], SB_FIRST[n] + SB_WIDE[n])
                act.wait_ge(S("sb_tail"), 3 * h + n + 1)
                nc.scalar.activation(sb_w[:, a], PM[:, n, 0:SB_WIDE[n]], ACT.Exp).then_inc(S("sb_weights"), 1)
            after_piece(*SB_PIECES[3 * h + 2])

        def after_piece(name, r, h, b):
            u = PH[name][0] + 2 * r + h
            if (b == 3 or name == "dt") and (name, r, h) not in (("wout_a", 1, 1), ("z_attn", 0, 1)):
                hi(0, u + 2, 0)
            if h == 1 and name != "z_attn":
                full_wait(act, name, b, r, u)
                if name == "xbc":
                    dst = xbc[:, 4 * r + b, 3:SEQ + 3]
                else:
                    dst = (zs if name == "z_ssm" else mix)[:, b, 512 * r:512 * r + 512]
                nc.scalar.activation(dst, PD[b], ACT.Copy).then_inc(S(f"bank_free{b}"), 1)

        hi(0, PH["xbc"][0] + 1, 0)
        nc.scalar.preload_act_table_set("natural_log_exp_and_others")
        for h in range(H1):
            sb_head(h)
        act.wait_ge(S("dt_clamped"), 1)
        nc.scalar.activation(dts[:, 0, :], dts[:, 0, :], ACT.Exp).then_inc(S("dt_exp"), 1)
        nc.scalar.activation(small[:, 16:32], small[:, 16:32], ACT.Exp).then_inc(S("dt_exp"), 1)
        act.wait_ge(S("dt_exp"), 2)
        nc.scalar.activation(dts[:, 0, :], dts[:, 0, :], ACT.Ln, bias=1.0).then_inc(S("dt_ln"), 1)
        act.wait_ge(S("sb_tail"), 3 * H1)

        def gate_round(i):
            for b in range(4):
                full_wait(act, "z_attn", b, i, PH["z_attn"][0] + 2 * i + 1)
                nc.scalar.activation(za[:, b, 512 * i:512 * i + 512], PD[b], ACT.Copy).then_inc(S(f"bank_free{b}"), 1)

        def scan_inputs(first, end):
            for ct in range(first, end):
                act.wait_ge(S("conv_sum"), ct + 1)
                nc.scalar.activation(xbc[:, ct, 0:SEQ], xbc[:, ct, 0:SEQ], ACT.Silu).then_inc(S("conv_done"), 1)

        gate_round(0)
        hi(0, PH["z_attn"][0] + 3, 0)
        scan_inputs(0, 8)
        hi(0, PH["wout_a"][0], 0)
        squares(1, lambda t: vo[:, t, :], "sb_out", lambda t: H1)
        scan_inputs(8, XBC_T)
        phase_done(act, "z_ssm")
        for t in range(TT):
            nc.scalar.activation(zs[:, t, :], zs[:, t, :], ACT.Silu).then_inc(S("zs_silu"), 1)
        gate_round(1)
        hi(0, PH["wout_a"][0] + 1, 0)
        phase_done(act, "z_attn")
        for t in range(TT):
            nc.scalar.activation(za[:, t, :], za[:, t, :], ACT.Silu).then_inc(S("za_silu"), 1)
        copy_tiles("scan", 10, lambda k: yt[:, :, k * P:k * P + P] if k < 8 else b_tm[:, :, (k - 8) * P:(k - 7) * P])
        act.wait_ge(S("scan_cum"), 1)
        nc.scalar.activation(dts[:, 2:5, :], PM[:, 3, 0:192].rearrange("p (a b) -> p a b", a=3), ACT.Exp)\
            .then_inc(S("scan_exps"), 1)
        split_tiles("y_attn", 8, lambda k: col_a[:, C_SBG + k:C_SBG + k + 1], 0, "wout_a")
        for n in range(2 * TT):
            act.wait_ge(S("scan_seg"), n + 1)
            if n >= 2:
                act.wait_ge(S("scan_diag"), n - 1)
            nc.scalar.activation(dec[n % 2][:, :, :].rearrange("p h l -> p (h l)"),
                                 PM[:, 0:2, :].rearrange("p a b -> p (a b)"), ACT.Exp).then_inc(S("scan_dec"), 1)
            for p in step_pieces(n):
                after_piece(*p)
        for p in SCAN_PIECES[3 * TT:]:
            after_piece(*p)
        squares(2, lambda t: yt[:, t, :], "y_gated", lambda t: t + 1)
        split_tiles("y_ssm", 8, lambda k: col_a[:, C_SSG + k:C_SSG + k + 1], 0, "wout_s")
        rounds("wout_s", 2)
        squares(3, lambda t: xres[:, t, :], "x2_made", lambda t: t + 1)
        squares(4, lambda t: xres[:, t, :], "first_out", lambda t: t + 1)
        split_tiles("mix0", 8, lambda k: col_a[:, C_MIX + k:C_MIX + k + 1], 0, "qi")
        rounds("qi", 2, lambda i, b: qi_tm[:, b, bass.ds(i * 512, 512)])
        hi(0, PH["kiw"][0] + 1, 0)
        copy_tiles("qi", 8, lambda k: qit[:, k, :])
        copy_tiles("ki", 1, lambda k: kit[:, :])
        for h in range(H1):
            if h >= 2:
                act.wait_ge(S("idx_sum"), 3 * (h - 1))
            for t in range(1, TT):
                act.wait_ge(S("idx_dots"), 3 * h + t)
                nc.scalar.activation(relu_s[:, h % 2, IDX_AT[t]:IDX_AT[t] + (t + 1) * P], PM[:, t - 1, 0:(t + 1) * P],
                                     ACT.Relu).then_inc(S("idx_relu"), 1)
        rounds("qk2", 2, lambda i, b: qk_tm[:, b, bass.ds(i * 512, 512)])
        rounds("v2", 1, lambda i, b: v2[:, b, :])
        act.wait_ge(S("idx_sum"), 3 * H1)
        rounds("gates", 3, lambda i, b: [gb[:, b, :], gc[:, b, 2:SEQ + 2], xi[:, b, :]][i], unrolled=True)
        copy_tiles("qk", 8, lambda k: qkt[:, k, :], lambda k: HD ** -0.5 if k < 4 else 1.0)
        act.wait_ge(S("w_used"), PH["wo2"][0])
        for f in range(4):
            act.wait_ge(S("conv2_out"), f + 1)
            nc.scalar.activation(hhi[:, 4 + f, :], ca[:, f, :], ACT.Copy).then_inc(S("conv2_hi"), 1)

        def exps(n, p, m, d):
            s = n % 2
            if n >= 2:
                act.wait_ge(S("att_out"), n - 1)
            for q, t in enumerate((3, 2, 0, 1)):
                b, c0 = QB_AT[t]
                w = (t + 1) * P
                act.wait_ge(S("att_max"), 4 * n + (1, 3, 3, 4)[q])
                nc.scalar.activation(p[s][:, QB_FIRST[t]:QB_FIRST[t] + w], PX[s][:, b, c0:c0 + w], ACT.Exp,
                                     bias=m[:, s, t:t + 1], accum_out=d[:, s, t:t + 1]).then_inc(S("att_exps"), 1)

        def turned(n, pt):
            act.wait_ge(S("att_turned"), n + 1)
            if n >= 2:
                act.wait_ge(S("att_pv"), n - 1)
            nc.scalar.activation(pt[n % 2][:, 0:SEQ], PX[n % 2][:, 0, :], ACT.Copy).then_inc(S("att_pt"), 1)

        for h in range(A_H + 1):
            if h:
                turned(h - 1, prt)
            if h < A_H:
                exps(h, pr, mx, den)
        split_tiles("attn", 4, lambda k: 1.0, 0, "wo2")
        rounds("wo2", 2, lambda i, b: mix2[:, b, bass.ds(i * 512, 512)])
        phase_done(act, "wo2")
        squares(5, lambda t: mix2[:, t, :], None, None)
        squares(6, lambda t: xres[:, t, :], "post_mix0", lambda t: t + 1)
        split_tiles("ffn0", 8, lambda k: col_a[:, C_FFN + k:C_FFN + k + 1], 0, "mlp0")
        mlp("mlp0", 0)
        phase_done(act, "mlp0")
        squares(7, lambda t: mixm[:, t, :], None, None)
        squares(8, lambda t: xres[:, t, :], "post_ffn0", lambda t: t + 1)
        split_tiles("mix1", 8, lambda k: col_a[:, C_MIX + 8 + k:C_MIX + 9 + k], 0, "dq")
        for name, dst, n in (("dq", cq, Q_RANK), ("dkv", kva, KV_RANK + 32)):
            u0 = PH[name][0]
            hi(0, u0 + 1, 0)
            hi(0, u0 + 2, 0)
            for b in range(4):
                full_wait(act, name, b, 0, u0 + 1)
                nc.scalar.activation(dst[:, b, :], PD[b][:, 0:n], ACT.Copy).then_inc(S(f"bank_free{b}"), 1)
        phase_done(act, "dkv")
        squares(9, lambda t: cq[:, t, :], None, None, Q_RANK)
        squares(10, lambda t: kva[:, t, 0:KV_RANK], None, None, KV_RANK)
        split_tiles("cq", 3, lambda k: col_b[:, C_QN + k:C_QN + k + 1], 0, "uq")
        split_tiles("ckv", 2, lambda k: col_b[:, C_KN + k:C_KN + k + 1], 3, "uq")
        u0 = PH["uq"][0]
        for n in range(3):
            hi(0, u0 + n + 1, 0)
            for t in range(TT):
                full_wait(act, "uq", t, n, u0 + n)
                nc.scalar.activation(q_tm[:, t, 512 * n:512 * n + 512], PD[t], ACT.Copy)\
                    .then_inc(S(f"bank_free{t}"), 1)
        u0 = PH["ukv"][0]
        hi(0, u0 + 1, 0)
        hi(0, u0 + 2, 0)

        def turned_q(h):
            act.wait_ge(S("tr_done"), TR["heads"][0] + 2 * h + 1)
            nc.scalar.activation(qth[h % 2][0:C_QK, :], PDT[0:C_QK, 3, :], ACT.Copy, scale=C_QK ** -0.5)\
                .then_inc(S("tr_read"), 1)

        turned_q(0)
        for h in range(C_H + 1):
            if h + 1 < C_H:
                turned_q(h + 1)
            if h:
                turned(A_H + h - 1, prt3)
            if h < C_H:
                exps(A_H + h, pr3, mx3, den3)
        split_tiles("lat", 8, lambda k: 1.0, 0, "wo3")
        rounds("wo3", 2, lambda i, b: mix3[:, b, bass.ds(i * 512, 512)])
        phase_done(act, "wo3")
        squares(11, lambda t: mix3[:, t, :], None, None)
        squares(12, lambda t: xres[:, t, :], "post_mix1", lambda t: t + 1)
        split_tiles("ffn1", 8, lambda k: col_a[:, C_FFN + 8 + k:C_FFN + 9 + k], 0, "mlp1")
        mlp("mlp1", 1)
        phase_done(act, "mlp1")
        squares(13, lambda t: mixm[:, t, :], None, None)

    @block.gpsimd
    def _(pool):
        g = nc.gpsimd

        def lo(i, base, stride):
            if base >= PH["end"][0]:
                return
            pool.wait_ge(S("w_hi"), i * stride + (base + 1))
            g.tensor_tensor(wlo[base % 2][:, :], wraw[base % 2][:, :], fl(whi[base % 2][:, :]), ALU.subtract)\
                .then_inc(S("w_split"), 1)

        def units(name, to):
            for u in range(PH[name][0] + 1, PH[to][0] + 1):
                lo(0, u, 0)

        def pairs(name, n):
            u0 = PH[name][0]

            def body(i):
                lo(i, u0 + 1, 2)
                lo(i, u0 + 2, 2)
            loop(pool, n, body)

        def rsqrt(s, n=1):
            for m in range(s, s + n):
                pool.wait_ge(S("mean_sq"), m + 1)
                g.tensor_tensor(rstd[:, m, :], stat[:, m, :], mhalf[:, :], ALU.pow).then_inc(S("rstd_done"), 1)

        g.memset(ident[:, :], 0.0).then_inc(S("filled"), 1)
        g.memset(ones[:, :], 1.0).then_inc(S("filled"), 1)
        g.memset(scratch[:, :], 0.0).then_inc(S("filled"), 1)
        g.memset(scratch1[:, :], -1.0).then_inc(S("filled"), 1)
        g.memset(mhalf[:, :], -0.5).then_inc(S("filled"), 1)
        pool.wait_ge(S("filled"), 5)
        g.affine_select(out=ident[:, :], in_=ident[:, :], compare_op=ALU.not_equal, fill=1.0, base=0,
                        pattern=[[-1, P]], channel_multiplier=1).then_inc(S("masks"), 1)
        lo(0, 0, 0)
        g.affine_select(out=identr[:, :], in_=scratch[:, :], compare_op=ALU.not_equal, fill=1.0, base=0,
                        pattern=[[-1, P]], channel_multiplier=1)
        g.affine_select(out=tri_le[:, :], in_=ones[:, :], compare_op=ALU.is_ge, fill=0.0, base=0,
                        pattern=[[1, P]], channel_multiplier=-1)
        g.affine_select(out=tri_gt[:, :], in_=ones[:, :], compare_op=ALU.is_gt, fill=0.0, base=0,
                        pattern=[[-1, P]], channel_multiplier=1)
        g.affine_select(out=neg_ge[:, :], in_=scratch1[:, :], compare_op=ALU.is_ge, fill=0.0, base=0,
                        pattern=[[-1, P]], channel_multiplier=1)
        g.affine_select(out=mask_t[:, :], in_=scratch[:, :], compare_op=ALU.is_gt, fill=NEG, base=0,
                        pattern=[[1, P]], channel_multiplier=-1)
        g.affine_select(out=mask_q[:, :], in_=scratch[:, :], compare_op=ALU.is_ge, fill=NEG, base=0,
                        pattern=[[-1, P]], channel_multiplier=1)
        g.tensor_copy(neg_one[:, :], scratch1[:, :]).then_inc(S("masks"), 1)
        for j in range(8):
            g.memset(freq[:, j:j + 1], THETA ** (-2.0 * j / 16))
        for j in range(16):
            g.memset(freq[:, 8 + j:9 + j], THETA ** (-2.0 * j / 32)).then_inc(S("freqs"), 1)
        lo(0, 1, 0)
        lo(0, 2, 0)
        rsqrt(0)
        for u in range(3, 9):
            lo(0, u, 0)
        units("ada_g", "q")
        pairs("q", 2)
        pairs("k", 2)
        pairs("v", 2)
        g.memset(xbc[:, :, 0:3], 0.0).then_inc(S("pads"), 1)
        pairs("xbc", 3)
        pairs("z_ssm", 2)
        lo(0, PH["dt"][0] + 1, 0)
        pairs("z_attn", 2)
        rsqrt(1)
        pairs("wout_a", 2)
        rsqrt(2)
        pairs("wout_s", 2)
        rsqrt(3, 2)
        pairs("qi", 2)
        lo(0, PH["kiw"][0] + 1, 0)
        for t in range(1, TT):
            pool.wait_ge(S("idx_sum"), 3 * H1)
            g.affine_select(out=score[:, t, t * P:t * P + P], in_=score[:, t, t * P:t * P + P], compare_op=ALU.is_ge,
                            fill=DROPPED, base=0, pattern=[[-1, P]], channel_multiplier=1)\
                .then_inc(S("score_masked"), 1)
        pairs("qk2", 2)
        pairs("v2", 1)
        g.memset(gc[:, :, 0:2], 0.0).then_inc(S("pads"), 1)
        pairs("gates", 3)
        pairs("wo2", 2)
        rsqrt(5, 2)

        def mlp(name, layer):
            u0 = PH[name][0]
            pool.wait_ge(S(f"post_mix{layer}"), TT)
            g.memset(mixm[:, :, :], 0.0).then_inc(S("acc_zero"), 1)
            for u in (1, 2):
                lo(0, u0 + u, 0)
            with pool.Fori(0, 3) as i:
                for u in range(3, 11):
                    lo(i, u0 + u, 8)
            for u in range(27, 33):
                lo(0, u0 + u, 0)

        mlp("mlp0", 0)
        rsqrt(7, 2)
        units("dq", "uq")
        rsqrt(9, 2)
        units("uq", "wo3")
        pairs("wo3", 2)
        rsqrt(11, 2)
        mlp("mlp1", 1)
        rsqrt(13)

    @block.vector
    def _(dve):
        v = nc.vector
        chained = [0]

        def link(ins):
            chained[0] += 1
            ins.then_inc(S("dve_chain"), 1)
            dve.wait_ge(S("dve_chain"), chained[0])

        def split_tiles(name, nk, gain, k0):
            for k in range(nk):
                dve.wait_ge(S("tr_hi"), TR[name][1] + k + 1)
                v.scalar_tensor_tensor(out=hlo[:, k0 + k, :], in0=PM[:, k % 4, :], scalar=gain(k),
                                       in1=fl(hhi[:, k0 + k, :]), op0=ALU.mult, op1=ALU.subtract)\
                    .then_inc(S("tr_read"), 1)

        def mean_square(s, d=DM):
            dve.wait_ge(S("squares"), TT * (s + 1))
            v.tensor_scalar(stat[:, s, :], stat[:, s, :], 1.0 / d, EPS, ALU.mult, ALU.add).then_inc(S("mean_sq"), 1)
            dve.wait_ge(S("rstd_done"), s + 1)

        def rope(view, heads, half, c, s, tmp):
            n = TT * heads * half
            shape = [P, TT, heads, half]
            cb = c[:, :, :].unsqueeze(2).to_broadcast(shape)
            sb = s[:, :, :].unsqueeze(2).to_broadcast(shape)
            x1, x2 = view[:, :, :, 0:half], view[:, :, :, half:2 * half]
            t = [tmp[:, j, 0:n].rearrange("p (a h d) -> p a h d", a=TT, h=heads) for j in range(4)]
            v.tensor_tensor(t[0], x1, cb, ALU.mult)
            v.tensor_tensor(t[1], x2, sb, ALU.mult)
            v.tensor_tensor(t[2], x2, cb, ALU.mult)
            link(v.tensor_tensor(t[3], x1, sb, ALU.mult))
            v.tensor_tensor(x1, t[0], t[1], ALU.subtract)
            link(v.tensor_tensor(x2, t[2], t[3], ALU.add))

        dve.wait_ge(S("c_hi"), 1)
        v.tensor_tensor(clo[:, :, :], cact[:, :].unsqueeze(2).to_broadcast([P, KT, P]), fl(chi[:, :, :]),
                        ALU.subtract).then_inc(S("c_split"), 1)
        dve.wait_ge(S("tr_done"), 2)
        v.tensor_copy(col_a[:, 0:ROWS_A], PM[:, 2, 0:ROWS_A])
        v.tensor_copy(col_b[:, 0:ROWS_B], PM[:, 2, P:P + ROWS_B]).then_inc(S("tr_read"), 1)
        dve.wait_ge(S("params"), 16 * N_PARAMS)
        dve.wait_ge(S("freqs"), 16)
        link(v.tensor_copy(pos_f[:, :], pos_i[:, :]))
        link(v.tensor_tensor(ang[:, :, :], pos_f[:, :].unsqueeze(2).to_broadcast([P, TT, 24]),
                             freq[:, :].unsqueeze(1).to_broadcast([P, TT, 24]), ALU.mult))
        link(v.tensor_scalar(ang_n[:, :, :], ang[:, :, :], 1.0 / (2 * math.pi), ROUNDER, ALU.mult, ALU.add))
        link(v.tensor_scalar(ang_n[:, :, :], ang_n[:, :, :], -ROUNDER, None, ALU.add))
        for part in TWO_PI:
            link(v.scalar_tensor_tensor(out=ang[:, :, :], in0=ang_n[:, :, :], scalar=-part, in1=ang[:, :, :],
                                        op0=ALU.mult, op1=ALU.add))
        v.tensor_scalar(ang[:, :, :], ang[:, :, :], PI_BELOW, -PI_BELOW, ALU.min, ALU.max).then_inc(S("angles"), 1)
        mean_square(0)
        for j, c0 in enumerate((DM, DM + 512, 0, 512)):
            full_unit = PH["ada_ss"][0] + 2 * j + 2
            dve.wait_ge(S("w_used"), full_unit)
            v.tensor_tensor(mod[:, c0:c0 + 512], PD[j], b_row[:, c0:c0 + 512], ALU.add).then_inc(S(f"bank_free{j}"), 1)
            if j < 2:
                dve.wait_ge(S(f"bank_free{j}"), 1)
                v.scalar_tensor_tensor(out=mod[:, c0:c0 + 512], in0=mod[:, c0:c0 + 512], scalar=1.0,
                                       in1=row_a[:, c0 - DM:c0 - DM + 512], op0=ALU.add, op1=ALU.mult)
        dve.wait_ge(S("sines"), 2)
        link(v.tensor_tensor(ang_s[:, :, :], ang_s[:, :, :], ang_s[:, :, :], ALU.mult))
        v.tensor_scalar(cosq[:, :, :], ang_s[:, :, 0:8], -2.0, 1.0, ALU.mult, ALU.add)
        v.tensor_scalar(cosm[:, :, :], ang_s[:, :, 8:24], -2.0, 1.0, ALU.mult, ALU.add)
        v.tensor_copy(sinq[:, :, :], sinall[:, :, 0:8])
        link(v.tensor_copy(sinm[:, :, :], sinall[:, :, 8:24]))
        for t in range(TT):
            v.scalar_tensor_tensor(out=xn[:, t, :], in0=xres[:, t, :], scalar=rstd[:, 0, t:t + 1],
                                   in1=mod[:, DM:2 * DM], op0=ALU.mult, op1=ALU.mult).then_inc(S("h_scaled"), 1)
        for t in range(TT):
            dve.wait_ge(S("h_scaled"), t + 1)
            v.tensor_tensor(xn[:, t, :], xn[:, t, :], mod[:, 0:DM], ALU.add).then_inc(S("h_made"), 1)
        for j in range(2):
            dve.wait_ge(S("w_used"), PH["ada_g"][0] + 2 * j + 2)
            v.tensor_tensor(gate[:, 512 * j:512 * j + 512], PD[j], row_b[:, 512 * j:512 * j + 512], ALU.add)\
                .then_inc(S(f"bank_free{j}"), 1)
        split_tiles("h", 8, lambda k: 1.0, 0)

        def sb_emit(h):
            dve.wait_ge(S("sb_pv"), h + 1)
            v.tensor_copy(vo[:, :, h * HD:h * HD + HD],
                          PM[:, 3, (h % 2) * 256:(h % 2) * 256 + 256].rearrange("p (t d) -> p t d", t=TT))\
                .then_inc(S("sb_out"), 1)

        rows4 = [P, TT, H1]

        def dt_raw():
            dve.wait_ge(S("w_used"), PH["dt"][0] + 1)
            v.tensor_tensor(dts[:, 5, :].rearrange("p (t h) -> p t h", t=TT),
                            PD[0][:, 0:64].rearrange("p (t h) -> p t h", t=TT),
                            small[:, 0:16].unsqueeze(1).to_broadcast(rows4), ALU.add).then_inc(S("bank_free0"), 1)
            dve.wait_ge(S("bank_free0"), PH["z_attn"][1][0])
            v.tensor_scalar(dts[:, 0, :], dts[:, 5, :], CLAMP, None, ALU.min).then_inc(S("dt_clamped"), 1)

        def convolution(ct):
            acc = conv_acc[:, ct % 2, :]
            dve.wait_ge(S(f"bank_free{ct % 4}"), PH["xbc"][1][ct % 4] + ct // 4 + 1)
            if ct == 0:
                dve.wait_ge(S("pads"), 1)
            if ct >= 2:
                dve.wait_ge(S("conv_sum"), ct - 1)
            col = [col_a[:, C_CW + 12 * j + ct:C_CW + 12 * j + ct + 1] for j in range(4)]
            link(v.tensor_scalar(acc, xbc[:, ct, 0:SEQ], col[0], col_a[:, C_CB + ct:C_CB + ct + 1], ALU.mult, ALU.add))
            for j in range(1, 3):
                link(v.scalar_tensor_tensor(out=acc, in0=xbc[:, ct, j:j + SEQ], scalar=col[j], in1=acc,
                                            op0=ALU.mult, op1=ALU.add))
            v.scalar_tensor_tensor(out=xbc[:, ct, 0:SEQ], in0=xbc[:, ct, 3:3 + SEQ], scalar=col[3], in1=acc,
                                   op0=ALU.mult, op1=ALU.add).then_inc(S("conv_sum"), 1)

        dt_at = SB_PIECES.index(("dt", 0, 0, 0))
        for h in range(H1):
            for n in range(3):
                a = slice(SB_FIRST[n], SB_FIRST[n] + SB_WIDE[n])
                dve.wait_ge(S("sb_z"), 3 * h + n + 1)
                if h:
                    dve.wait_ge(S("sb_split"), 3 * (h - 1) + n + 1)
                v.tensor_scalar(sb_l[:, a], PM[:, n, 0:SB_WIDE[n]], CLAMP, None, ALU.min).then_inc(S("sb_clamped"), 1)
            if h:
                sb_emit(h - 1)
            if h == dt_at // 3:
                dt_raw()
            for n in range(3):
                a = slice(SB_FIRST[n], SB_FIRST[n] + SB_WIDE[n])
                dve.wait_ge(S("sb_ln"), 3 * h + n + 1)
                v.tensor_tensor(sb_l[:, a], PM[:, n, 0:SB_WIDE[n]], sb_l[:, a], ALU.max).then_inc(S("sb_softplus"), 1)
            for n in range(3):
                a = slice(SB_FIRST[n], SB_FIRST[n] + SB_WIDE[n])
                dve.wait_ge(S("sb_high"), 3 * h + n + 1)
                v.tensor_tensor(sb_lo[:, a], sb_l[:, a], fl(sb_hi[:, a]), ALU.subtract).then_inc(S("sb_split"), 1)
            if 3 <= h < 3 + XBC_T:
                convolution(h - 3)
        sb_emit(H1 - 1)
        dve.wait_ge(S("dt_ln"), 1)
        link(v.tensor_tensor(dts[:, 0, :], dts[:, 5, :], dts[:, 0, :], ALU.max))
        v.scalar_tensor_tensor(out=dts[:, 1, :].rearrange("p (t h) -> p t h", t=TT),
                               in0=dts[:, 0, :].rearrange("p (t h) -> p t h", t=TT), scalar=-1.0,
                               in1=small[:, 16:32].unsqueeze(1).to_broadcast(rows4), op0=ALU.mult, op1=ALU.mult)\
            .then_inc(S("ld_made"), 1)
        mean_square(1)
        dve.wait_ge(S("scan_cb"), 1)
        for g in range(GROUPS):
            op = v.tensor_tensor(cbm[:, 4 * g:4 * g + 4, :], PM[:, g, :].rearrange("p (t l) -> p t l", t=TT),
                                 tri_le[:, :].unsqueeze(1).to_broadcast([P, TT, P]), ALU.mult)
        op.then_inc(S("cbm_made"), 1)
        for t in range(TT):
            dve.wait_ge(S("za_silu"), t + 1)
            v.scalar_tensor_tensor(out=vo[:, t, :], in0=vo[:, t, :], scalar=rstd[:, 1, t:t + 1], in1=za[:, t, :],
                                   op0=ALU.mult, op1=ALU.mult).then_inc(S("y_attn_made"), 1)

        def per_head(row, t, g, n=HG):
            a = t * H1 + g * HG
            return dts[:, row, a:a + n].unsqueeze(2).to_broadcast([P, n, HD])

        def heads(ap):
            return ap.rearrange("p (h d) -> p h d", d=HD)

        def log_decays(t):
            v.tensor_tensor(ldm[:, :, :], tri_gt[:, :].unsqueeze(1).to_broadcast([P, H1, P]),
                            dts[:, 1, t * H1:t * H1 + H1].unsqueeze(2).to_broadcast([P, H1, P]), ALU.mult)\
                .then_inc(S("ldm_made"), 1)

        log_decays(0)
        split_tiles("y_attn", 8, lambda k: col_a[:, C_SBG + k:C_SBG + k + 1], 0)
        dve.wait_ge(S("cbm_made"), 1)
        dve.wait_ge(S("scan_exps"), 1)
        dve.wait_ge(S("zs_silu"), TT)
        for t in range(TT):
            if t:
                dve.wait_ge(S("scan_diag"), 2 * t)
                dve.wait_ge(S("xdte_made"), t)
            link(v.tensor_tensor(heads(xdt[:, :]), heads(yt[:, t, :]), per_head(0, t, 0, H1), ALU.mult))
            if t < TT - 1:
                if t:
                    dve.wait_ge(S("scan_st"), 2 * t)
                v.tensor_tensor(heads(xdte[:, :]), heads(xdt[:, :]), per_head(3, t, 0, H1), ALU.mult)\
                    .then_inc(S("xdte_made"), 1)
            for g in range(GROUPS):
                n = 2 * t + g
                cols = slice(g * 512, g * 512 + 512)
                dve.wait_ge(S("scan_dec"), n + 1)
                v.tensor_tensor(dec[g][:, :, :], dec[g][:, :, :],
                                cbm[:, 4 * g + t, :].unsqueeze(1).to_broadcast([P, HG, P]), ALU.mult)\
                    .then_inc(S("scan_m"), 1)
                if g and t < TT - 1:
                    log_decays(t + 1)
                if n:
                    dve.wait_ge(S("scan_y"), n)
                link(v.tensor_tensor(heads(xd[:, :]), heads(yt[:, t, cols]),
                                     small[:, 32 + g * HG:32 + g * HG + HG].unsqueeze(2).to_broadcast([P, HG, HD]),
                                     ALU.mult))
                if t:
                    dve.wait_ge(S("scan_off"), n - 1)
                    v.tensor_tensor(heads(off[:, :]), heads(PM[:, 3, :]), per_head(2, t, g), ALU.mult)\
                        .then_inc(S("off_read"), 1)
                    dve.wait_ge(S("off_read"), n - 1)
                    link(v.tensor_tensor(xd[:, :], xd[:, :], off[:, :], ALU.add))
                dve.wait_ge(S("scan_diag"), n + 1)
                v.tensor_tensor(yt[:, t, cols], PM[:, 2, :], xd[:, :], ALU.add).then_inc(S("scan_y"), 1)
                if t < TT - 1:
                    if t:
                        link(v.tensor_tensor(heads(hst[:, cols]), heads(hst[:, cols]), per_head(4, t, g), ALU.mult))
                    dve.wait_ge(S("scan_st"), n + 1)
                    if t:
                        v.tensor_tensor(hst[:, cols], hst[:, cols], PM[:, 3, :], ALU.add).then_inc(S("hst_made"), 1)
                    else:
                        v.tensor_copy(hst[:, cols], PM[:, 3, :]).then_inc(S("hst_made"), 1)
            dve.wait_ge(S("scan_y"), 2 * t + 2)
            v.tensor_tensor(yt[:, t, :], yt[:, t, :], zs[:, t, :], ALU.mult).then_inc(S("y_gated"), 1)
        mean_square(2)
        for t in range(TT):
            v.tensor_scalar(yt[:, t, :], yt[:, t, :], rstd[:, 2, t:t + 1], None, ALU.mult).then_inc(S("y_ssm_made"), 1)
        split_tiles("y_ssm", 8, lambda k: col_a[:, C_SSG + k:C_SSG + k + 1], 0)
        u0 = PH["wout_s"][0]

        def add_mix(i):
            for b in range(4):
                full_wait(dve, "wout_s", b, i, i * 2 + (u0 + 1))
                m = mix[:, b, bass.ds(i * 512, 512)]
                v.tensor_tensor(m, PD[b], m, ALU.add).then_inc(S(f"bank_free{b}"), 1)
        loop(dve, 2, add_mix)
        phase_done(dve, "wout_s")
        dve.wait_ge(S("x_again"), 16)
        for t in range(TT):
            link(v.tensor_tensor(mix[:, t, :], mix[:, t, :], gate[:, :], ALU.mult))
            v.tensor_tensor(xres[:, t, :], xres[:, t, :], mix[:, t, :], ALU.add).then_inc(S("x2_made"), 1)
        mean_square(3)
        dve.wait_ge(S("row_f"), 16)
        for t in range(TT):
            v.scalar_tensor_tensor(out=xres[:, t, :], in0=xres[:, t, :], scalar=rstd[:, 3, t:t + 1], in1=row_a[:, :],
                                   op0=ALU.mult, op1=ALU.mult).then_inc(S("first_out"), 1)

        def normed(s, sem):
            mean_square(s)
            for t in range(TT):
                v.tensor_scalar(xn[:, t, :], xres[:, t, :], rstd[:, s, t:t + 1], None, ALU.mult).then_inc(S(sem), 1)

        def post_norm(s, m, row, sem):
            mean_square(s)
            for t in range(TT):
                link(v.scalar_tensor_tensor(out=m[:, t, :], in0=m[:, t, :], scalar=rstd[:, s, t:t + 1], in1=row[:, :],
                                            op0=ALU.mult, op1=ALU.mult))
                v.tensor_tensor(xres[:, t, :], xres[:, t, :], m[:, t, :], ALU.add).then_inc(S(sem), 1)

        normed(4, "mix0_made")
        split_tiles("mix0", 8, lambda k: col_a[:, C_MIX + k:C_MIX + k + 1], 0)

        for t in range(TT):
            full_wait(dve, "kiw", t, 0, PH["kiw"][0])
            v.tensor_copy(kiw[:, t, 0:64], PD[t][:, 0:64])
            v.tensor_scalar(kiw[:, t, 128:144], PD[t][:, 64:80], H1 ** -0.5 * HD ** -0.5, None, ALU.mult)\
                .then_inc(S(f"bank_free{t}"), 1)
        phase_done(dve, "qi")
        phase_done(dve, "kiw")
        rope(qi_tm[:, :, :].rearrange("p t (h d) -> p t h d", d=HD), H1, 8, cosq, sinq, rt)
        rope(kiw[:, :, 0:64].rearrange("p t (h d) -> p t h d", d=HD), 1, 8, cosq, sinq, rt)
        v.tensor_copy(kiw[:, :, 64:128], kiw[:, :, 0:64]).then_inc(S("qi_roped"), 1)
        for h in range(H1):
            for t in range(1, TT):
                dve.wait_ge(S("idx_relu"), 3 * h + t)
                r = relu_s[:, h % 2, IDX_AT[t]:IDX_AT[t] + (t + 1) * P]
                sc = score[:, t, 0:(t + 1) * P]
                w = kiw[:, t, 128 + h:129 + h]
                if h:
                    dve.wait_ge(S("idx_sum"), 3 * (h - 1) + t)
                    v.scalar_tensor_tensor(out=sc, in0=r, scalar=w, in1=sc, op0=ALU.mult, op1=ALU.add)\
                        .then_inc(S("idx_sum"), 1)
                else:
                    v.tensor_scalar(sc, r, w, None, ALU.mult).then_inc(S("idx_sum"), 1)
        for r in range(TOPK // 8):
            for t in range(1, TT):
                if r == 0:
                    dve.wait_ge(S("score_masked"), t)
                else:
                    dve.wait_ge(S("top_taken"), 3 * (r - 1) + t)
                v.max(top8[:, t, :], score[:, t, 0:(t + 1) * P]).then_inc(S("top_found"), 1)
            for t in range(1, TT):
                dve.wait_ge(S("top_found"), 3 * r + t)
                v.match_replace(score[:, t, 0:(t + 1) * P], top8[:, t, :], score[:, t, 0:(t + 1) * P], CHOSEN)\
                    .then_inc(S("top_taken"), 1)
        for t in range(1, TT):
            dve.wait_ge(S("top_taken"), 3 * (TOPK // 8 - 1) + t)
            v.tensor_scalar(bias_q[:, t, 0:(t + 1) * P], score[:, t, 0:(t + 1) * P], CHOSEN, NEG, ALU.not_equal,
                            ALU.mult).then_inc(S("bias_made"), 1)
        phase_done(dve, "qk2")
        rope(qk_tm[:, :, :].rearrange("p t (h d) -> p t h d", d=HD), H1, 8, cosq, sinq, rt)
        v.tensor_copy(kiw[:, :, 64:128], kiw[:, :, 0:64]).then_inc(S("qk_roped"), 1)
        phase_done(dve, "gates")
        dve.wait_ge(S("pads"), 2)
        dve.wait_ge(S("tr_read"), TR["qk"][0] + 8)
        link(v.tensor_tensor(gc[:, :, 2:SEQ + 2], gc[:, :, 2:SEQ + 2], xi[:, :, :], ALU.mult))
        for f in range(4):
            col = [col_b[:, C_CW2 + 4 * j + f:C_CW2 + 4 * j + f + 1] for j in range(3)]
            link(v.tensor_scalar(ca[:, f, :], gc[:, f, 0:SEQ], col[0], None, ALU.mult))
            for j in (1, 2):
                link(v.scalar_tensor_tensor(out=ca[:, f, :], in0=gc[:, f, j:j + SEQ], scalar=col[j], in1=ca[:, f, :],
                                            op0=ALU.mult, op1=ALU.add))
            v.tensor_tensor(ca[:, f, :], ca[:, f, :], gb[:, f, :], ALU.mult).then_inc(S("conv2_out"), 1)
        for f in range(4):
            dve.wait_ge(S("conv2_hi"), f + 1)
            v.tensor_tensor(hlo[:, 4 + f, :], ca[:, f, :], fl(hhi[:, 4 + f, :]), ALU.subtract)\
                .then_inc(S("conv2_done"), 1)

        def row_max(n, m):
            for q, t in enumerate((3, 2, 0, 1)):
                b, c0 = QB_AT[t]
                dve.wait_ge(S("att_logits"), 3 * n + [1, 2, 2, 3][q])
                v.reduce_max(m[:, n % 2, t:t + 1], PX[n % 2][:, b, c0:c0 + (t + 1) * P], AX, negate=True)\
                    .then_inc(S("att_max"), 1)

        def turned(n, pt):
            dve.wait_ge(S("att_turned"), n + 1)
            if n >= 2:
                dve.wait_ge(S("att_pv"), n - 1)
            v.tensor_copy(pt[n % 2][:, SEQ:1280], PX[n % 2][:, 1:3, :].rearrange("p a b -> p (a b)")[:, 0:1280 - SEQ])\
                .then_inc(S("att_pt"), 1)

        def emit(n, d, dst):
            s = n % 2
            dve.wait_ge(S("att_exps"), 4 * n + 4)
            link(v.reciprocal(d[:, s, :], d[:, s, :]))
            dve.wait_ge(S("att_pv"), n + 1)
            v.tensor_tensor(dst, PM[:, 3, 256 * s:256 * s + 256].rearrange("p (t d) -> p t d", t=TT),
                            d[:, s, :].unsqueeze(2).to_broadcast([P, TT, HD]), ALU.mult).then_inc(S("att_out"), 1)

        for h in range(A_H + 1):
            if h < A_H:
                row_max(h, mx)
            if h:
                turned(h - 1, prt)
                emit(h - 1, den, v2[:, :, (h - 1) * HD:h * HD])
        split_tiles("attn", 4, lambda k: 1.0, 0)
        dve.wait_ge(S("row_mix0"), 16)
        post_norm(5, mix2, row_b, "post_mix0")
        normed(6, "ffn0_made")
        split_tiles("ffn0", 8, lambda k: col_a[:, C_FFN + k:C_FFN + k + 1], 0)

        def mlp(name, layer):
            u0 = PH[name][0]
            MPAR = {0: 0, 2: 1, 6: 0}

            def up(first, i, m):
                base = m * 4 + 32 * layer

                def square(b, r):
                    dve.wait_ge(S(f"bank_free{b}"), r + (PH[name][1][b] + 1))
                    v.tensor_tensor(mh_r[:, b % 2, :], mh_r[:, b % 2, :], mh_r[:, b % 2, :], ALU.mult)\
                        .then_inc(S("hidden_sq"), 1)

                def low(b):
                    dve.wait_ge(S("hidden_hi"), base + (b + 1))
                    v.tensor_tensor(mh_lo[MPAR[first]][:, b, :], mh_r[:, b % 2, :], fl(mh_hi[MPAR[first]][:, b, :]),
                                    ALU.subtract).then_inc(S("hidden_ready"), 1)
                r = {0: 0, 2: i * 6 + 1, 6: i * 6 + 4}[first]
                square(0, r)
                square(1, r)
                low(0)
                square(2, r)
                low(1)
                square(3, r)
                low(2)
                low(3)

            def down(first, r, i):
                for h in range(2):
                    for b in range(4):
                        full_wait(dve, name, b, r + h, i * 8 + (u0 + first + h))
                        m = mixm[:, b, 512 * h:512 * h + 512]
                        v.tensor_tensor(m, PD[b], m, ALU.add).then_inc(S(f"bank_free{b}"), 1)

            dve.wait_ge(S("acc_zero"), layer + 1)
            up(0, 0, 0)
            with dve.Fori(0, 3) as i:
                up(2, i, i * 2 + 1)
                down(4, i * 6 + 2, i)
                up(6, i, i * 2 + 2)
                down(8, i * 6 + 5, i)
            up(2, 3, 7)
            down(4, 20, 3)
            down(6, 22, 3)

        mlp("mlp0", 0)
        dve.wait_ge(S("row_ffn0"), 16)
        post_norm(7, mixm, row_a, "post_ffn0")
        normed(8, "mix1_made")
        split_tiles("mix1", 8, lambda k: col_a[:, C_MIX + 8 + k:C_MIX + 9 + k], 0)
        mean_square(9, Q_RANK)
        for t in range(TT):
            v.tensor_scalar(cq[:, t, :], cq[:, t, :], rstd[:, 9, t:t + 1], None, ALU.mult).then_inc(S("cq_made"), 1)
        mean_square(10, KV_RANK)
        for t in range(TT):
            v.tensor_scalar(kva[:, t, 0:KV_RANK], kva[:, t, 0:KV_RANK], rstd[:, 10, t:t + 1], None, ALU.mult)\
                .then_inc(S("ckv_made"), 1)
        split_tiles("cq", 3, lambda k: col_b[:, C_QN + k:C_QN + k + 1], 0)
        split_tiles("ckv", 2, lambda k: col_b[:, C_KN + k:C_KN + k + 1], 3)
        rope(kva[:, :, 256:288].rearrange("p t (h d) -> p t h d", h=1), 1, 16, cosm, sinm, rtm)
        v.tensor_copy(k_tm[:, :, :, C_NOPE:C_QK], kva[:, :, 256:288].unsqueeze(2).to_broadcast([P, TT, C_H, 32]))
        u0 = PH["ukv"][0]
        for n in range(2):
            for r in range(2):
                for t in range(TT):
                    if t == 3 and r == 0:
                        dve.wait_ge(S("bank_full3"), PH["ukv"][2][3] + n + 1)
                    else:
                        full_wait(dve, "ukv", t, 2 * n + r, u0 + n)
                    h0 = 8 * n + 4 * r
                    kv = PD[t].rearrange("p (h d) -> p h d", h=4)
                    v.tensor_copy(k_tm[:, t, h0:h0 + 4, 0:C_NOPE], kv[:, :, 0:64])
                    v.tensor_copy(heads(v3[:, t, h0 * HD:(h0 + 4) * HD]), kv[:, :, 64:128])\
                        .then_inc(S(f"bank_free{t}"), 1)
        phase_done(dve, "uq")
        q4 = q_tm[:, :, :].rearrange("p t (h d) -> p t h d", d=C_QK)
        rope(q4[:, :, :, C_NOPE:C_QK], C_H, 16, cosm, sinm, rtm)
        v.tensor_copy(kva[:, 0, 0:8], kva[:, 0, 8:16]).then_inc(S("mla_roped"), 1)

        def turned_k(h):
            dve.wait_ge(S("tr_done"), TR["heads"][0] + 2 * h + 2)
            v.tensor_copy(kth[h % 2][0:C_QK, :], PDT[0:C_QK, 3, :]).then_inc(S("tr_read"), 1)

        turned_k(0)
        for h in range(C_H + 1):
            if h < C_H:
                row_max(A_H + h, mx3)
            if h:
                turned(A_H + h - 1, prt3)
            if h + 1 < C_H:
                turned_k(h + 1)
            if h:
                emit(A_H + h - 1, den3, v3[:, :, (h - 1) * HD:h * HD])
        split_tiles("lat", 8, lambda k: 1.0, 0)
        dve.wait_ge(S("row_mix1"), 16)
        post_norm(11, mix3, row_b, "post_mix1")
        normed(12, "ffn1_made")
        split_tiles("ffn1", 8, lambda k: col_a[:, C_FFN + 8 + k:C_FFN + 9 + k], 0)
        mlp("mlp1", 1)
        dve.wait_ge(S("row_ffn1"), 16)
        post_norm(13, mixm, row_a, "post_ffn1")

    ctx.close()


NAMES = ["x", "c", "w_ada", "b_ada", "norm_in_gain", "w_in", "conv_w", "conv_b", "dt_bias", "a_log", "d_skip",
         "sb_norm_gain", "ssm_norm_gain", "w_out", "norm_f_gain", "positions_2", "norm_mix_pre_2",
         "norm_mix_post_2", "norm_ffn_pre_2", "norm_ffn_post_2", "even_w_in_2", "even_conv_w_2", "even_w_out_2",
         "odd_w_dq_2", "odd_q_norm_2", "odd_w_uq_2", "odd_w_dkv_2", "odd_kv_norm_2", "odd_w_ukv_2", "odd_w_o_2",
         "mlp_w1_2", "mlp_w2_2"]


def kernel(**inputs):
    import numpy as np
    import concourse.bacc as bacc
    from concourse.bass_utils import run_bass_kernel_spmd

    nc = bacc.Bacc("TRN2", target_bir_lowering=False, num_devices=1, dynamic_dma_scratch_size=1024)
    arrays, args = {}, []
    for name in NAMES:
        a = np.ascontiguousarray(inputs[name])
        arrays[f"in_{name}"] = a
        args.append(nc.dram_tensor(f"in_{name}", a.shape, mybir.dt.from_np(a.dtype), kind="ExternalInput").ap())
    args.append(nc.dram_tensor("out_0", (1, SEQ, DM), F32, kind="ExternalOutput").ap())
    build_program(nc, *args)
    r = run_bass_kernel_spmd(nc, [arrays], core_ids=[0])
    return r.results[0]["out_0"]
```

```python
import math
from contextlib import ExitStack

import concourse.bass as bass
from concourse import mybir

F32 = mybir.dt.float32
F32R = mybir.dt.float32r
I32 = mybir.dt.int32
ACT = mybir.ActivationFunctionType
ALU = mybir.AluOpType
AX = mybir.AxisListType.X

P = 128
SEQ = 512
DM = 1024
TT = SEQ // P
KT = DM // P
UNIT = 2048
NEG = -1e30
DROPPED = -3e38
CHOSEN = -2e38
EPS = 1e-6
H1 = 16
HD = 64
GROUPS = 2
HG = H1 // GROUPS
XBC_T = 12
A_H = 8
TOPK = 128
C_H = 16
C_QK = 96
C_NOPE = 64
Q_RANK = 384
KV_RANK = 256
D_FF = 4096
THETA = 500000.0
N_PARAMS = 14
ROUNDER = 1.5 * 2.0 ** 23
TWO_PI = [6.28125, 1014 / 2.0 ** 19, 2 * math.pi - 6.28125 - 1014 / 2.0 ** 19]
PI_BELOW = 3.1415925
CLAMP = 20.0
IDX_AT = {1: 0, 2: 256, 3: 640}


def phase_table():
    def rounds(n):
        return [n] * 4, [n, n, n, 0]

    rows = [
        ("ada_ss", 0, ([1] * 4, [0] * 4)), ("ada_g", 0, ([1, 1, 0, 0], [0] * 4)), ("q", 4, rounds(2)), ("k", 4, rounds(2)), ("v", 4, rounds(2)),
        ("xbc", 6, rounds(3)), ("z_ssm", 4, rounds(2)), ("dt", 1, ([0, 0, 0, 2], [0] * 4)),
        ("z_attn", 4, rounds(2)), ("wout_a", 4, rounds(2)),
        ("wout_s", 4, rounds(2)), ("qi", 2, rounds(1)), ("kiw", 1, ([0, 0, 0, 1], [0] * 4)), ("qi2", 2, rounds(1)), ("qk2", 4, rounds(2)),
        ("v2", 2, rounds(1)), ("gates", 6, rounds(3)), ("wo2", 4, rounds(2)), ("mlp0", 32, rounds(24)),
        ("dq", 2, rounds(1)), ("dkv", 2, rounds(1)), ("uq", 3, rounds(3)),
        ("ukv", 2, ([4] * 4, [4, 4, 4, 2])), ("wo3", 4, rounds(2)), ("mlp1", 32, rounds(24)),
    ]
    unit, free, full, table = 0, [0] * 4, [0] * 4, {}
    for name, units, (f, g) in rows:
        table[name] = (unit, list(free), list(full), units)
        unit += units
        free = [a + b for a, b in zip(free, f)]
        full = [a + b for a, b in zip(full, g)]
    table["end"] = (unit, list(free), list(full), 0)
    return table


def transpose_table():
    rows = [("params", 2, 0), ("h", 8, 1), ("scan", 10, 0), ("y_attn", 8, 1), ("y_ssm", 8, 1), ("mix0", 8, 1),
            ("qi", 8, 0), ("ki", 1, 0), ("qk", 8, 0), ("attn", 4, 1), ("ffn0", 8, 1), ("mix1", 8, 1),
            ("cq", 3, 1), ("ckv", 2, 1), ("heads", 2 * C_H, 0), ("lat", 8, 1), ("ffn1", 8, 1)]
    n, split, table = 0, 0, {}
    for name, groups, is_split in rows:
        table[name] = (n, split)
        n += groups
        split += groups * is_split
    return table


def build_program(nc, x, c, w_ada, b_ada, norm_in_gain, w_in, conv_w, conv_b, dt_bias, a_log, d_skip,
                  sb_norm_gain, ssm_norm_gain, w_out, norm_f_gain, positions_2, norm_mix_pre_2,
                  norm_mix_post_2, norm_ffn_pre_2, norm_ffn_post_2, even_w_in_2, even_conv_w_2,
                  even_w_out_2, odd_w_dq_2, odd_q_norm_2, odd_w_uq_2, odd_w_dkv_2, odd_kv_norm_2,
                  odd_w_ukv_2, odd_w_o_2, mlp_w1_2, mlp_w2_2, out):
    PH = phase_table()
    TR = transpose_table()
    ctx = ExitStack()
    sems = {}

    def S(name):
        if name not in sems:
            sems[name] = ctx.enter_context(nc.semaphore(name))
        return sems[name]

    cursor = [(nc.sbuf_base + 63) // 64 * 64]

    place = {}

    def at(name, shape, dtype=F32, offset=None):
        size = 4
        for n in shape[1:]:
            size *= n
        if offset is None:
            offset = cursor[0]
            cursor[0] += (size + 31) // 32 * 32
        place[name] = offset
        return nc.alloc_sbuf_tensor_at(name, shape, dtype, offset=offset)

    wraw = [at(f"wraw{s}", [P, UNIT]) for s in range(2)]
    whi = [at(f"whi{s}", [P, UNIT], F32R) for s in range(2)]
    wlo = [at(f"wlo{s}", [P, UNIT], F32R) for s in range(2)]
    hhi = at("hhi", [P, KT, SEQ], F32R)
    hlo = at("hlo", [P, KT, SEQ], F32R)
    xres = at("xres", [P, TT, DM])
    ident = at("ident", [P, P])
    identr = at("identr", [P, P], F32R)
    ones = at("ones", [P, P])
    tri_le = at("tri_le", [P, P])
    tri_gt = at("tri_gt", [P, P])
    neg_ge = at("neg_ge", [P, P], F32R)
    neg_one = at("neg_one", [P, P], F32R)
    mask_t = at("mask_t", [P, P], F32R)
    mask_q = at("mask_q", [P, P], F32R)
    scratch = at("scratch", [P, P])
    scratch1 = at("scratch1", [P, P])
    junk = at("junk", [P, 2, DM], mybir.dt.bfloat16)
    tall = at("tall", [P, SEQ], offset=place["junk"])
    sinall = at("sinall", [P, TT, 24])
    col_a = at("col_a", [P, P])
    col_b = at("col_b", [P, 32])
    stat = at("stat", [P, 16, TT])
    rstd = at("rstd", [P, 16, TT])
    stat0 = at("stat0", [P, 16, TT])
    eps = at("eps", [P, 1])
    small = at("small", [P, 64])
    cosq = at("cosq", [P, TT, 8])
    sinq = at("sinq", [P, TT, 8])
    cosm = at("cosm", [P, TT, 16])
    sinm = at("sinm", [P, TT, 16])
    row_a = at("row_a", [P, DM])
    row_b = at("row_b", [P, DM])
    A0 = cursor[0]
    KB = 1024

    def arena(name, shape, kb, dtype=F32):
        return at(name, shape, dtype, offset=A0 + int(kb * KB))

    xn = arena("xn", [P, TT, DM], 0)
    b_row = arena("b_row", [P, 2 * DM], 40)
    mod = arena("mod", [P, 2 * DM], 48)
    prm_a = arena("prm_a", [P, P], 60)
    prm_b = arena("prm_b", [32, P], 60.5)
    pos_i = arena("pos_i", [P, TT], 64, I32)
    pos_f = arena("pos_f", [P, TT], 64.25)
    freq = arena("freq", [P, 24], 64.5)
    ang = arena("ang", [P, TT, 24], 65)
    ang_n = arena("ang_n", [P, TT, 24], 66)
    ang_s = arena("ang_s", [P, TT, 24], 67)
    silu_c = arena("silu_c", [P, KT, P], 70)
    gate = arena("gate", [P, DM], 98)
    row_c = arena("row_c", [P, DM], 52)
    qt = arena("qt", [P, KT, SEQ], 0)
    kt = arena("kt", [P, KT, SEQ], 16)
    vo = arena("vo", [P, TT, DM], 32)
    sb_l = arena("sb_l", [P, 1280], 48)
    sb_hi = arena("sb_hi", [P, 1280], 53, F32R)
    sb_lo = arena("sb_lo", [P, 1280], 58, F32R)
    sb_w = arena("sb_w", [P, 1280], 63)
    za = arena("za", [P, TT, DM], 16)
    mix = arena("mix", [P, TT, DM], 16)
    xbc = arena("xbc", [P, XBC_T, SEQ + 3], 68)
    dts = arena("dts", [P, 6, TT * H1], 92.5)
    conv_acc = arena("conv_acc", [P, 2, SEQ], 94)
    zs = xres
    yt = arena("yt", [P, TT, DM], 0)
    xdt = arena("xdt", [P, DM], 48)
    xdte = arena("xdte", [P, DM], 52)
    hst = arena("hst", [P, DM], 56)
    b_tm = arena("b_tm", [P, TT, 2 * P], 60)
    cbm = arena("cbm", [P, 8, P], 64)
    ldm = arena("ldm", [P, H1, P], 68)
    dec = [arena(f"dec{s}", [P, HG, P], 76 + 4 * s) for s in range(2)]
    off = arena("off", [P, SEQ], 94)
    xd = arena("xd", [P, SEQ], 96)
    qi_tm = arena("qi_tm", [P, TT, DM], 0)
    qk_tm = arena("qk_tm", [P, TT, DM], 16)
    kiw = arena("kiw", [P, TT, 144], 32)
    v2 = arena("v2", [P, TT, 512], 34.5)
    qit = arena("qit", [P, KT, SEQ], 42.5)
    kit = arena("kit", [P, SEQ], 58.5)
    score = arena("score", [P, TT, SEQ], 60.5)
    relu_s = arena("relu_s", [P, 2, 1152], 68.5)
    top8 = arena("top8", [P, TT, 8], 77.5)
    qkt = arena("qkt", [P, KT, SEQ], 78)
    rt = arena("rt", [P, 4, TT * H1 * 8], 94)
    bias_q = arena("bias_q", [P, TT, SEQ], 0, F32R)
    pr = [arena("pr0", [P, 1280], 8), arena("pr1", [P, 1280], 13)]
    prt = [arena("prt0", [P, 1280], 18), arena("prt1", [P, 1280], 23)]
    mx = arena("mx", [P, 4, TT], 77.625)
    den = arena("den", [P, 4, TT], 77.75)
    gb = arena("gb", [P, TT, SEQ], 42.5)
    gc = arena("gc", [P, TT, SEQ + 2], 50.5)
    xi = arena("xi", [P, TT, SEQ], 68.5)
    ca = arena("ca", [P, TT, SEQ], 94)
    mix2 = arena("mix2", [P, TT, DM], 58.75)
    mh_hi = [arena(f"mh_hi{s}", [P, 4, SEQ], 16 + 16 * s, F32R) for s in range(2)]
    mh_lo = [arena(f"mh_lo{s}", [P, 4, SEQ], 24 + 16 * s, F32R) for s in range(2)]
    mh_r = arena("mh_r", [P, 2, SEQ], 48)
    mixm = arena("mixm", [P, TT, DM], 56)
    kva = arena("kva", [P, TT, 288], 16)
    cq = arena("cq", [P, TT, Q_RANK], 21)
    q_tm = arena("q_tm", [P, TT, C_H * C_QK], 27)
    k_tm = arena("k_tm", [P, TT, C_H, C_QK], 51)
    v3 = arena("v3", [P, TT, DM], 75)
    rtm = arena("rtm", [P, 4, TT * C_H * 16], 0)
    qth = [arena(f"qth{s}", [P, SEQ], 2 * s) for s in range(2)]
    kth = [arena(f"kth{s}", [P, SEQ], 4 + 2 * s) for s in range(2)]
    pr3 = [arena("pr30", [P, 1280], 8), arena("pr31", [P, 1280], 16)]
    prt3 = [arena("prt30", [P, 1280], 21), arena("prt31", [P, 1280], 91)]
    mx3 = arena("mx3", [P, 4, TT], 14)
    den3 = arena("den3", [P, 4, TT], 14.5)
    mix3 = arena("mix3", [P, TT, DM], 27)
    assert A0 + 102 * KB <= nc.sbuf_usable_end, (A0, nc.sbuf_usable_end)

    PDT = ctx.enter_context(nc.psum_tensor("PDT", [P, 4, SEQ], F32))
    PM = ctx.enter_context(nc.psum_tensor("PM", [P, 4, SEQ], F32))
    PD = [PDT[:, b, :] for b in range(4)]
    PX = [PM, PDT]

    ada_places = [place[w] for w in ("whi0", "whi1", "wlo0", "wlo1")]
    ada_places += [place[w] + half * 8 * KB for w in ("hhi", "hlo") for half in range(2)]
    ada_places += [A0 + kb * KB for kb in (16, 24, 32, 78)]
    ADA_SLOTS = [at(f"w_ada{n}", [P, UNIT], offset=o) for n, o in enumerate(ada_places)]
    ADA_COLUMNS = [DM, DM + 512, 0, 512, 2 * DM, 2 * DM + 512]

    C_C, C_CW, C_CB, C_SBG, C_SSG, C_MIX, C_FFN = 0, 8, 56, 68, 76, 84, 100
    C_QN, C_KN, C_CW2 = 0, 3, 5
    ROWS_A, ROWS_B = 116, 17

    SB_CHUNKS = [[(1, 0), (3, 384)], [(2, 0)], [(0, 0)]]
    SB_FIRST = [0, 512, 768]
    SB_WIDE = [512, 256, 512]
    SB_AT = {1: (0, 0), 3: (0, 384), 2: (1, 0), 0: (2, 0)}
    QB_AT = {3: (0, 0), 2: (1, 0), 0: (1, 384), 1: (2, 0)}
    QB_FIRST = {3: 0, 2: 512, 0: 896, 1: 1024}

    def kmajor(w):
        return w.rearrange("(k p) n -> p k n", p=P)

    w_ada_v, w_in_v, w_out_v = kmajor(w_ada[0]), kmajor(w_in[0]), kmajor(w_out[0])
    w_even_v, w_eo_v = kmajor(even_w_in_2[0]), kmajor(even_w_out_2[0])
    w_dq_v, w_uq_v, w_dkv_v = kmajor(odd_w_dq_2[0]), kmajor(odd_w_uq_2[0]), kmajor(odd_w_dkv_2[0])
    w_ukv_v, w_oo_v = kmajor(odd_w_ukv_2[0]), kmajor(odd_w_o_2[0])
    w1_v = [kmajor(mlp_w1_2[j]) for j in range(2)]
    w2_v = [kmajor(mlp_w2_2[j]) for j in range(2)]

    def wview(t, kn, n):
        return t[:, 0:kn * n].rearrange("p (k n) -> p k n", k=kn)

    def fl(ap):
        return ap.bitcast(F32)

    def loop(eng, n, body):
        if n == 1:
            body(0)
        else:
            with eng.Fori(0, n) as i:
                body(i)

    def dyn(t, i, b):
        return t[:, bass.ds(i * 4 + b, 1), :]

    def phase_done(eng, name):
        names = list(PH)
        after = PH[names[names.index(name) + 1]][1]
        for b in range(4):
            if after[b] > PH[name][1][b]:
                eng.wait_ge(S(f"bank_free{b}"), after[b])

    def full_wait(eng, name, b, r, unit):
        if b < 3:
            eng.wait_ge(S(f"bank_full{b}"), r + (PH[name][2][b] + 1))
        else:
            eng.wait_ge(S("w_used"), unit + 1)

    def pieces(name, rounds):
        return [(name, r, h, b) for r in range(rounds) for h in range(2) for b in range(4)]

    SB_PIECES = pieces("xbc", 3) + pieces("z_ssm", 2) + [("dt", 0, 0, 3)] + pieces("z_attn", 1)
    SCAN_PIECES = pieces("wout_a", 2)
    INDEX_PIECES = pieces("qk2", 2)
    dt_head = SB_PIECES.index(("dt", 0, 0, 3)) // 3
    assert SB_PIECES.index(("dt", 0, 0, 3)) % 3 < 2

    def step_pieces(n):
        return SCAN_PIECES[(3 * n + 1) // 2:(3 * n + 4) // 2]

    NORM_ORDER = [("A", 0), ("A", 1), ("B", 0), ("A", 2), ("B", 1), ("A", 3), ("B", 2), ("C", 0), ("B", 3),
                  ("C", 1), ("C", 2), ("C", 3)]
    FIRST_ORDER = [("first", 0), ("first", 1), ("A", 0), ("first", 2), ("A", 1), ("B", 0), ("first", 3), ("A", 2),
                   ("B", 1), ("A", 3), ("B", 2), ("C", 0), ("B", 3), ("C", 1), ("C", 2), ("C", 3)]

    def rotation(view, heads, half, c, s, tmp):
        n = TT * heads * half
        shape = [P, TT, heads, half]
        cb = c[:, :, :].unsqueeze(2).to_broadcast(shape)
        sb = s[:, :, :].unsqueeze(2).to_broadcast(shape)
        x1, x2 = view[:, :, :, 0:half], view[:, :, :, half:2 * half]
        t = [tmp[:, j, 0:n].rearrange("p (a h d) -> p a h d", a=TT, h=heads) for j in range(4)]
        return [(t[0], x1, cb, ALU.mult), (t[1], x2, sb, ALU.mult), (t[2], x2, cb, ALU.mult),
                (t[3], x1, sb, ALU.mult), (x1, t[0], t[1], ALU.subtract), (x2, t[2], t[3], ALU.add)]

    block = ctx.enter_context(nc.Block())

    @block.sync
    def _(sp):
        def load(dst, src, sem="params"):
            sp.dma_start(dst, src).then_inc(S(sem), 16)

        def unit(u, par, kn, n, src):
            if not isinstance(u, int) or u >= 2:
                sp.wait_ge(S("w_split"), u - 1)
            sp.dma_start(wview(wraw[par], kn, n), src).then_inc(S(f"w_loaded{par}"), 16)

        def columns(name, w, n_chunks, c0, k0=0, unrolled=False):
            u0 = PH[name][0]

            def body(i):
                cc = c0 + i * 512 if isinstance(i, int) else sp.snap(i * 512 + c0)
                for h in range(2):
                    par = (u0 + h) % 2
                    unit(i * 2 + (u0 + h), par, 4, 512,
                         w[:, k0 + 4 * h:k0 + 4 * h + 4, bass.ds(cc, 512)])
            if unrolled:
                for i in range(n_chunks):
                    body(i)
            else:
                loop(sp, n_chunks, body)

        def mlp(name, j):
            u0 = PH[name][0]

            def up(i, d):
                cc = i * 1024 + 512 * d if isinstance(i, int) else sp.snap(i * 1024 + 512 * d)
                return [w1_v[j][:, 4 * h:4 * h + 4, bass.ds(cc, 512)] for h in range(2)]

            def down(i, d):
                kk = i * 8 + 4 * d if isinstance(i, int) else sp.snap(i * 8 + 4 * d)
                return [w2_v[j][:, bass.ds(kk, 4), 512 * h:512 * h + 512] for h in range(2)]

            def four(i, first, srcs):
                for n, s in enumerate(srcs):
                    unit(i * 8 + (u0 + first + n), (u0 + first + n) % 2, 4, 512, s)

            four(0, 0, up(0, 0))
            with sp.Fori(0, 3) as i:
                four(i, 2, up(i, 1))
                four(i, 4, down(i, 0))
                four(i, 6, up(i, 2))
                four(i, 8, down(i, 1))
            four(3, 2, up(3, 1))
            four(3, 4, down(3, 0))
            four(3, 6, down(3, 1))

        load(prm_a[C_C:C_C + 8, :], c.rearrange("a (k p) -> (a k) p", p=P), "params_c")

        def ada(first, end):
            for n in range(first, end):
                cc = ADA_COLUMNS[n // 2]
                load(wview(ADA_SLOTS[n], 4, 512), w_ada_v[:, 4 * (n % 2):4 * (n % 2) + 4, cc:cc + 512],
                     f"ada_loaded{n}")

        ada(0, 2)
        load(b_row[:, :], b_ada[0][0:2 * DM].partition_broadcast(P), "rows_mod")
        load(row_a[:, :], norm_in_gain[0].partition_broadcast(P), "rows_mod")
        ada(2, 4)
        load(xres[:, :, :], x[0].rearrange("(t p) n -> p t n", p=P), "x_loaded")
        ada(4, 8)
        with nc.allow_non_contiguous_dma(reason="512 positions"):
            load(pos_i[:, :], positions_2[0].rearrange("(t p) -> p t", p=P))
        ada(8, 10)
        load(row_b[:, :], b_ada[0][2 * DM:3 * DM].partition_broadcast(P))
        ada(10, 12)
        for h in range(2):
            unit(h, h, 4, 512, w_in_v[:, 4 * h:4 * h + 4, 0:512])
        load(prm_a[C_CW:C_CW + 48, :], conv_w[0].rearrange("j (k p) -> (j k) p", p=P))
        load(prm_a[C_CB:C_CB + 12, :], conv_b[0].rearrange("(k p) -> k p", p=P))
        load(prm_a[C_SBG:C_SBG + 8, :], sb_norm_gain[0].rearrange("(k p) -> k p", p=P))
        load(prm_a[C_SSG:C_SSG + 8, :], ssm_norm_gain[0].rearrange("(k p) -> k p", p=P))
        load(prm_a[C_MIX:C_MIX + 16, :], norm_mix_pre_2.rearrange("j (k p) -> (j k) p", p=P))
        load(prm_a[C_FFN:C_FFN + 16, :], norm_ffn_pre_2.rearrange("j (k p) -> (j k) p", p=P))
        load(prm_b[C_QN:C_QN + 3, :], odd_q_norm_2[0].rearrange("(k p) -> k p", p=P))
        load(prm_b[C_KN:C_KN + 2, :], odd_kv_norm_2[0].rearrange("(k p) -> k p", p=P))
        load(prm_b[C_CW2:C_CW2 + 12, :], even_conv_w_2[0].rearrange("j (k p) -> (j k) p", p=P))
        load(small[:, 0:16], dt_bias[0].partition_broadcast(P))
        load(small[:, 16:32], a_log[0].partition_broadcast(P))
        load(small[:, 32:48], d_skip[0].partition_broadcast(P))
        for h in range(2):
            unit(2 + h, h, 4, 512, w_in_v[:, 4 * h:4 * h + 4, 512:1024])
        columns("k", w_in_v, 2, DM)
        columns("v", w_in_v, 2, 2 * DM)
        sp.wait_ge(S("h_made"), TT)
        load(row_a[:, :], norm_f_gain.partition_broadcast(P), "row_f")
        columns("xbc", w_in_v, 3, 4 * DM)
        columns("z_ssm", w_in_v, 2, 4 * DM + 1552)
        u0 = PH["dt"][0]
        unit(u0, u0 % 2, 8, 16, w_in_v[:, :, 4 * DM + 1536:4 * DM + 1552])
        columns("z_attn", w_in_v, 2, 3 * DM)
        columns("wout_a", w_out_v, 2, 0)
        columns("wout_s", w_out_v, 2, 0, k0=8)
        sp.wait_ge(S("y_gated"), TT)
        load(xres[:, :, :], x[0].rearrange("(t p) n -> p t n", p=P), "x_again")
        load(row_c[:, :], norm_mix_pre_2[0].partition_broadcast(P), "row_pre")
        columns("qi", w_even_v, 1, 1536)
        u0 = PH["kiw"][0]
        unit(u0, u0 % 2, 8, 80, w_even_v[:, :, 2560:2640])
        columns("qi2", w_even_v, 1, 2048)
        phase_done(sp, "ada_g")
        load(row_b[:, :], norm_mix_post_2[0].partition_broadcast(P), "row_mix0")
        columns("qk2", w_even_v, 2, 0)
        columns("v2", w_even_v, 1, DM)
        columns("gates", w_even_v, 3, 2640)
        sp.wait_ge(S("first_out"), TT)
        load(row_a[:, :], norm_ffn_post_2[0].partition_broadcast(P), "row_ffn0")
        columns("wo2", w_eo_v, 2, 0)
        sp.wait_ge(S("conv2_done"), 4)
        load(row_c[:, :], norm_ffn_pre_2[0].partition_broadcast(P), "row_pre")
        mlp("mlp0", 0)
        sp.wait_ge(S("post_mix0"), TT)
        load(row_b[:, :], norm_mix_post_2[1].partition_broadcast(P), "row_mix1")
        sp.wait_ge(S("ffn0_made"), TT)
        load(row_c[:, :], norm_mix_pre_2[1].partition_broadcast(P), "row_pre")
        u0 = PH["dq"][0]
        for h in range(2):
            unit(u0 + h, (u0 + h) % 2, 4, Q_RANK, w_dq_v[:, 4 * h:4 * h + 4, :])
        u0 = PH["dkv"][0]
        for h in range(2):
            unit(u0 + h, (u0 + h) % 2, 4, 288, w_dkv_v[:, 4 * h:4 * h + 4, :])
        u0 = PH["uq"][0]
        for n in range(3):
            unit(u0 + n, (u0 + n) % 2, 3, 512, w_uq_v[:, :, 512 * n:512 * n + 512])
        u0 = PH["ukv"][0]
        for n in range(2):
            unit(u0 + n, (u0 + n) % 2, 2, 1024, w_ukv_v[:, :, 1024 * n:1024 * n + 1024])
        columns("wo3", w_oo_v, 2, 0)
        sp.wait_ge(S("tr_read"), TR["lat"][0])
        load(row_c[:, :], norm_ffn_pre_2[1].partition_broadcast(P), "row_pre")
        mlp("mlp1", 1)
        sp.wait_ge(S("post_ffn0"), TT)
        load(row_a[:, :], norm_ffn_post_2[1].partition_broadcast(P), "row_ffn1")
        for t in range(TT):
            sp.wait_ge(S("post_ffn1"), t + 1)
            sp.dma_start(out[0, t * P:(t + 1) * P, :], xres[:, t, :]).then_inc(S("stored"), 16)
        sp.wait_ge(S("stored"), 16 * TT)

    @block.tensor
    def _(pe):
        mm = nc.tensor.matmul

        def bank_wait(name, b, r):
            pe.wait_ge(S(f"bank_free{b}"), r + PH[name][1][b])

        def unit_wait(u):
            pe.wait_ge(S("w_split"), u + 1)

        def tm(bank, n, act, k0, ws, kn, nn, c0, start, stop, t):
            hi, lo = act
            wh, wl = wview(whi[ws], kn, nn), wview(wlo[ws], kn, nn)
            for k in range(kn):
                sth, stl = hi[:, k0 + k, t * P:t * P + P], lo[:, k0 + k, t * P:t * P + P]
                mm(bank, sth, wh[:, k, c0:c0 + n], start=start and k == 0, stop=False)
                mm(bank, sth, wl[:, k, c0:c0 + n], start=False, stop=False)
                last = mm(bank, stl, wh[:, k, c0:c0 + n], start=False, stop=stop and k == kn - 1)
            return last

        def fm(bank, act, k0, ws, f, start, stop):
            hi, lo = act
            wh, wl = wview(whi[ws], 4, 512), wview(wlo[ws], 4, 512)
            for k in range(4):
                sth, stl = wh[:, k, f * P:f * P + P], wl[:, k, f * P:f * P + P]
                mm(bank, sth, hi[:, k0 + k, :], start=start and k == 0, stop=False)
                mm(bank, sth, lo[:, k0 + k, :], start=False, stop=False)
                last = mm(bank, stl, hi[:, k0 + k, :], start=False, stop=stop and k == 3)
            return last

        def full(last, b):
            last.then_inc(S("w_used" if b == 3 else f"bank_full{b}"), 1)

        def two_units(name, first, r, i, stride, feature_major, n=512):
            u0 = PH[name][0] + first
            for h in range(2):
                unit_wait(i * stride + (u0 + h))
                for b in range(4):
                    if h == 0:
                        bank_wait(name, b, r)
                    if feature_major:
                        last = fm(PD[b], (hhi, hlo), 4 * h, (u0 + h) % 2, b, h == 0, h == 1)
                    else:
                        last = tm(PD[b][:, 0:n], n, (hhi, hlo), 4 * h, (u0 + h) % 2, 4, n, 0, h == 0, h == 1, b)
                    if h == 1:
                        full(last, b)
                if h == 0:
                    last.then_inc(S("w_used"), 1)

        def chunks(name, n, feature_major):
            loop(pe, n, lambda i: two_units(name, 0, i, i, 2, feature_major))

        def transposes(name, nk, src, first=0):
            for k in range(first, nk):
                n = TR[name][0] + k
                pe.wait_ge(S("tr_read"), max(TR[name][0], n - 3))
                for t in range(TT):
                    last = nc.tensor.transpose(PM[:, k % 4, t * P:t * P + P], src(t, k), ident[:, :])
                last.then_inc(S("tr_done"), 1)

        def tile_transposes(name, first=0, end=TT):
            for n in range(2 * first, 2 * end):
                t, q = n // 2, n % 2
                pe.wait_ge(S(f"{name}_made"), t + 1)
                pe.wait_ge(S("tr_read"), max(TR[name][0], TR[name][0] + n - 3))
                for k in range(4):
                    last = nc.tensor.transpose(PM[:, n % 4, k * P:k * P + P],
                                               xn[:, t, (4 * q + k) * P:(4 * q + k + 1) * P], ident[:, :])
                last.then_inc(S("tr_done"), 1)

        def tiles_and_units(tiles, name, n):
            tile_transposes(tiles, 0, 2)
            u0 = PH[name][0]
            for h in range(2):
                for b in range(4):
                    if b == 0:
                        unit_wait(u0 + h)
                    if h == 0:
                        pe.wait_ge(S("tr_read"), TR[tiles][0] + 2 * (b + 1))
                        bank_wait(name, b, 0)
                    last = tm(PD[b][:, 0:n], n, (hhi, hlo), 4 * h, (u0 + h) % 2, 4, n, 0, h == 0, h == 1, b)
                    if h == 1:
                        full(last, b)
                    elif b < 2:
                        tile_transposes(tiles, b + 2, b + 3)
                if h == 0:
                    last.then_inc(S("w_used"), 1)

        def transposed(name, nk):
            pe.wait_ge(S("tr_read"), TR[name][0] + nk)

        def mlp(name, layer):
            u0 = PH[name][0]

            def up(first, r, i):
                two_units(name, first, r, i, 8, True)

            def down(par, first, r, i, m):
                pe.wait_ge(S("hidden_ready"), m * 4 + (32 * layer + 4))
                for h in range(2):
                    unit_wait(i * 8 + (u0 + first + h))
                    for b in range(4):
                        bank_wait(name, b, r + h)
                        full(tm(PD[b], 512, (mh_hi[par], mh_lo[par]), 0, (u0 + first + h) % 2, 4, 512,
                                0, True, True, b), b)

            up(0, 0, 0)
            with pe.Fori(0, 3) as i:
                up(2, i * 6 + 1, i)
                down(0, 4, i * 6 + 2, i, i * 2)
                up(6, i * 6 + 4, i)
                down(1, 8, i * 6 + 5, i, i * 2 + 1)
            up(2, 19, 3)
            down(0, 4, 20, 3, 6)
            down(1, 6, 22, 3, 7)

        pe.wait_ge(S("masks"), 1)
        pe.wait_ge(S("params_c"), 16)
        nc.tensor.transpose(PM[:, 3, 0:8], prm_a[0:8, :], ident[0:8, 0:8]).then_inc(S("tr_done"), 1)
        pe.wait_ge(S("c_ready"), 1)
        for n in range(12):
            j = n // 2
            pe.wait_ge(S(f"ada_loaded{n}"), 16)
            if n in (8, 10):
                bank_wait("ada_g", j - 4, 0)
            w = wview(ADA_SLOTS[n], 4, 512)
            for k in range(4):
                last = mm(PD[j % 4], silu_c[:, 4 * (n % 2) + k, :], w[:, k, :], start=n % 2 == 0 and k == 0,
                          stop=n % 2 == 1 and k == 3)
            last.then_inc(S("ada_used"), 1)
        pe.wait_ge(S("params"), 16 * N_PARAMS)
        nc.tensor.transpose(PM[:, 2, 0:ROWS_A], prm_a[0:ROWS_A, :], ident[0:ROWS_A, 0:ROWS_A])
        nc.tensor.transpose(PM[:, 2, P:P + ROWS_B], prm_b[0:ROWS_B, :], ident[0:ROWS_B, 0:ROWS_B]).then_inc(S("tr_done"), 1)
        pe.wait_ge(S("h_made"), TT)
        transposes("h", 8, lambda t, k: xn[:, t, k * P:k * P + P])
        transposed("h", 8)
        chunks("q", 2, True)
        chunks("k", 2, True)
        chunks("v", 2, False)

        def sb_scores(h):
            p0, ft = HD * (h % 2), h // 2
            for n, blocks in enumerate(SB_CHUNKS):
                if h:
                    pe.wait_ge(S("sb_weights"), 3 * (h - 1) + n + 1)
                for m, (s, c0) in enumerate(blocks):
                    w = SEQ - s * P
                    mm(PM[:, n, c0:c0 + w], kt[p0:p0 + HD, ft, s * P:s * P + P], qt[p0:p0 + HD, ft, s * P:SEQ],
                       start=m == 0, stop=False, skip_group_check=True)
                    last = mm(PM[:, n, c0:c0 + P], identr[:, :], mask_t[:, :], start=False, stop=False,
                              skip_group_check=True)
                last.then_inc(S("sb_z"), 1)

        def sb_tails(h):
            for n, blocks in enumerate(SB_CHUNKS):
                pe.wait_ge(S("sb_split"), 3 * h + max(n + 1, 2))
                for m, (s, c0) in enumerate(blocks):
                    for j in range(s, TT):
                        cj, cc = SB_AT[j]
                        a = SB_FIRST[cj] + cc
                        w = SEQ - j * P
                        st = neg_ge if j == s else neg_one
                        o = PM[:, n, c0 + (j - s) * P:c0 + (j - s) * P + w]
                        for part in (sb_hi, sb_lo):
                            last = mm(o, st[:, :], part[:, a:a + w], start=False,
                                      stop=m == len(blocks) - 1 and j == TT - 1 and part is sb_lo,
                                      skip_group_check=True)
                last.then_inc(S("sb_tail"), 1)

        def sb_values(h):
            if h >= 2:
                pe.wait_ge(S("sb_out"), h - 1)
            pe.wait_ge(S("sb_weights"), 3 * h + 3)
            for t in range(TT):
                for s in range(t + 1):
                    cj, cc = SB_AT[s]
                    a = SB_FIRST[cj] + cc + (t - s) * P
                    last = mm(PM[:, 3, (h % 2) * 256 + t * HD:(h % 2) * 256 + t * HD + HD], sb_w[:, a:a + P],
                              vo[:, s, h * HD:h * HD + HD], start=s == 0, stop=s == t)
            last.then_inc(S("sb_pv"), 1)

        for name in ("q", "k", "v"):
            phase_done(pe, name)
        def narrow(name, n):
            u = PH[name][0]
            unit_wait(u)
            bank_wait(name, 3, 0)
            wh, wl = wview(whi[u % 2], KT, n), wview(wlo[u % 2], KT, n)
            for k in range(KT):
                mm(PD[3][0:n, :], wh[:, k, :], hhi[:, k, :], start=k == 0, stop=False)
                mm(PD[3][0:n, :], wh[:, k, :], hlo[:, k, :], start=False, stop=False)
                last = mm(PD[3][0:n, :], wl[:, k, :], hhi[:, k, :], start=False, stop=k == KT - 1)
            last.then_inc(S("w_used"), 1)

        def turn_narrow(name, n, bank):
            pe.wait_ge(S("bank_free3"), PH[name][1][3] + 1)
            for t in range(TT):
                last = nc.tensor.transpose(bank[:, n * t:n * t + n], tall[0:n, t * P:t * P + P], ident[0:n, 0:n])
            last.then_inc(S(f"{name}_turned"), 1)

        def piece(name, r, h, b):
            u = PH[name][0] + 2 * r + h
            if name == "dt":
                narrow("dt", H1)
                return
            if b == 0:
                unit_wait(u)
            if h == 0:
                bank_wait(name, b, r)
            if name == "xbc":
                last = fm(PD[b], (hhi, hlo), 4 * h, u % 2, b, h == 0, h == 1)
            else:
                last = tm(PD[b], 512, (hhi, hlo), 4 * h, u % 2, 4, 512, 0, h == 0, h == 1, b)
            if h == 1:
                full(last, b)
            elif b == 3:
                last.then_inc(S("w_used"), 1)

        for h in range(H1):
            sb_scores(h)
            if h:
                sb_values(h - 1)
            piece(*SB_PIECES[3 * h])
            piece(*SB_PIECES[3 * h + 1])
            sb_tails(h)
            piece(*SB_PIECES[3 * h + 2])
            if h == dt_head:
                turn_narrow("dt", H1, PD[3])
        sb_values(H1 - 1)
        for p in SB_PIECES[3 * H1:]:
            piece(*p)

        pe.wait_ge(S("conv_sum"), XBC_T)
        pe.wait_ge(S("sb_weights"), 3 * H1)
        pe.wait_ge(S("sb_out"), H1)
        for n, p in enumerate(pieces("z_attn", 2)[8:]):
            piece(*p)
            first = n + min(n, 2)
            if n == 6:
                pe.wait_ge(S("conv_done"), 2)
            transposes("scan", first + (2 if n < 2 else 1), lambda t, k: xbc[:, k, t * P:t * P + P], first)
        transposed("scan", 10)
        pe.wait_ge(S("conv_done"), 4)
        pe.wait_ge(S("ld_made"), 1)
        mm(PM[:, 3, 0:64], tri_le[:, :], dts[:, 1, :], start=True, stop=True)
        mm(PM[:, 3, 64:128], tri_gt[:, :], dts[:, 1, :], start=True, stop=True)
        mm(PM[:, 3, 128:192], ones[:, :], dts[:, 1, :], start=True, stop=True).then_inc(S("scan_cum"), 1)
        for g in range(GROUPS):
            for t in range(TT):
                last = mm(PM[:, g, t * P:t * P + P], xbc[:, 8 + g, t * P:t * P + P], xbc[:, 10 + g, t * P:t * P + P],
                          start=True, stop=True)
        last.then_inc(S("scan_cb"), 1)
        pe.wait_ge(S("cum_read"), 1)
        for half in range(2):
            pe.wait_ge(S("y_attn_made"), TT * (half + 1))
            transposes("y_attn", 4 * half + 4, lambda t, k: vo[:, t, k * P:k * P + P], 4 * half)
        transposed("y_attn", 8)

        def segment(n):
            t, g = n // 2, n % 2
            pe.wait_ge(S("ldm_made"), t + 1)
            if n:
                pe.wait_ge(S("scan_dec"), n)
            for h in range(HG):
                last = mm(PM[:, h // 4, (h % 4) * P:(h % 4) * P + P], ldm[:, g * HG + h, :], tri_le[:, :],
                          start=True, stop=True)
            last.then_inc(S("scan_seg"), 1)

        pe.wait_ge(S("scan_exps"), 1)
        segment(0)
        for n in range(2 * TT):
            t, g = n // 2, n % 2
            first, *rest = step_pieces(n)
            piece(*first)
            if t:
                pe.wait_ge(S("hst_made"), min(n, 2 * (TT - 1)))
                if n == 2 * TT - 1:
                    pe.wait_ge(S("off_read"), n - 2)
                mm(PM[:, 3, :], xbc[:, 10 + g, t * P:t * P + P], hst[:, g * 512:g * 512 + 512],
                   start=True, stop=True).then_inc(S("scan_off"), 1)
            for p in rest:
                piece(*p)
            pe.wait_ge(S("scan_m"), n + 1)
            if n:
                pe.wait_ge(S("scan_y"), n)
            for h in range(HG):
                a = (g * HG + h) * HD
                last = mm(PM[:, 2, h * HD:h * HD + HD], dec[g][:, h, :], xdt[:, a:a + HD], start=True, stop=True)
            last.then_inc(S("scan_diag"), 1)
            if t < TT - 1:
                pe.wait_ge(S("xdte_made"), t + 1)
                if t:
                    pe.wait_ge(S("off_read"), n - 1)
                elif g:
                    pe.wait_ge(S("hst_made"), 1)
                mm(PM[:, 3, :], b_tm[:, t, g * P:g * P + P], xdte[:, g * 512:g * 512 + 512],
                   start=True, stop=True).then_inc(S("scan_st"), 1)
            if n < 2 * TT - 1:
                segment(n + 1)
        for p in SCAN_PIECES[3 * TT:]:
            piece(*p)
        pe.wait_ge(S("y_ssm_made"), TT)
        transposes("y_ssm", 8, lambda t, k: yt[:, t, k * P:k * P + P])
        transposed("y_ssm", 8)
        chunks("wout_s", 2, False)

        tiles_and_units("mix0", "qi", 512)
        narrow("kiw", 80)
        two_units("qi2", 0, 0, 0, 2, False)
        turn_narrow("kiw", 80, PM[:, 0, :])
        pe.wait_ge(S("ki_roped"), 1)
        for half in range(2):
            pe.wait_ge(S("qi_roped"), half + 1)
            transposes("qi", 4 * half + 4, lambda t, k: qi_tm[:, t, k * P:k * P + P], 4 * half)
        transposes("ki", 1, lambda t, k: kiw[:, t, 0:P])
        transposed("ki", 1)
        for h in range(H1):
            p0 = HD * (h % 2)
            for t in range(1, TT):
                if h:
                    pe.wait_ge(S("idx_relu"), 3 * (h - 1) + t)
                mm(PM[:, t - 1, 0:(t + 1) * P], qit[p0:p0 + HD, h // 2, t * P:t * P + P],
                   kit[p0:p0 + HD, 0:(t + 1) * P], start=True, stop=True).then_inc(S("idx_dots"), 1)
            piece(*INDEX_PIECES[h])
        two_units("v2", 0, 0, 0, 2, False)
        chunks("gates", 3, True)
        pe.wait_ge(S("qk_roped"), 1)
        transposes("qk", 8, lambda t, k: qk_tm[:, t, k * P:k * P + P])
        transposed("qk", 8)

        def logits(n, q, k, bias):
            X = PX[n % 2]
            for t in (3, 2, 0, 1):
                b, c0 = QB_AT[t]
                w = (t + 1) * P
                mm(X[:, b, c0:c0 + w], q(t), k(w), start=t != 0, stop=False, skip_group_check=True)
                bw = bias(t)
                last = mm(X[:, b, c0 + w - bw.shape[1]:c0 + w], identr[:, :], bw, start=False, stop=t != 2,
                          skip_group_check=True)
                if t != 2:
                    last.then_inc(S("att_logits"), 1)

        def probs_taken(n):
            pe.wait_ge(S("probs_s"), n)
            pe.wait_ge(S("probs_v"), n)

        def turn_probs(n, p):
            X = PX[n % 2]
            pe.wait_ge(S("att_exps"), 4 * n + 4)
            at_block = 0
            for t in (3, 2, 0, 1):
                for j in range(t + 1):
                    last = nc.tensor.transpose(X[:, at_block // 4, (at_block % 4) * P:(at_block % 4) * P + P],
                                               p[n % 2][:, QB_FIRST[t] + j * P:QB_FIRST[t] + j * P + P], ident[:, :])
                    at_block += 1
            last.then_inc(S("att_turned"), 1)

        def values(n, pt, v):
            c0 = 256 * (n % 2)
            probs_taken(n + 1)
            if n:
                pe.wait_ge(S("att_out"), n)
            for t in range(TT):
                for j in range(t + 1):
                    a = QB_FIRST[t] + j * P
                    last = mm(PM[:, 3, c0 + t * HD:c0 + t * HD + HD], pt[n % 2][:, a:a + P], v(j),
                              start=j == 0, stop=j == t)
            last.then_inc(S("att_pv"), 1)

        pe.wait_ge(S("bias_made"), 3)
        phase_done(pe, "gates")
        for h in range(A_H + 2):
            if h < A_H:
                if h >= 2:
                    probs_taken(h - 1)
                p0, f = HD * (h % 2), h // 2
                logits(h, lambda t: qkt[p0:p0 + HD, f, t * P:t * P + P], lambda w: qkt[p0:p0 + HD, 4 + f, 0:w],
                       lambda t: bias_q[:, t, 0:(t + 1) * P] if t else mask_q[:, :])
            if 1 <= h <= A_H:
                turn_probs(h - 1, pr)
            if h >= 2:
                values(h - 2, prt, lambda j: v2[:, j, (h - 2) * HD:(h - 1) * HD])
        pe.wait_ge(S("att_out"), A_H)
        transposes("attn", 4, lambda t, k: v2[:, t, k * P:k * P + P])
        transposed("attn", 4)
        pe.wait_ge(S("conv2_done"), 4)
        chunks("wo2", 2, False)
        tile_transposes("ffn0")
        transposed("ffn0", 8)
        mlp("mlp0", 0)

        tiles_and_units("mix1", "dq", Q_RANK)
        two_units("dkv", 0, 0, 0, 2, False, KV_RANK + 32)
        pe.wait_ge(S("cq_made"), TT)
        transposes("cq", 3, lambda t, k: cq[:, t, k * P:k * P + P])
        pe.wait_ge(S("ckv_made"), TT)
        transposes("ckv", 2, lambda t, k: kva[:, t, k * P:k * P + P])
        transposed("ckv", 2)
        u0 = PH["uq"][0]
        for n in range(3):
            unit_wait(u0 + n)
            for t in range(TT):
                bank_wait("uq", t, n)
                full(tm(PD[t], 512, (hhi, hlo), 0, (u0 + n) % 2, 3, 512, 0, True, True, t), t)
        u0 = PH["ukv"][0]
        for n in range(2):
            unit_wait(u0 + n)
            for r in range(2):
                for t in range(TT):
                    bank_wait("ukv", t, 2 * n + r)
                    last = tm(PD[t], 512, (hhi, hlo), 3, (u0 + n) % 2, 2, 1024, 512 * r, True, True, t)
                    if t == 3 and r == 0:
                        last.then_inc(S("bank_full3"), 1)
                    else:
                        full(last, t)
        pe.wait_ge(S("mla_roped"), 1)
        phase_done(pe, "ukv")

        def turn_qk(h, m):
            pe.wait_ge(S("tr_read"), TR["heads"][0] + 2 * h + m)
            for t in range(TT):
                src = k_tm[:, t, h, :] if m else q_tm[:, t, h * C_QK:h * C_QK + C_QK]
                last = nc.tensor.transpose(PDT[0:C_QK, 3, t * P:t * P + P], src, ident[:, :])
            last.then_inc(S("tr_done"), 1)

        for h in range(2):
            turn_qk(h, 0)
            turn_qk(h, 1)
        for h in range(C_H + 2):
            n = A_H + h
            if h < C_H:
                probs_taken(n - 1)
                pe.wait_ge(S("tr_read"), TR["heads"][0] + 2 * h + 2)
                qh, kh = qth[h % 2], kth[h % 2]
                logits(n, lambda t: qh[0:C_QK, t * P:t * P + P], lambda w: kh[0:C_QK, 0:w], lambda t: mask_q[:, :])
            if h + 2 < C_H:
                turn_qk(h + 2, 0)
            if 1 <= h <= C_H:
                turn_probs(n - 1, pr3)
            if h + 2 < C_H:
                turn_qk(h + 2, 1)
            if h >= 2:
                values(n - 2, prt3, lambda j: v3[:, j, (h - 2) * HD:(h - 1) * HD])
        pe.wait_ge(S("att_out"), A_H + C_H)
        transposes("lat", 8, lambda t, k: v3[:, t, k * P:k * P + P])
        transposed("lat", 8)
        chunks("wo3", 2, False)
        tile_transposes("ffn1")
        transposed("ffn1", 8)
        mlp("mlp1", 1)

    @block.scalar
    def _(act):
        def hi(i, base, stride):
            if isinstance(i, int):
                i, base = 0, i * stride + base
                if base >= PH["end"][0]:
                    return
            act.wait_ge(S(f"w_loaded{base % 2}"), i * (8 * stride) + 16 * (base // 2 + 1))
            if base >= 2:
                act.wait_ge(S("w_used"), i * stride + (base - 1))
            nc.scalar.activation(whi[base % 2][:, :], wraw[base % 2][:, :], ACT.Copy).then_inc(S("w_hi"), 1)

        def rounds(name, n, dst=None, func=ACT.Copy, scale=1.0, unrolled=False):
            u0 = PH[name][0]

            def body(i):
                hi(i, u0 + 1, 2)
                hi(i, u0 + 2, 2)
                for b in range(4):
                    if dst is not None:
                        full_wait(act, name, b, i, i * 2 + (u0 + 1))
                        nc.scalar.activation(dst(i, b), PD[b], func, scale=scale).then_inc(S(f"bank_free{b}"), 1)
            if unrolled:
                for i in range(n):
                    body(i)
            else:
                loop(act, n, body)

        def split_tiles(name, nk, gain, k0, after):
            act.wait_ge(S("w_used"), PH[after][0])
            for k in range(nk):
                act.wait_ge(S("tr_done"), TR[name][0] + k + 1)
                nc.scalar.activation(hhi[:, k0 + k, :], PM[:, k % 4, :], ACT.Copy, scale=gain(k))\
                    .then_inc(S("tr_hi"), 1)

        def copy_tiles(name, nk, dst, scale=lambda k: 1.0, func=ACT.Copy, first=0):
            for k in range(first, nk):
                act.wait_ge(S("tr_done"), TR[name][0] + k + 1)
                nc.scalar.activation(dst(k), PM[:, k % 4, :], func, scale=scale(k))\
                    .then_inc(S("tr_read"), 1)

        n_squares = [0]
        n_logs = [0]

        def square(src, total):
            n = n_squares[0]
            if n >= 2:
                act.wait_ge(S("squares"), n - 1)
            nc.scalar.activation(junk[:, n % 2, 0:src.shape[1]], src, ACT.Square, accum_out=total)\
                .then_inc(S("squares"), 1)
            n_squares[0] += 1

        def inverse_rms(s, t, src, d=DM, first_half=False):
            square(src, stat[:, s, t:t + 1])
            act.wait_ge(S("squares"), n_squares[0])
            nc.scalar.activation(stat[:, s, t:t + 1], stat[:, s, t:t + 1], ACT.Ln, scale=1.0 / d,
                                 bias=stat0[:, s, t:t + 1] if first_half else eps[:, :]).then_inc(S("logs"), 1)
            n_logs[0] += 1
            act.wait_ge(S("logs"), n_logs[0])
            nc.scalar.activation(rstd[:, s, t:t + 1], stat[:, s, t:t + 1], ACT.Exp, scale=-0.5)\
                .then_inc(S(f"rms{s}"), 1)

        def half_square(s, t, src):
            square(src, stat0[:, s, t:t + 1])
            act.wait_ge(S("squares"), n_squares[0])
            nc.scalar.activation(stat0[:, s, t:t + 1], stat0[:, s, t:t + 1], ACT.Identity, scale=1.0 / DM,
                                 bias=eps[:, :]).then_inc(S("logs"), 1)
            n_logs[0] += 1

        def norm_tiles(s, result, x_ready, name, after, early=None):
            for step, t in NORM_ORDER:
                if step == "A":
                    inverse_rms(s, t, result(t), first_half=True)
                    if t == TT - 1 and early is not None:
                        hi(0, early, 0)
                elif step == "B":
                    act.wait_ge(S(x_ready), t + 1)
                    inverse_rms(s + 1, t, xres[:, t, :])
                else:
                    if t == 0:
                        act.wait_ge(S("w_used"), PH[after][0])
                    for q in range(2):
                        n = 2 * t + q
                        act.wait_ge(S("tr_done"), TR[name][0] + n + 1)
                        nc.scalar.activation(hhi[:, 4 * q:4 * q + 4, t * P:t * P + P],
                                             PM[:, n % 4, :].rearrange("p (k c) -> p k c", k=4), ACT.Copy)\
                            .then_inc(S("tr_hi"), 1)

        def output_layer(name, s, m):
            u0 = PH[name][0]
            hi(0, u0 + 1, 0)
            hi(0, u0 + 2, 0)
            for b in range(4):
                full_wait(act, name, b, 0, u0 + 1)
                half_square(s, b, PD[b])
                nc.scalar.activation(m[:, b, 0:512], PD[b], ACT.Copy).then_inc(S(f"bank_free{b}"), 1)
            hi(0, u0 + 3, 0)
            hi(0, u0 + 4, 0)

        def second_half(name):
            def result(t):
                full_wait(act, name, t, 1, PH[name][0] + 3)
                return PD[t]
            return result

        def mlp(name, layer):
            u0 = PH[name][0]

            def up(first, r, i, m):
                hi(i, u0 + first + 1, 8)
                hi(i, u0 + first + 2, 8)
                base = m * 4 + 32 * layer

                def relu(b):
                    full_wait(act, name, b, r, i * 8 + (u0 + first + 1))
                    if b >= 2:
                        act.wait_ge(S("hidden_ready"), base + (b - 1))
                    nc.scalar.activation(mh_r[:, b % 2, :], PD[b], ACT.Relu).then_inc(S(f"bank_free{b}"), 1)

                def part(b):
                    act.wait_ge(S("hidden_sq"), base + (b + 1))
                    nc.scalar.activation(mh_hi[MPAR[first]][:, b, :], mh_r[:, b % 2, :], ACT.Copy)\
                        .then_inc(S("hidden_hi"), 1)
                if not (isinstance(m, int) and m == 0):
                    act.wait_ge(S("hidden_ready"), base)
                relu(0)
                relu(1)
                part(0)
                relu(2)
                part(1)
                relu(3)
                part(2)
                part(3)

            def down(first, i):
                hi(i, u0 + first + 1, 8)
                hi(i, u0 + first + 2, 8)

            MPAR = {0: 0, 2: 1, 6: 0}
            up(0, 0, 0, 0)
            with act.Fori(0, 3) as i:
                up(2, i * 6 + 1, i, i * 2 + 1)
                down(4, i)
                up(6, i * 6 + 4, i, i * 2 + 2)
                down(8, i)
            up(2, 19, 3, 7)
            down(4, 3)
            down(6, 3)

        def mlp_sums(name, s):
            for h in range(2):
                def result(t):
                    act.wait_ge(S(f"bank_free{t}"), PH[name][1][t] + 23 + h)
                    return mixm[:, t, 512 * h:512 * h + 512]
                if h == 0:
                    for t in range(TT):
                        half_square(s, t, result(t))
            return result

        act.wait_ge(S("tr_done"), 1)
        nc.scalar.activation(silu_c[:, :, :], PM[:, 3, 0:8].unsqueeze(2).to_broadcast([P, KT, P]), ACT.Silu)\
            .then_inc(S("c_ready"), 1)
        nc.scalar.preload_act_table_set("natural_log_exp_and_others")
        act.wait_ge(S("x_loaded"), 16)
        act.wait_ge(S("filled"), 5)
        for t in range(TT):
            inverse_rms(0, t, xres[:, t, :])
        act.wait_ge(S("ada_used"), 2)
        hi(0, 0, 0)
        split_tiles("h", 8, lambda k: 1.0, 0, "ada_ss")
        rounds("q", 2, lambda i, b: dyn(qt, i, b), scale=HD ** -0.5, unrolled=True)
        rounds("k", 2, lambda i, b: dyn(kt, i, b))
        rounds("v", 2, lambda i, b: vo[:, b, bass.ds(i * 512, 512)])

        def sb_head(h):
            for n in range(3):
                a = slice(SB_FIRST[n], SB_FIRST[n] + SB_WIDE[n])
                act.wait_ge(S("sb_clamped"), 3 * h + n + 1)
                nc.scalar.activation(sb_l[:, a], sb_l[:, a], ACT.Exp).then_inc(S("sb_exp"), 1)
                act.wait_ge(S("sb_exp"), 3 * h + n + 1)
                nc.scalar.activation(sb_l[:, a], sb_l[:, a], ACT.Ln, bias=1.0).then_inc(S("sb_ln"), 1)
            if h:
                act.wait_ge(S("sb_tail"), 3 * h)
            for n in range(3):
                a = slice(SB_FIRST[n], SB_FIRST[n] + SB_WIDE[n])
                act.wait_ge(S("sb_softplus"), 3 * h + n + 1)
                nc.scalar.activation(sb_hi[:, a], sb_l[:, a], ACT.Copy).then_inc(S("sb_high"), 1)
            after_piece(*SB_PIECES[3 * h])
            after_piece(*SB_PIECES[3 * h + 1])
            if h:
                act.wait_ge(S("sb_pv"), h)
            for n in range(3):
                a = slice(SB_FIRST[n], SB_FIRST[n] + SB_WIDE[n])
                act.wait_ge(S("sb_tail"), 3 * h + n + 1)
                nc.scalar.activation(sb_w[:, a], PM[:, n, 0:SB_WIDE[n]], ACT.Exp).then_inc(S("sb_weights"), 1)
            after_piece(*SB_PIECES[3 * h + 2])

        def after_piece(name, r, h, b):
            u = PH[name][0] + 2 * r + h
            if (b == 3 or name == "dt") and (name, r, h) not in (("wout_a", 1, 1), ("z_attn", 0, 1), ("qk2", 1, 1)):
                hi(0, u + 2, 0)
            if h == 1 and name != "z_attn":
                full_wait(act, name, b, r, u)
                if name == "xbc":
                    dst = xbc[:, 4 * r + b, 3:SEQ + 3]
                else:
                    dst = {"z_ssm": zs, "wout_a": mix, "qk2": qk_tm}[name][:, b, 512 * r:512 * r + 512]
                nc.scalar.activation(dst, PD[b], ACT.Copy).then_inc(S(f"bank_free{b}"), 1)

        act.wait_ge(S("angles"), 1)
        nc.scalar.activation(sinall[:, :, :], ang[:, :, :], ACT.Sin).then_inc(S("sines"), 1)
        nc.scalar.activation(ang_s[:, :, :], ang[:, :, :], ACT.Sin, scale=0.5).then_inc(S("sines"), 1)
        hi(0, PH["xbc"][0] + 1, 0)
        nc.scalar.preload_act_table_set("natural_log_exp_and_others")
        for h in range(H1):
            sb_head(h)
        act.wait_ge(S("dt_clamped"), 1)
        nc.scalar.activation(dts[:, 0, :], dts[:, 0, :], ACT.Exp).then_inc(S("dt_exp"), 1)
        nc.scalar.activation(small[:, 16:32], small[:, 16:32], ACT.Exp).then_inc(S("dt_exp"), 1)
        act.wait_ge(S("dt_exp"), 2)
        nc.scalar.activation(dts[:, 0, :], dts[:, 0, :], ACT.Ln, bias=1.0).then_inc(S("dt_ln"), 1)
        u0 = PH["z_attn"][0]
        hi(0, u0 + 3, 0)
        act.wait_ge(S("sb_out"), H1)
        for t in range(TT):
            inverse_rms(1, t, vo[:, t, :])
        for ct in range(8, XBC_T):
            if ct == 8:
                act.wait_ge(S("conv_sum"), XBC_T)
            nc.scalar.activation(xbc[:, ct, 0:SEQ], xbc[:, ct, 0:SEQ], ACT.Silu).then_inc(S("conv_done"), 1)

        def turned_scan(first, end):
            copy_tiles("scan", min(end, 8), lambda k: yt[:, :, k * P:k * P + P], func=ACT.Silu, first=first)
            copy_tiles("scan", end, lambda k: b_tm[:, :, (k - 8) * P:(k - 7) * P], first=max(first, 8))

        turned_scan(0, 6)
        hi(0, u0 + 4, 0)
        for t in range(TT):
            act.wait_ge(S(f"bank_free{t}"), PH["z_attn"][1][t] + 1)
            nc.scalar.activation(za[:, t, 0:512], za[:, t, 0:512], ACT.Silu).then_inc(S("za_silu"), 1)
        phase_done(act, "z_ssm")
        for t in range(TT):
            nc.scalar.activation(zs[:, t, :], zs[:, t, :], ACT.Silu).then_inc(S("zs_silu"), 1)
        turned_scan(6, 10)
        for t in range(TT):
            full_wait(act, "z_attn", t, 1, u0 + 3)
            nc.scalar.activation(za[:, t, 512:DM], PD[t], ACT.Silu).then_inc(S(f"bank_free{t}"), 1)
        hi(0, u0 + 5, 0)
        split_tiles("y_attn", 8, lambda k: col_a[:, C_SBG + k:C_SBG + k + 1], 0, "wout_a")
        nc.scalar.preload_act_table_set("natural_log_exp_and_others")
        act.wait_ge(S("cum_read"), 1)
        nc.scalar.activation(dts[:, 2:5, :], dts[:, 2:5, :], ACT.Exp)\
            .then_inc(S("scan_exps"), 1)
        for n in range(2 * TT):
            act.wait_ge(S("scan_seg"), n + 1)
            if n >= 2:
                act.wait_ge(S("scan_diag"), n - 1)
            nc.scalar.activation(dec[n % 2][:, :, :].rearrange("p h l -> p (h l)"),
                                 PM[:, 0:2, :].rearrange("p a b -> p (a b)"), ACT.Exp).then_inc(S("scan_dec"), 1)
            if n % 2 == 0 and n:
                act.wait_ge(S("y_gated"), n // 2)
                inverse_rms(2, n // 2 - 1, yt[:, n // 2 - 1, :])
            for p in step_pieces(n):
                after_piece(*p)
        for p in SCAN_PIECES[3 * TT:]:
            after_piece(*p)
        act.wait_ge(S("y_gated"), TT)
        inverse_rms(2, TT - 1, yt[:, TT - 1, :])
        split_tiles("y_ssm", 8, lambda k: col_a[:, C_SSG + k:C_SSG + k + 1], 0, "wout_s")
        u0 = PH["wout_s"][0]
        for u in range(1, 5):
            hi(0, u0 + u, 0)
            if u == 3:
                for t in range(TT):
                    act.wait_ge(S("x2_made"), t + 1)
                    half_square(3, t, xres[:, t, 0:512])

        def second_sum(t):
            act.wait_ge(S("x2_made"), TT + t + 1)
            return xres[:, t, 512:DM]

        norm_tiles(3, second_sum, "first_out", "mix0", "qi", early=PH["qi"][0] + 1)
        hi(0, PH["kiw"][0], 0)
        for b in range(4):
            full_wait(act, "qi", b, 0, PH["qi"][0] + 1)
            nc.scalar.activation(qi_tm[:, b, 0:512], PD[b], ACT.Copy).then_inc(S(f"bank_free{b}"), 1)
        hi(0, PH["qi2"][0], 0)
        rounds("qi2", 1, lambda i, b: qi_tm[:, b, 512:DM])
        copy_tiles("qi", 8, lambda k: qit[:, k, :])
        copy_tiles("ki", 1, lambda k: kit[:, :])
        hi(0, PH["qk2"][0] + 1, 0)
        for h in range(H1):
            if h >= 2:
                act.wait_ge(S("idx_sum"), 3 * (h - 1))
            for t in range(1, TT):
                act.wait_ge(S("idx_dots"), 3 * h + t)
                nc.scalar.activation(relu_s[:, h % 2, IDX_AT[t]:IDX_AT[t] + (t + 1) * P], PM[:, t - 1, 0:(t + 1) * P],
                                     ACT.Relu).then_inc(S("idx_relu"), 1)
            after_piece(*INDEX_PIECES[h])
        rounds("v2", 1, lambda i, b: v2[:, b, :])
        act.wait_ge(S("idx_sum"), 3 * H1)
        rounds("gates", 3, lambda i, b: [gb[:, b, :], gc[:, b, 2:SEQ + 2], xi[:, b, :]][i], unrolled=True)
        copy_tiles("qk", 8, lambda k: qkt[:, k, :], lambda k: HD ** -0.5 if k < 4 else 1.0)

        def convolution2_high(f):
            act.wait_ge(S("w_used"), PH["wo2"][0])
            act.wait_ge(S("conv2_out"), f + 1)
            nc.scalar.activation(hhi[:, 4 + f, :], ca[:, f, :], ACT.Copy).then_inc(S("conv2_hi"), 1)

        def exps(n, p, m, d):
            s = n % 2
            if n >= 2:
                act.wait_ge(S("att_turned"), n - 1)
            if n >= 4:
                act.wait_ge(S("att_out"), n - 3)
            for q, t in enumerate((3, 2, 0, 1)):
                b, c0 = QB_AT[t]
                w = (t + 1) * P
                act.wait_ge(S("att_max"), 4 * n + (1, 3, 3, 4)[q])
                nc.scalar.activation(p[s][:, QB_FIRST[t]:QB_FIRST[t] + w], PX[s][:, b, c0:c0 + w], ACT.Exp,
                                     bias=m[:, n % 4, t:t + 1], accum_out=d[:, n % 4, t:t + 1]).then_inc(S("att_exps"), 1)

        def turned(n, pt):
            act.wait_ge(S("att_turned"), n + 1)
            if n >= 2:
                act.wait_ge(S("att_pv"), n - 1)
            nc.scalar.activation(pt[n % 2][:, 0:SEQ], PX[n % 2][:, 0, :], ACT.Copy).then_inc(S("probs_s"), 1)

        for h in range(A_H + 1):
            if h < A_H:
                exps(h, pr, mx, den)
            if h:
                turned(h - 1, prt)
            if 1 <= h < 5:
                convolution2_high(h - 1)
        split_tiles("attn", 4, lambda k: 1.0, 0, "wo2")
        output_layer("wo2", 5, mix2)
        norm_tiles(5, second_half("wo2"), "post_mix0", "ffn0", "mlp0")
        mlp("mlp0", 0)
        norm_tiles(7, mlp_sums("mlp0", 7), "post_ffn0", "mix1", "dq", early=PH["dq"][0] + 1)
        u0 = PH["dq"][0]
        hi(0, u0 + 2, 0)
        for t in range(TT):
            full_wait(act, "dq", t, 0, u0 + 1)
            nc.scalar.activation(cq[:, t, :], PD[t][:, 0:Q_RANK], ACT.Copy).then_inc(S(f"bank_free{t}"), 1)
        hi(0, u0 + 3, 0)
        for t in range(TT):
            act.wait_ge(S(f"bank_free{t}"), PH["dkv"][1][t])
            inverse_rms(9, t, cq[:, t, :], Q_RANK)
        hi(0, u0 + 4, 0)
        for t in range(TT):
            full_wait(act, "dkv", t, 0, u0 + 3)
            nc.scalar.activation(kva[:, t, :], PD[t][:, 0:KV_RANK + 32], ACT.Copy).then_inc(S(f"bank_free{t}"), 1)
            act.wait_ge(S(f"bank_free{t}"), PH["uq"][1][t])
            inverse_rms(10, t, kva[:, t, 0:KV_RANK], KV_RANK)
        split_tiles("cq", 3, lambda k: col_b[:, C_QN + k:C_QN + k + 1], 0, "uq")
        split_tiles("ckv", 2, lambda k: col_b[:, C_KN + k:C_KN + k + 1], 3, "uq")
        u0 = PH["uq"][0]
        for n in range(3):
            hi(0, u0 + n + 1, 0)
            for t in range(TT):
                full_wait(act, "uq", t, n, u0 + n)
                nc.scalar.activation(q_tm[:, t, 512 * n:512 * n + 512], PD[t], ACT.Copy)\
                    .then_inc(S(f"bank_free{t}"), 1)
        u0 = PH["ukv"][0]
        for n in range(2):
            hi(0, u0 + n + 1, 0)
            for r in range(2):
                for t in range(TT):
                    if t == 3 and r == 0:
                        act.wait_ge(S("bank_full3"), PH["ukv"][2][3] + n + 1)
                    else:
                        full_wait(act, "ukv", t, 2 * n + r, u0 + n)
                    h0 = 8 * n + 4 * r
                    kv = PD[t].rearrange("p (h d) -> p h d", h=4)
                    nc.scalar.activation(k_tm[:, t, h0:h0 + 4, 0:C_NOPE], kv[:, :, 0:64], ACT.Copy)
                    nc.scalar.activation(v3[:, t, h0 * HD:(h0 + 4) * HD].rearrange("p (h d) -> p h d", d=HD),
                                         kv[:, :, 64:128], ACT.Copy).then_inc(S(f"bank_free{t}"), 1)

        def turned_q(h):
            act.wait_ge(S("tr_done"), TR["heads"][0] + 2 * h + 1)
            nc.scalar.activation(qth[h % 2][0:C_QK, :], PDT[0:C_QK, 3, :], ACT.Copy, scale=C_QK ** -0.5)\
                .then_inc(S("tr_read"), 1)

        turned_q(0)
        turned_q(1)
        for h in range(C_H + 1):
            if h + 2 < C_H:
                turned_q(h + 2)
            if h < C_H:
                exps(A_H + h, pr3, mx3, den3)
            if h:
                turned(A_H + h - 1, prt3)
        split_tiles("lat", 8, lambda k: 1.0, 0, "wo3")
        output_layer("wo3", 11, mix3)
        norm_tiles(11, second_half("wo3"), "post_mix1", "ffn1", "mlp1")
        mlp("mlp1", 1)
        sums = mlp_sums("mlp1", 13)
        for t in range(TT):
            inverse_rms(13, t, sums(t), first_half=True)

    @block.gpsimd
    def _(pool):
        g = nc.gpsimd

        def lo(i, base, stride):
            if base >= PH["end"][0]:
                return
            pool.wait_ge(S("w_hi"), i * stride + (base + 1))
            g.tensor_tensor(wlo[base % 2][:, :], wraw[base % 2][:, :], fl(whi[base % 2][:, :]), ALU.subtract)\
                .then_inc(S("w_split"), 1)

        def units(name, to):
            for u in range(PH[name][0] + 1, PH[to][0] + 1):
                lo(0, u, 0)

        def pairs(name, n):
            u0 = PH[name][0]

            def body(i):
                lo(i, u0 + 1, 2)
                lo(i, u0 + 2, 2)
            loop(pool, n, body)

        g.memset(ident[:, :], 0.0).then_inc(S("filled"), 1)
        g.memset(ones[:, :], 1.0).then_inc(S("filled"), 1)
        g.memset(scratch[:, :], 0.0).then_inc(S("filled"), 1)
        g.memset(scratch1[:, :], -1.0).then_inc(S("filled"), 1)
        g.memset(eps[:, :], EPS).then_inc(S("filled"), 1)
        pool.wait_ge(S("filled"), 5)
        g.affine_select(out=ident[:, :], in_=ident[:, :], compare_op=ALU.not_equal, fill=1.0, base=0,
                        pattern=[[-1, P]], channel_multiplier=1).then_inc(S("masks"), 1)
        g.affine_select(out=identr[:, :], in_=scratch[:, :], compare_op=ALU.not_equal, fill=1.0, base=0,
                        pattern=[[-1, P]], channel_multiplier=1)
        g.affine_select(out=tri_le[:, :], in_=ones[:, :], compare_op=ALU.is_ge, fill=0.0, base=0,
                        pattern=[[1, P]], channel_multiplier=-1)
        g.affine_select(out=tri_gt[:, :], in_=ones[:, :], compare_op=ALU.is_gt, fill=0.0, base=0,
                        pattern=[[-1, P]], channel_multiplier=1)
        g.affine_select(out=neg_ge[:, :], in_=scratch1[:, :], compare_op=ALU.is_ge, fill=0.0, base=0,
                        pattern=[[-1, P]], channel_multiplier=1)
        g.affine_select(out=mask_t[:, :], in_=scratch[:, :], compare_op=ALU.is_gt, fill=NEG, base=0,
                        pattern=[[1, P]], channel_multiplier=-1)
        g.affine_select(out=mask_q[:, :], in_=scratch[:, :], compare_op=ALU.is_ge, fill=NEG, base=0,
                        pattern=[[-1, P]], channel_multiplier=1)
        g.tensor_copy(neg_one[:, :], scratch1[:, :]).then_inc(S("masks"), 1)
        for j in range(8):
            g.memset(freq[:, j:j + 1], THETA ** (-2.0 * j / 16))
        for j in range(16):
            g.memset(freq[:, 8 + j:9 + j], THETA ** (-2.0 * j / 32)).then_inc(S("freqs"), 1)
        pool.wait_ge(S("ada_used"), 4)
        lo(0, 0, 0)
        pairs("q", 2)
        pairs("k", 2)
        pairs("v", 2)
        g.memset(xbc[:, :, 0:3], 0.0).then_inc(S("pads"), 1)
        pairs("xbc", 3)
        pairs("z_ssm", 2)
        lo(0, PH["dt"][0] + 1, 0)
        pairs("z_attn", 2)
        pairs("wout_a", 2)
        pairs("wout_s", 2)
        pairs("qi", 1)
        lo(0, PH["kiw"][0] + 1, 0)
        pairs("qi2", 1)
        pairs("qk2", 2)
        for t in range(1, TT):
            pool.wait_ge(S("idx_sum"), 3 * H1)
            g.affine_select(out=score[:, t, t * P:t * P + P], in_=score[:, t, t * P:t * P + P], compare_op=ALU.is_ge,
                            fill=DROPPED, base=0, pattern=[[-1, P]], channel_multiplier=1)\
                .then_inc(S("score_masked"), 1)
        pairs("v2", 1)
        g.memset(gc[:, :, 0:2], 0.0).then_inc(S("pads"), 1)
        pairs("gates", 3)
        pairs("wo2", 2)

        def mlp(name, layer):
            u0 = PH[name][0]
            pool.wait_ge(S(f"post_mix{layer}"), TT)
            g.memset(mixm[:, :, :], 0.0).then_inc(S("acc_zero"), 1)
            for u in (1, 2):
                lo(0, u0 + u, 0)
            with pool.Fori(0, 3) as i:
                for u in range(3, 11):
                    lo(i, u0 + u, 8)
            for u in range(27, 33):
                lo(0, u0 + u, 0)

        mlp("mlp0", 0)
        units("dq", "uq")
        units("uq", "wo3")
        pairs("wo3", 2)
        mlp("mlp1", 1)

    @block.vector
    def _(dve):
        v = nc.vector
        chained = [0]

        def link(ins):
            chained[0] += 1
            ins.then_inc(S("dve_chain"), 1)
            dve.wait_ge(S("dve_chain"), chained[0])

        def split_tiles(name, nk, gain, k0):
            for k in range(nk):
                dve.wait_ge(S("tr_hi"), TR[name][1] + k + 1)
                v.scalar_tensor_tensor(out=hlo[:, k0 + k, :], in0=PM[:, k % 4, :], scalar=gain(k),
                                       in1=fl(hhi[:, k0 + k, :]), op0=ALU.mult, op1=ALU.subtract)\
                    .then_inc(S("tr_read"), 1)

        def norm_tiles(s, order, first, onto_x, name, row_wait):
            dve.wait_ge(S("row_pre"), row_wait)
            for step, t in order:
                if step == "first":
                    first(t)
                elif step == "A":
                    dve.wait_ge(S(f"rms{s}"), t + 1)
                    onto_x(t)
                elif step == "B":
                    dve.wait_ge(S(f"rms{s + 1}"), t + 1)
                    v.scalar_tensor_tensor(out=xn[:, t, :], in0=xres[:, t, :], scalar=rstd[:, s + 1, t:t + 1],
                                           in1=row_c[:, :], op0=ALU.mult, op1=ALU.mult)\
                        .then_inc(S(f"{name}_made"), 1)
                else:
                    for q in range(2):
                        n = 2 * t + q
                        dve.wait_ge(S("tr_hi"), TR[name][1] + n + 1)
                        tile_lo = (slice(None), slice(4 * q, 4 * q + 4), slice(t * P, t * P + P))
                        v.tensor_tensor(hlo[tile_lo], PM[:, n % 4, :].rearrange("p (k c) -> p k c", k=4),
                                        fl(hhi[tile_lo]), ALU.subtract).then_inc(S("tr_read"), 1)

        def rope(view, heads, half, c, s, tmp, sem=None):
            for n, (out, a, b, op) in enumerate(rotation(view, heads, half, c, s, tmp)):
                ins = v.tensor_tensor(out, a, b, op)
                if n == 5 and sem is not None:
                    ins.then_inc(sem, 1)
                elif n in (3, 5):
                    link(ins)

        for j, c0 in enumerate((DM, DM + 512, 0, 512)):
            dve.wait_ge(S("ada_used"), 2 * j + 2)
            if j == 0:
                dve.wait_ge(S("rows_mod"), 32)
            v.tensor_tensor(mod[:, c0:c0 + 512], PD[j], b_row[:, c0:c0 + 512], ALU.add).then_inc(S(f"bank_free{j}"), 1)
            if j == 3:
                dve.wait_ge(S("bank_free3"), 1)
            if j < 2:
                dve.wait_ge(S(f"bank_free{j}"), 1)
                link(v.scalar_tensor_tensor(out=mod[:, c0:c0 + 512], in0=mod[:, c0:c0 + 512], scalar=1.0,
                                            in1=row_a[:, c0 - DM:c0 - DM + 512], op0=ALU.add, op1=ALU.mult))
            if j == 1:
                for t in range(TT):
                    dve.wait_ge(S("rms0"), t + 1)
                    v.scalar_tensor_tensor(out=xn[:, t, :], in0=xres[:, t, :], scalar=rstd[:, 0, t:t + 1],
                                           in1=mod[:, DM:2 * DM], op0=ALU.mult, op1=ALU.mult)\
                        .then_inc(S("h_scaled"), 1)
        for t in range(TT):
            dve.wait_ge(S("h_scaled"), t + 1)
            v.tensor_tensor(xn[:, t, :], xn[:, t, :], mod[:, 0:DM], ALU.add).then_inc(S("h_made"), 1)
        dve.wait_ge(S("params"), 16 * N_PARAMS)
        for j in range(2):
            dve.wait_ge(S("ada_used"), 8 + 2 * j + 2)
            v.tensor_tensor(gate[:, 512 * j:512 * j + 512], PD[j], row_b[:, 512 * j:512 * j + 512], ALU.add)\
                .then_inc(S(f"bank_free{j}"), 1)
        dve.wait_ge(S("tr_done"), 2)
        v.tensor_copy(col_a[:, 0:ROWS_A], PM[:, 2, 0:ROWS_A]).then_inc(S("tr_read"), 1)
        v.tensor_copy(col_b[:, 0:ROWS_B], PM[:, 2, P:P + ROWS_B]).then_inc(S("tr_read"), 1)
        split_tiles("h", 8, lambda k: 1.0, 0)
        dve.wait_ge(S("freqs"), 16)
        link(v.tensor_copy(pos_f[:, :], pos_i[:, :]))
        link(v.tensor_tensor(ang[:, :, :], pos_f[:, :].unsqueeze(2).to_broadcast([P, TT, 24]),
                             freq[:, :].unsqueeze(1).to_broadcast([P, TT, 24]), ALU.mult))
        link(v.tensor_scalar(ang_n[:, :, :], ang[:, :, :], 1.0 / (2 * math.pi), ROUNDER, ALU.mult, ALU.add))
        link(v.tensor_scalar(ang_n[:, :, :], ang_n[:, :, :], -ROUNDER, None, ALU.add))
        for part in TWO_PI:
            link(v.scalar_tensor_tensor(out=ang[:, :, :], in0=ang_n[:, :, :], scalar=-part, in1=ang[:, :, :],
                                        op0=ALU.mult, op1=ALU.add))
        v.tensor_scalar(ang[:, :, :], ang[:, :, :], PI_BELOW, -PI_BELOW, ALU.min, ALU.max).then_inc(S("angles"), 1)
        dve.wait_ge(S("sines"), 2)
        link(v.tensor_tensor(ang_s[:, :, :], ang_s[:, :, :], ang_s[:, :, :], ALU.mult))
        v.tensor_scalar(cosq[:, :, :], ang_s[:, :, 0:8], -2.0, 1.0, ALU.mult, ALU.add)
        v.tensor_scalar(cosm[:, :, :], ang_s[:, :, 8:24], -2.0, 1.0, ALU.mult, ALU.add)
        v.tensor_copy(sinq[:, :, :], sinall[:, :, 0:8])
        link(v.tensor_copy(sinm[:, :, :], sinall[:, :, 8:24]))

        def sb_emit(h):
            dve.wait_ge(S("sb_pv"), h + 1)
            v.tensor_copy(vo[:, :, h * HD:h * HD + HD],
                          PM[:, 3, (h % 2) * 256:(h % 2) * 256 + 256].rearrange("p (t d) -> p t d", t=TT))\
                .then_inc(S("sb_out"), 1)

        rows4 = [P, TT, H1]

        def narrow_out(name, n):
            dve.wait_ge(S("w_used"), PH[name][0] + 1)
            v.tensor_copy(tall[0:n, :], PD[3][0:n, :]).then_inc(S("bank_free3"), 1)

        def dt_raw():
            dve.wait_ge(S("dt_turned"), 1)
            v.tensor_tensor(dts[:, 5, :].rearrange("p (t h) -> p t h", t=TT),
                            PD[3][:, 0:64].rearrange("p (t h) -> p t h", t=TT),
                            small[:, 0:16].unsqueeze(1).to_broadcast(rows4), ALU.add).then_inc(S("bank_free3"), 1)
            dve.wait_ge(S("bank_free3"), PH["z_attn"][1][3])
            v.tensor_scalar(dts[:, 0, :], dts[:, 5, :], CLAMP, None, ALU.min).then_inc(S("dt_clamped"), 1)

        def convolution(ct):
            acc = conv_acc[:, ct % 2, :]
            dve.wait_ge(S(f"bank_free{ct % 4}"), PH["xbc"][1][ct % 4] + ct // 4 + 1)
            if ct == 0:
                dve.wait_ge(S("pads"), 1)
            if ct >= 2:
                dve.wait_ge(S("conv_sum"), ct - 1)
            col = [col_a[:, C_CW + 12 * j + ct:C_CW + 12 * j + ct + 1] for j in range(4)]
            link(v.tensor_scalar(acc, xbc[:, ct, 0:SEQ], col[0], col_a[:, C_CB + ct:C_CB + ct + 1], ALU.mult, ALU.add))
            for j in range(1, 3):
                link(v.scalar_tensor_tensor(out=acc, in0=xbc[:, ct, j:j + SEQ], scalar=col[j], in1=acc,
                                            op0=ALU.mult, op1=ALU.add))
            v.scalar_tensor_tensor(out=xbc[:, ct, 0:SEQ], in0=xbc[:, ct, 3:3 + SEQ], scalar=col[3], in1=acc,
                                   op0=ALU.mult, op1=ALU.add).then_inc(S("conv_sum"), 1)

        for h in range(H1):
            for n in range(3):
                a = slice(SB_FIRST[n], SB_FIRST[n] + SB_WIDE[n])
                dve.wait_ge(S("sb_z"), 3 * h + n + 1)
                if h:
                    dve.wait_ge(S("sb_split"), 3 * (h - 1) + n + 1)
                v.tensor_scalar(sb_l[:, a], PM[:, n, 0:SB_WIDE[n]], CLAMP, None, ALU.min).then_inc(S("sb_clamped"), 1)
            if h:
                sb_emit(h - 1)
            if h == dt_head + 1:
                dt_raw()
            for n in range(3):
                a = slice(SB_FIRST[n], SB_FIRST[n] + SB_WIDE[n])
                dve.wait_ge(S("sb_ln"), 3 * h + n + 1)
                v.tensor_tensor(sb_l[:, a], PM[:, n, 0:SB_WIDE[n]], sb_l[:, a], ALU.max).then_inc(S("sb_softplus"), 1)
            for n in range(3):
                a = slice(SB_FIRST[n], SB_FIRST[n] + SB_WIDE[n])
                dve.wait_ge(S("sb_high"), 3 * h + n + 1)
                v.tensor_tensor(sb_lo[:, a], sb_l[:, a], fl(sb_hi[:, a]), ALU.subtract).then_inc(S("sb_split"), 1)
            if h == dt_head:
                narrow_out("dt", H1)
            if 3 <= h < 3 + XBC_T:
                convolution(h - 3)
        sb_emit(H1 - 1)
        for b in range(TT):
            full_wait(dve, "z_attn", b, 0, PH["z_attn"][0] + 1)
            v.tensor_copy(za[:, b, 0:512], PD[b]).then_inc(S(f"bank_free{b}"), 1)
        dve.wait_ge(S("dt_ln"), 1)
        link(v.tensor_tensor(dts[:, 0, :], dts[:, 5, :], dts[:, 0, :], ALU.max))
        v.scalar_tensor_tensor(out=dts[:, 1, :].rearrange("p (t h) -> p t h", t=TT),
                               in0=dts[:, 0, :].rearrange("p (t h) -> p t h", t=TT), scalar=-1.0,
                               in1=small[:, 16:32].unsqueeze(1).to_broadcast(rows4), op0=ALU.mult, op1=ALU.mult)\
            .then_inc(S("ld_made"), 1)
        dve.wait_ge(S("rms1"), TT)

        def gated_attention(half):
            for t in range(TT):
                if half:
                    dve.wait_ge(S(f"bank_free{t}"), PH["z_attn"][1][t] + 2)
                else:
                    dve.wait_ge(S("za_silu"), t + 1)
                cols = slice(512 * half, 512 * half + 512)
                v.scalar_tensor_tensor(out=vo[:, t, cols], in0=vo[:, t, cols], scalar=rstd[:, 1, t:t + 1],
                                       in1=za[:, t, cols], op0=ALU.mult, op1=ALU.mult).then_inc(S("y_attn_made"), 1)

        gated_attention(0)
        dve.wait_ge(S("scan_cb"), 1)
        for g in range(GROUPS):
            op = v.tensor_tensor(cbm[:, 4 * g:4 * g + 4, :], PM[:, g, :].rearrange("p (t l) -> p t l", t=TT),
                                 tri_le[:, :].unsqueeze(1).to_broadcast([P, TT, P]), ALU.mult)
        op.then_inc(S("cbm_made"), 1)
        dve.wait_ge(S("scan_cum"), 1)
        v.tensor_copy(dts[:, 2:5, :], PM[:, 3, 0:192].rearrange("p (a b) -> p a b", a=3)).then_inc(S("cum_read"), 1)
        gated_attention(1)

        def per_head(row, t, g, n=HG):
            a = t * H1 + g * HG
            return dts[:, row, a:a + n].unsqueeze(2).to_broadcast([P, n, HD])

        def heads(ap):
            return ap.rearrange("p (h d) -> p h d", d=HD)

        def log_decays(t):
            v.tensor_tensor(ldm[:, :, :], tri_gt[:, :].unsqueeze(1).to_broadcast([P, H1, P]),
                            dts[:, 1, t * H1:t * H1 + H1].unsqueeze(2).to_broadcast([P, H1, P]), ALU.mult)\
                .then_inc(S("ldm_made"), 1)

        log_decays(0)
        split_tiles("y_attn", 8, lambda k: col_a[:, C_SBG + k:C_SBG + k + 1], 0)
        dve.wait_ge(S("cbm_made"), 1)
        dve.wait_ge(S("scan_exps"), 1)
        dve.wait_ge(S("zs_silu"), TT)
        for t in range(TT):
            if t:
                dve.wait_ge(S("scan_diag"), 2 * t)
                dve.wait_ge(S("xdte_made"), t)
            link(v.tensor_tensor(heads(xdt[:, :]), heads(yt[:, t, :]), per_head(0, t, 0, H1), ALU.mult))
            if t < TT - 1:
                if t:
                    dve.wait_ge(S("scan_st"), 2 * t)
                v.tensor_tensor(heads(xdte[:, :]), heads(xdt[:, :]), per_head(3, t, 0, H1), ALU.mult)\
                    .then_inc(S("xdte_made"), 1)
            for g in range(GROUPS):
                n = 2 * t + g
                cols = slice(g * 512, g * 512 + 512)
                dve.wait_ge(S("scan_dec"), n + 1)
                v.tensor_tensor(dec[g][:, :, :], dec[g][:, :, :],
                                cbm[:, 4 * g + t, :].unsqueeze(1).to_broadcast([P, HG, P]), ALU.mult)\
                    .then_inc(S("scan_m"), 1)
                if g and t < TT - 1:
                    log_decays(t + 1)
                if n:
                    dve.wait_ge(S("scan_y"), n)
                link(v.tensor_tensor(heads(xd[:, :]), heads(yt[:, t, cols]),
                                     small[:, 32 + g * HG:32 + g * HG + HG].unsqueeze(2).to_broadcast([P, HG, HD]),
                                     ALU.mult))
                if t:
                    dve.wait_ge(S("scan_off"), n - 1)
                    v.tensor_tensor(heads(off[:, :]), heads(PM[:, 3, :]), per_head(2, t, g), ALU.mult)\
                        .then_inc(S("off_read"), 1)
                    dve.wait_ge(S("off_read"), n - 1)
                    link(v.tensor_tensor(xd[:, :], xd[:, :], off[:, :], ALU.add))
                dve.wait_ge(S("scan_diag"), n + 1)
                v.tensor_tensor(yt[:, t, cols], PM[:, 2, :], xd[:, :], ALU.add).then_inc(S("scan_y"), 1)
                if t < TT - 1:
                    if t:
                        link(v.tensor_tensor(heads(hst[:, cols]), heads(hst[:, cols]), per_head(4, t, g), ALU.mult))
                    dve.wait_ge(S("scan_st"), n + 1)
                    if t:
                        v.tensor_tensor(hst[:, cols], hst[:, cols], PM[:, 3, :], ALU.add).then_inc(S("hst_made"), 1)
                    else:
                        v.tensor_copy(hst[:, cols], PM[:, 3, :]).then_inc(S("hst_made"), 1)
            dve.wait_ge(S("scan_y"), 2 * t + 2)
            v.tensor_tensor(yt[:, t, :], yt[:, t, :], zs[:, t, :], ALU.mult).then_inc(S("y_gated"), 1)
        for t in range(TT):
            dve.wait_ge(S("rms2"), t + 1)
            v.tensor_scalar(yt[:, t, :], yt[:, t, :], rstd[:, 2, t:t + 1], None, ALU.mult).then_inc(S("y_ssm_made"), 1)
        split_tiles("y_ssm", 8, lambda k: col_a[:, C_SSG + k:C_SSG + k + 1], 0)
        dve.wait_ge(S("x_again"), 16)

        def add_mix(b, i):
            full_wait(dve, "wout_s", b, i, PH["wout_s"][0] + 2 * i + 1)
            cols = slice(512 * i, 512 * i + 512)
            m = mix[:, b, cols]
            v.tensor_tensor(m, PD[b], m, ALU.add).then_inc(S(f"bank_free{b}"), 1)
            dve.wait_ge(S(f"bank_free{b}"), PH["wout_s"][1][b] + i + 1)
            link(v.tensor_tensor(m, m, gate[:, cols], ALU.mult))
            v.tensor_tensor(xres[:, b, cols], xres[:, b, cols], m, ALU.add).then_inc(S("x2_made"), 1)

        for b in range(4):
            add_mix(b, 0)

        def last_norm(t):
            v.scalar_tensor_tensor(out=xres[:, t, :], in0=xres[:, t, :], scalar=rstd[:, 3, t:t + 1], in1=row_a[:, :],
                                   op0=ALU.mult, op1=ALU.mult).then_inc(S("first_out"), 1)

        dve.wait_ge(S("row_f"), 16)
        norm_tiles(3, FIRST_ORDER, lambda t: add_mix(t, 1), last_norm, "mix0", 16)

        def post_norm(s, m, row, sem, psum=None):
            def step(t):
                if psum is None:
                    link(v.scalar_tensor_tensor(out=m[:, t, :], in0=m[:, t, :], scalar=rstd[:, s, t:t + 1],
                                                in1=row[:, :], op0=ALU.mult, op1=ALU.mult))
                else:
                    dve.wait_ge(S(f"bank_free{t}"), PH[psum][1][t] + 1)
                    for h, src in enumerate((m[:, t, 0:512], PD[t])):
                        op = v.scalar_tensor_tensor(out=m[:, t, 512 * h:512 * h + 512], in0=src,
                                                    scalar=rstd[:, s, t:t + 1], in1=row[:, 512 * h:512 * h + 512],
                                                    op0=ALU.mult, op1=ALU.mult)
                        if h == 0:
                            link(op)
                        else:
                            op.then_inc(S(f"bank_free{t}"), 1)
                    dve.wait_ge(S(f"bank_free{t}"), PH[psum][1][t] + 2)
                v.tensor_tensor(xres[:, t, :], xres[:, t, :], m[:, t, :], ALU.add).then_inc(S(sem), 1)
            return step

        narrow_out("kiw", 80)
        phase_done(dve, "qi")
        rope(qi_tm[:, :, 0:512].rearrange("p t (h d) -> p t h d", d=HD), H1 // 2, 8, cosq, sinq, rt, S("qi_roped"))
        dve.wait_ge(S("qi_roped"), 1)
        dve.wait_ge(S("kiw_turned"), 1)
        turned_kiw = PM[:, 0, 0:80 * TT].rearrange("p (t n) -> p t n", t=TT)
        v.tensor_copy(kiw[:, :, 0:64], turned_kiw[:, :, 0:64])
        link(v.tensor_scalar(kiw[:, :, 128:144], turned_kiw[:, :, 64:80], H1 ** -0.5 * HD ** -0.5, None, ALU.mult))
        rope(kiw[:, :, 0:64].rearrange("p t (h d) -> p t h d", d=HD), 1, 8, cosq, sinq, rt)
        v.tensor_copy(kiw[:, :, 64:128], kiw[:, :, 0:64]).then_inc(S("ki_roped"), 1)
        phase_done(dve, "qi2")
        rope(qi_tm[:, :, 512:DM].rearrange("p t (h d) -> p t h d", d=HD), H1 // 2, 8, cosq, sinq, rt, S("qi_roped"))
        for h in range(H1):
            for t in range(1, TT):
                dve.wait_ge(S("idx_relu"), 3 * h + t)
                r = relu_s[:, h % 2, IDX_AT[t]:IDX_AT[t] + (t + 1) * P]
                sc = score[:, t, 0:(t + 1) * P]
                w = kiw[:, t, 128 + h:129 + h]
                if h:
                    dve.wait_ge(S("idx_sum"), 3 * (h - 1) + t)
                    v.scalar_tensor_tensor(out=sc, in0=r, scalar=w, in1=sc, op0=ALU.mult, op1=ALU.add)\
                        .then_inc(S("idx_sum"), 1)
                else:
                    v.tensor_scalar(sc, r, w, None, ALU.mult).then_inc(S("idx_sum"), 1)
        for r in range(TOPK // 8):
            for t in range(1, TT):
                if r == 0:
                    dve.wait_ge(S("score_masked"), t)
                else:
                    dve.wait_ge(S("top_taken"), 3 * (r - 1) + t)
                v.max(top8[:, t, :], score[:, t, 0:(t + 1) * P]).then_inc(S("top_found"), 1)
            for t in range(1, TT):
                dve.wait_ge(S("top_found"), 3 * r + t)
                v.match_replace(score[:, t, 0:(t + 1) * P], top8[:, t, :], score[:, t, 0:(t + 1) * P], CHOSEN)\
                    .then_inc(S("top_taken"), 1)
        for t in range(1, TT):
            dve.wait_ge(S("top_taken"), 3 * (TOPK // 8 - 1) + t)
            v.tensor_scalar(bias_q[:, t, 0:(t + 1) * P], score[:, t, 0:(t + 1) * P], CHOSEN, NEG, ALU.not_equal,
                            ALU.mult).then_inc(S("bias_made"), 1)
        phase_done(dve, "qk2")
        rope(qk_tm[:, :, :].rearrange("p t (h d) -> p t h d", d=HD), H1, 8, cosq, sinq, rt, S("qk_roped"))
        phase_done(dve, "gates")
        dve.wait_ge(S("pads"), 2)
        dve.wait_ge(S("tr_read"), TR["qk"][0] + 8)

        def convolution2(f):
            col = [col_b[:, C_CW2 + 4 * j + f:C_CW2 + 4 * j + f + 1] for j in range(3)]
            link(v.tensor_scalar(ca[:, f, :], gc[:, f, 0:SEQ], col[0], None, ALU.mult))
            for j in (1, 2):
                link(v.scalar_tensor_tensor(out=ca[:, f, :], in0=gc[:, f, j:j + SEQ], scalar=col[j], in1=ca[:, f, :],
                                            op0=ALU.mult, op1=ALU.add))
            v.tensor_tensor(ca[:, f, :], ca[:, f, :], gb[:, f, :], ALU.mult).then_inc(S("conv2_out"), 1)

        def convolution2_low(f):
            dve.wait_ge(S("conv2_hi"), f + 1)
            v.tensor_tensor(hlo[:, 4 + f, :], ca[:, f, :], fl(hhi[:, 4 + f, :]), ALU.subtract)\
                .then_inc(S("conv2_done"), 1)

        def row_max(n, m):
            for q, t in enumerate((3, 2, 0, 1)):
                b, c0 = QB_AT[t]
                dve.wait_ge(S("att_logits"), 3 * n + [1, 2, 2, 3][q])
                v.reduce_max(m[:, n % 4, t:t + 1], PX[n % 2][:, b, c0:c0 + (t + 1) * P], AX, negate=True)\
                    .then_inc(S("att_max"), 1)

        def turned(n, pt):
            dve.wait_ge(S("att_turned"), n + 1)
            if n >= 2:
                dve.wait_ge(S("att_pv"), n - 1)
            v.tensor_copy(pt[n % 2][:, SEQ:1280], PX[n % 2][:, 1:3, :].rearrange("p a b -> p (a b)")[:, 0:1280 - SEQ])\
                .then_inc(S("probs_v"), 1)

        def emit(n, d, dst):
            s = n % 2
            dve.wait_ge(S("att_exps"), 4 * n + 4)
            link(v.reciprocal(d[:, n % 4, :], d[:, n % 4, :]))
            dve.wait_ge(S("att_pv"), n + 1)
            v.tensor_tensor(dst, PM[:, 3, 256 * s:256 * s + 256].rearrange("p (t d) -> p t d", t=TT),
                            d[:, n % 4, :].unsqueeze(2).to_broadcast([P, TT, HD]), ALU.mult).then_inc(S("att_out"), 1)

        for h in range(A_H + 2):
            if h < A_H:
                row_max(h, mx)
            if 1 <= h <= A_H:
                turned(h - 1, prt)
            if h >= 2:
                emit(h - 2, den, v2[:, :, (h - 2) * HD:(h - 1) * HD])
            if h < 4:
                link(v.tensor_tensor(gc[:, h, 2:SEQ + 2], gc[:, h, 2:SEQ + 2], xi[:, h, :], ALU.mult))
                convolution2(h)
            if 2 <= h < 6:
                convolution2_low(h - 2)
        split_tiles("attn", 4, lambda k: 1.0, 0)
        dve.wait_ge(S("row_mix0"), 16)
        norm_tiles(5, NORM_ORDER, None, post_norm(5, mix2, row_b, "post_mix0", "wo2"), "ffn0", 32)

        def mlp(name, layer):
            u0 = PH[name][0]
            MPAR = {0: 0, 2: 1, 6: 0}

            def up(first, i, m):
                base = m * 4 + 32 * layer

                def square(b, r):
                    dve.wait_ge(S(f"bank_free{b}"), r + (PH[name][1][b] + 1))
                    v.tensor_tensor(mh_r[:, b % 2, :], mh_r[:, b % 2, :], mh_r[:, b % 2, :], ALU.mult)\
                        .then_inc(S("hidden_sq"), 1)

                def low(b):
                    dve.wait_ge(S("hidden_hi"), base + (b + 1))
                    v.tensor_tensor(mh_lo[MPAR[first]][:, b, :], mh_r[:, b % 2, :], fl(mh_hi[MPAR[first]][:, b, :]),
                                    ALU.subtract).then_inc(S("hidden_ready"), 1)
                r = {0: 0, 2: i * 6 + 1, 6: i * 6 + 4}[first]
                square(0, r)
                square(1, r)
                low(0)
                square(2, r)
                low(1)
                square(3, r)
                low(2)
                low(3)

            def down(first, r, i):
                for h in range(2):
                    for b in range(4):
                        full_wait(dve, name, b, r + h, i * 8 + (u0 + first + h))
                        m = mixm[:, b, 512 * h:512 * h + 512]
                        v.tensor_tensor(m, PD[b], m, ALU.add).then_inc(S(f"bank_free{b}"), 1)

            dve.wait_ge(S("acc_zero"), layer + 1)
            up(0, 0, 0)
            with dve.Fori(0, 3) as i:
                up(2, i, i * 2 + 1)
                down(4, i * 6 + 2, i)
                up(6, i, i * 2 + 2)
                down(8, i * 6 + 5, i)
            up(2, 3, 7)
            down(4, 20, 3)
            for b in range(4):
                last_sum(name, 0, b)

        def last_sum(name, h, b):
            full_wait(dve, name, b, 22 + h, PH[name][0] + 30 + h)
            m = mixm[:, b, 512 * h:512 * h + 512]
            v.tensor_tensor(m, PD[b], m, ALU.add).then_inc(S(f"bank_free{b}"), 1)

        mlp("mlp0", 0)
        dve.wait_ge(S("row_ffn0"), 16)
        norm_tiles(7, FIRST_ORDER, lambda t: last_sum("mlp0", 1, t), post_norm(7, mixm, row_a, "post_ffn0"), "mix1", 48)
        for t in range(TT):
            dve.wait_ge(S("rms9"), t + 1)
            v.tensor_scalar(cq[:, t, :], cq[:, t, :], rstd[:, 9, t:t + 1], None, ALU.mult).then_inc(S("cq_made"), 1)
        for t in range(TT):
            dve.wait_ge(S("rms10"), t + 1)
            v.tensor_scalar(kva[:, t, 0:KV_RANK], kva[:, t, 0:KV_RANK], rstd[:, 10, t:t + 1], None, ALU.mult)\
                .then_inc(S("ckv_made"), 1)
        split_tiles("cq", 3, lambda k: col_b[:, C_QN + k:C_QN + k + 1], 0)
        split_tiles("ckv", 2, lambda k: col_b[:, C_KN + k:C_KN + k + 1], 3)
        phase_done(dve, "uq")
        q4 = q_tm[:, :, :].rearrange("p t (h d) -> p t h d", d=C_QK)
        rope(q4[:, :, :, C_NOPE:C_QK], C_H, 16, cosm, sinm, rtm)
        rope(kva[:, :, 256:288].rearrange("p t (h d) -> p t h d", h=1), 1, 16, cosm, sinm, rtm)
        v.tensor_copy(k_tm[:, :, :, C_NOPE:C_QK], kva[:, :, 256:288].unsqueeze(2).to_broadcast([P, TT, C_H, 32]))\
            .then_inc(S("mla_roped"), 1)

        def turned_k(h):
            dve.wait_ge(S("tr_done"), TR["heads"][0] + 2 * h + 2)
            v.tensor_copy(kth[h % 2][0:C_QK, :], PDT[0:C_QK, 3, :]).then_inc(S("tr_read"), 1)

        turned_k(0)
        turned_k(1)
        for h in range(C_H + 2):
            if h < C_H:
                row_max(A_H + h, mx3)
            if 1 <= h <= C_H:
                turned(A_H + h - 1, prt3)
            if h + 2 < C_H:
                turned_k(h + 2)
            if h >= 2:
                emit(A_H + h - 2, den3, v3[:, :, (h - 2) * HD:(h - 1) * HD])
        split_tiles("lat", 8, lambda k: 1.0, 0)
        dve.wait_ge(S("row_mix1"), 16)
        norm_tiles(11, NORM_ORDER, None, post_norm(11, mix3, row_b, "post_mix1", "wo3"), "ffn1", 64)
        mlp("mlp1", 1)
        dve.wait_ge(S("row_ffn1"), 16)
        last = post_norm(13, mixm, row_a, "post_ffn1")
        for step, t in [p for p in FIRST_ORDER if p[0] in ("first", "A")]:
            if step == "first":
                last_sum("mlp1", 1, t)
            else:
                dve.wait_ge(S("rms13"), t + 1)
                last(t)

    ctx.close()


NAMES = ["x", "c", "w_ada", "b_ada", "norm_in_gain", "w_in", "conv_w", "conv_b", "dt_bias", "a_log", "d_skip",
         "sb_norm_gain", "ssm_norm_gain", "w_out", "norm_f_gain", "positions_2", "norm_mix_pre_2",
         "norm_mix_post_2", "norm_ffn_pre_2", "norm_ffn_post_2", "even_w_in_2", "even_conv_w_2", "even_w_out_2",
         "odd_w_dq_2", "odd_q_norm_2", "odd_w_uq_2", "odd_w_dkv_2", "odd_kv_norm_2", "odd_w_ukv_2", "odd_w_o_2",
         "mlp_w1_2", "mlp_w2_2"]


def kernel(**inputs):
    import numpy as np
    import concourse.bacc as bacc
    from concourse.bass_utils import run_bass_kernel_spmd

    nc = bacc.Bacc("TRN2", target_bir_lowering=False, num_devices=1, dynamic_dma_scratch_size=1024)
    arrays, args = {}, []
    for name in NAMES:
        a = np.ascontiguousarray(inputs[name])
        arrays[f"in_{name}"] = a
        args.append(nc.dram_tensor(f"in_{name}", a.shape, mybir.dt.from_np(a.dtype), kind="ExternalInput").ap())
    args.append(nc.dram_tensor("out_0", (1, SEQ, DM), F32, kind="ExternalOutput").ap())
    build_program(nc, *args)
    r = run_bass_kernel_spmd(nc, [arrays], core_ids=[0])
    return r.results[0]["out_0"]
```
